# Optimizing a Trainium2 kernel written in Bass

```python
import math
import jax, jax.numpy as jnp
from jax import lax
import numpy as np

D_MODEL = 1024
BATCH = 1
SEQ = 1024
DEPTH = 1
DEC_BATCH = 8
DEC_SEQ = 8
PAST_LEN = 4096
PAGE_SIZE = 128

HEAD_DIM = 64
RW_HEADS = 4
RW_WIDTH = RW_HEADS * HEAD_DIM
RW_W_LORA = 64
RW_A_LORA = 64
RW_G_LORA = 128
RW_SHIFT_COLS = 3 * RW_WIDTH + RW_W_LORA + RW_A_LORA + RW_G_LORA
RW_GN_EPS = 64e-5
ML_HEADS = 4
ML_WIDTH = ML_HEADS * HEAD_DIM
ML_CONV = 4
ML_CHUNK = 64
ML_COLS = 3 * ML_WIDTH + 2 * ML_HEADS
NSA_HEADS = 8
NSA_KV_HEADS = 2
NSA_GROUP = NSA_HEADS // NSA_KV_HEADS
NSA_WIDTH = NSA_HEADS * HEAD_DIM
NSA_KV = NSA_KV_HEADS * HEAD_DIM
NSA_BLOCK = 64
NSA_TOPN = 8
NSA_WINDOW = 512
NSA_QBLOCK = 64
WIN_QBLOCK = 128
NSA_COLS = NSA_WIDTH + 6 * NSA_KV + 3 * NSA_HEADS
MIX_WIDTH = RW_WIDTH + ML_WIDTH + NSA_WIDTH
IN_COLS = RW_SHIFT_COLS + ML_COLS + NSA_COLS
MEM_LEN = 256
MEM_HEADS = 4
MEM_WIDTH = MEM_HEADS * HEAD_DIM
D_FF = 2816
NORM_EPS = 1e-6
BIG = 1e9

kernel_name = 'hybrid_rwkv7_mlstm_nsa_macaron_decode_step'

def _split(x, sizes):
    offs = [0]
    for s in sizes:
        offs.append(offs[-1] + s)
    return [x[..., offs[i]:offs[i + 1]] for i in range(len(sizes))]

def _rms_norm(x, g, eps=NORM_EPS):
    xf = x.astype(jnp.float32)
    y = xf * lax.rsqrt(jnp.mean(xf * xf, axis=-1, keepdims=True) + eps)
    return (y * g.astype(jnp.float32)).astype(x.dtype)

def _masked_softmax(s, mask):
    s = jnp.where(mask, s.astype(jnp.float32), -jnp.inf)
    m = jnp.max(s, axis=-1, keepdims=True)
    m = jnp.where(jnp.isfinite(m), m, 0.0)
    e = jnp.exp(s - m)
    return e / jnp.maximum(jnp.sum(e, axis=-1, keepdims=True), 1e-30)

def _swiglu(h, w_up, w_down):
    gate, up = jnp.split(h @ w_up, 2, axis=-1)
    return (jax.nn.silu(gate) * up) @ w_down

def _qblocks(z, qb):
    B, T = z.shape[:2]
    return jnp.moveaxis(z.reshape(B, T // qb, qb, *z.shape[2:]), 1, 0)

def _unblock(z):
    z = jnp.moveaxis(z, 0, 1)
    return z.reshape(z.shape[0], -1, *z.shape[3:])

def _rwkv7(p, shift_prev, S0, mu, w0, w2, a0, a2, g2, kk_s, ka, rk, gn_g, gn_b):
    B, T, _ = p.shape
    H, N = RW_HEADS, HEAD_DIM
    f32 = jnp.float32
    p_prev = jnp.concatenate([shift_prev.astype(p.dtype), p[:, :-1]], axis=1)
    xm = p + (p_prev - p) * mu
    r, k, v, wd, ad, gd = _split(xm, [RW_WIDTH, RW_WIDTH, RW_WIDTH, RW_W_LORA, RW_A_LORA, RW_G_LORA])
    w = -jax.nn.softplus(-(w0 + jnp.tanh(wd) @ w2)) - 0.5
    a = jax.nn.sigmoid(a0 + ad @ a2)
    g = jax.nn.sigmoid(gd) @ g2
    kk = (k * kk_s).reshape(B, T, H, N).astype(f32)
    kk = kk / jnp.maximum(jnp.sqrt(jnp.sum(kk * kk, axis=-1, keepdims=True)), 1e-12)
    k = k * (1.0 + (a - 1.0) * ka)
    hd = lambda z: z.reshape(B, T, H, N).astype(f32)
    rh, kh, vh, ah = hd(r), hd(k), hd(v), hd(a)
    decay = jnp.exp(-jnp.exp(hd(w)))
    tm = lambda z: jnp.moveaxis(z, 1, 0)

    def step(S, inp):
        r_t, w_t, k_t, v_t, kk_t, a_t = inp
        sa = jnp.einsum('bhij,bhj->bhi', S, -kk_t)
        S = (S * w_t[:, :, None, :] + sa[..., None] * (kk_t * a_t)[:, :, None, :]
             + v_t[..., None] * k_t[:, :, None, :])
        return S, jnp.einsum('bhij,bhj->bhi', S, r_t)

    S_T, ys = lax.scan(step, S0.astype(f32), (tm(rh), tm(decay), tm(kh), tm(vh), tm(kk), tm(ah)))
    y = jnp.moveaxis(ys, 0, 1)
    mean = jnp.mean(y, axis=-1, keepdims=True)
    var = jnp.mean(jnp.square(y - mean), axis=-1, keepdims=True)
    y = ((y - mean) * lax.rsqrt(var + RW_GN_EPS)).reshape(B, T, RW_WIDTH) * gn_g + gn_b
    bonus = (jnp.sum(rh * kh * rk, axis=-1, keepdims=True) * vh).reshape(B, T, RW_WIDTH)
    out = ((y + bonus) * g).astype(p.dtype)
    return out, p[:, -1:], S_T

def _mlstm_chunkwise(q, k, v, logi, logf, C0, n0, m0):
    B, H, T, dh = q.shape
    Lc = ML_CHUNK if T % ML_CHUNK == 0 else T
    nc = T // Lc

    def chunks(z):
        return jnp.moveaxis(z.reshape(B, H, nc, Lc, *z.shape[3:]), 2, 0)

    causal = jnp.tril(jnp.ones((Lc, Lc), dtype=bool))

    def step(carry, inp):
        C, n, m = carry
        qc, kc, vc, ic, fc = inp
        b = jnp.cumsum(fc, axis=-1)
        dmat = jnp.where(causal, b[..., :, None] - b[..., None, :] + ic[..., None, :], -jnp.inf)
        inter = b + m[..., None]
        m_t = jnp.maximum(inter, jnp.max(dmat, axis=-1))
        a = jnp.einsum('bhtd,bhsd->bhts', qc, kc) * jnp.exp(dmat - m_t[..., None])
        sc = jnp.exp(inter - m_t)
        num = sc[..., None] * jnp.einsum('bhij,bhtj->bhti', C, qc) + jnp.einsum('bhts,bhsi->bhti', a, vc)
        den = sc * jnp.einsum('bhj,bhtj->bht', n, qc) + jnp.sum(a, axis=-1)
        h = num / jnp.maximum(jnp.abs(den), jnp.exp(-m_t))[..., None]
        b_end = b[..., -1]
        gs = b_end[..., None] - b + ic
        m_new = jnp.maximum(b_end + m, jnp.max(gs, axis=-1))
        dec = jnp.exp(b_end + m - m_new)
        wg = jnp.exp(gs - m_new[..., None])
        C = dec[..., None, None] * C + jnp.einsum('bhs,bhsi,bhsj->bhij', wg, vc, kc)
        n = dec[..., None] * n + jnp.einsum('bhs,bhsj->bhj', wg, kc)
        return (C, n, m_new), h

    (C, n, m), hs = lax.scan(step, (C0, n0, m0), tuple(chunks(z) for z in (q, k, v, logi, logf)))
    h = jnp.moveaxis(hs, 0, 2).reshape(B, H, T, dh)
    return h, C, n, m

def _mlstm(p, conv_prev, C0, n0, m0, conv_w, conv_b, wq, wk, gate_b, norm_g, skip):
    B, T, _ = p.shape
    H, dh = ML_HEADS, HEAD_DIM
    f32 = jnp.float32
    qk_in, v, o_pre, i_pre, f_pre = _split(p, [ML_WIDTH, ML_WIDTH, ML_WIDTH, ML_HEADS, ML_HEADS])
    xpad = jnp.concatenate([conv_prev.astype(p.dtype), qk_in], axis=1)
    conv = conv_b + sum(conv_w[j] * xpad[:, j:j + T] for j in range(ML_CONV))
    ca = jax.nn.silu(conv)
    cah = ca.reshape(B, T, H, dh)
    q = jnp.einsum('bthd,hde->bhte', cah, wq).astype(f32)
    k = (jnp.einsum('bthd,hde->bhte', cah, wk) * dh ** -0.5).astype(f32)
    vh = jnp.moveaxis(v.reshape(B, T, H, dh), 1, 2).astype(f32)
    logi = jnp.moveaxis((i_pre + gate_b[0]).astype(f32), 1, 2)
    logf = jax.nn.log_sigmoid(jnp.moveaxis((f_pre + gate_b[1]).astype(f32), 1, 2))
    h, C, n, m = _mlstm_chunkwise(q, k, vh, logi, logf, C0.astype(f32), n0.astype(f32), m0.astype(f32))
    h = jnp.moveaxis(h, 1, 2)
    h = h * lax.rsqrt(jnp.mean(h * h, axis=-1, keepdims=True) + NORM_EPS)
    out = (h.reshape(B, T, ML_WIDTH) * norm_g + skip * ca) * jax.nn.sigmoid(o_pre)
    return out.astype(p.dtype), xpad[:, T:], C, n, m

def _nsa_compress(kv_full, wpos, wc, kc_g):
    B, L = kv_full.shape[:2]
    nc = L // NSA_BLOCK
    blk = kv_full[:, :nc * NSA_BLOCK].reshape(B, nc, NSA_BLOCK, *kv_full.shape[2:])
    c = jnp.einsum('bnlcgd,lcgd->bncgd', blk, wpos)
    c = jnp.einsum('bncgd,cgde->bncge', c, wc)
    return _rms_norm(c[:, :, 0], kc_g), c[:, :, 1]

def _nsa_cmp_attend(q, qpos, ck, cv):
    dh = q.shape[-1]
    nc = ck.shape[1]
    s = jnp.einsum('btgrd,bngd->btgrn', q, ck) * dh ** -0.5
    vis = (jnp.arange(nc) + 1) * NSA_BLOCK - 1 <= qpos[:, None]
    p = _masked_softmax(s, vis[None, :, None, None, :])
    o = jnp.einsum('btgrn,bngd->btgrd', p, cv.astype(jnp.float32))
    return o, jnp.sum(p, axis=3)

def _nsa_select(imp, qpos, n_blocks):
    nc = imp.shape[-1]
    imp = jnp.pad(imp, ((0, 0), (0, 0), (0, 0), (0, n_blocks - nc)))
    j = jnp.arange(n_blocks)[None, :]
    cur = (qpos // NSA_BLOCK)[:, None]
    forced = (j == 0) | (j == cur) | (j == cur - 1)
    score = jnp.where(forced[None, :, None, :], BIG,
                      jnp.where((j <= cur)[None, :, None, :], imp, -BIG))
    _, idx = lax.top_k(score, min(NSA_TOPN, n_blocks))
    return idx

def _nsa_sel_attend(q, qpos, idx, kvb):
    B, T, G, R, dh = q.shape
    kb, vb = kvb[..., 0, :], kvb[..., 1, :]
    s = jnp.einsum('btgrd,btgkld->btgrkl', q, kb) * dh ** -0.5
    kpos = idx[..., None] * NSA_BLOCK + jnp.arange(NSA_BLOCK)
    mask = kpos <= qpos[None, :, None, None, None]
    p = _masked_softmax(s.reshape(B, T, G, R, -1), mask.reshape(B, T, G, 1, -1))
    return jnp.einsum('btgrn,btgnd->btgrd', p, vb.reshape(B, T, G, -1, dh).astype(jnp.float32))

def _nsa_win_attend(q, qpos, kv, kpos):
    dh = q.shape[-1]
    s = jnp.einsum('btgrd,bsgd->btgrs', q, kv[:, :, 0]) * dh ** -0.5
    d = qpos[:, None] - kpos[None, :]
    mask = (kpos[None, :] >= 0) & (d >= 0) & (d < NSA_WINDOW)
    p = _masked_softmax(s, mask[None, :, None, None, :])
    return jnp.einsum('btgrs,bsgd->btgrd', p, kv[:, :, 1].astype(jnp.float32))

def _nsa(p, is_prompt, page_table, pool_cmp, pool_sel, win_prev, qk_g, wpos, wc, gate_b):
    B, T, _ = p.shape
    G, R, dh = NSA_KV_HEADS, NSA_GROUP, HEAD_DIM
    q, kc, vc, ks, vs, kw, vw, gates = _split(p, [NSA_WIDTH] + [NSA_KV] * 6 + [3 * NSA_HEADS])
    q = _rms_norm(q.reshape(B, T, G, R, dh), qk_g[0])
    sh = lambda z: z.reshape(B, T, G, dh)
    kv_c = jnp.stack([sh(kc), sh(vc)], axis=2)
    kv_s = jnp.stack([_rms_norm(sh(ks), qk_g[2]), sh(vs)], axis=2)
    kv_w = jnp.stack([_rms_norm(sh(kw), qk_g[3]), sh(vw)], axis=2)
    bidx = jnp.arange(B)[:, None, None, None]
    gidx = jnp.arange(G)[None, None, :, None]
    if is_prompt:
        pos0 = 0
        kv_c_full = kv_c
    else:
        pos0 = page_table.shape[1] * PAGE_SIZE
        past = pool_cmp[page_table].reshape(B, pos0, 2, G, dh)
        kv_c_full = jnp.concatenate([past.astype(kv_c.dtype), kv_c], axis=1)
    qpos = pos0 + jnp.arange(T)
    n_blocks = -(-(pos0 + T) // NSA_BLOCK)
    ck, cv = _nsa_compress(kv_c_full, wpos, wc, qk_g[1])
    o_c, imp = _nsa_cmp_attend(q, qpos, ck, cv)
    idx = _nsa_select(imp, qpos, n_blocks)
    if is_prompt:
        blocks = kv_s.reshape(B, n_blocks, NSA_BLOCK, 2, G, dh)

        def sel_block(args):
            qb, ib, pb = args
            return _nsa_sel_attend(qb, pb, ib, blocks[bidx, ib, :, :, gidx])

        o_s = _unblock(lax.map(sel_block, (_qblocks(q, NSA_QBLOCK), _qblocks(idx, NSA_QBLOCK),
                                           qpos.reshape(T // NSA_QBLOCK, NSA_QBLOCK))))
        kv_pad = jnp.pad(kv_w, ((0, 0), (NSA_WINDOW, 0), (0, 0), (0, 0), (0, 0)))
        span = NSA_WINDOW + WIN_QBLOCK

        def win_block(args):
            qb, i = args
            start = i * WIN_QBLOCK
            kvb = lax.dynamic_slice_in_dim(kv_pad, start, span, axis=1)
            kpos = start - NSA_WINDOW + jnp.arange(span)
            return _nsa_win_attend(qb, start + jnp.arange(WIN_QBLOCK), kvb, kpos)

        o_w = _unblock(lax.map(win_block, (_qblocks(q, WIN_QBLOCK), jnp.arange(T // WIN_QBLOCK))))
        new_win = kv_w[:, T - min(NSA_WINDOW, T):]
    else:
        bpp = PAGE_SIZE // NSA_BLOCK
        n_past = pos0 // NSA_BLOCK
        n_new = n_blocks - n_past
        pool_blk = pool_sel.reshape(-1, NSA_BLOCK, 2, G, dh)
        new_blk = jnp.pad(kv_s, ((0, 0), (0, n_new * NSA_BLOCK - T), (0, 0), (0, 0), (0, 0)))
        new_blk = new_blk.reshape(B, n_new, NSA_BLOCK, 2, G, dh)
        jp = jnp.minimum(idx, n_past - 1)
        phys = page_table[bidx, jp // bpp] * bpp + jp % bpp
        g_pool = pool_blk[phys, :, :, gidx].astype(kv_s.dtype)
        g_new = new_blk[bidx, jnp.clip(idx - n_past, 0, n_new - 1), :, :, gidx]
        kvb = jnp.where((idx < n_past)[..., None, None, None], g_pool, g_new)
        o_s = _nsa_sel_attend(q, qpos, idx, kvb)
        wb = win_prev.shape[1]
        kv_all = jnp.concatenate([win_prev.astype(kv_w.dtype), kv_w], axis=1)
        o_w = _nsa_win_attend(q, qpos, kv_all, pos0 - wb + jnp.arange(wb + T))
        new_win = kv_all[:, wb + T - min(NSA_WINDOW, wb + T):]
    gt = jax.nn.sigmoid((gates + gate_b).astype(jnp.float32)).reshape(B, T, G, R, 3)
    o = gt[..., 0:1] * o_c + gt[..., 1:2] * o_s + gt[..., 2:3] * o_w
    return o.reshape(B, T, NSA_WIDTH).astype(p.dtype), kv_c, kv_s, new_win

def _mem_kv(mem, src_g, w_kv, k_g):
    B, M, _ = mem.shape
    kv = (_rms_norm(mem, src_g) @ w_kv).reshape(B, M, 2, MEM_HEADS, HEAD_DIM)
    return jnp.stack([_rms_norm(kv[:, :, 0], k_g), kv[:, :, 1]], axis=2)

def _mem_attend(h, kv, w_q, q_g, w_o):
    B, T, _ = h.shape
    q = _rms_norm((h @ w_q).reshape(B, T, MEM_HEADS, HEAD_DIM), q_g)
    s = jnp.einsum('bthd,bshd->bths', q, kv[:, :, 0].astype(q.dtype)).astype(jnp.float32) * HEAD_DIM ** -0.5
    pr = jax.nn.softmax(s, axis=-1)
    o = jnp.einsum('bths,bshd->bthd', pr, kv[:, :, 1].astype(jnp.float32))
    return o.reshape(B, T, MEM_WIDTH).astype(h.dtype) @ w_o

def _layer(x, W, st, is_prompt, page_table, mem):
    B, T, _ = x.shape
    dt = x.dtype
    g = W['norm_g']
    x = x + 0.5 * _swiglu(_rms_norm(x, g[0]), W['ffa_up'], W['ffa_down'])
    p = _rms_norm(x, g[1]) @ W['w_in']
    p_rw, p_ml, p_nsa = _split(p, [RW_SHIFT_COLS, ML_COLS, NSA_COLS])
    if is_prompt:
        z = lambda *shape: jnp.zeros(shape, jnp.float32)
        st = {'rw_shift': z(B, 1, RW_SHIFT_COLS), 'rw_S': z(B, RW_HEADS, HEAD_DIM, HEAD_DIM),
              'ml_conv': z(B, ML_CONV - 1, ML_WIDTH), 'ml_C': z(B, ML_HEADS, HEAD_DIM, HEAD_DIM),
              'ml_n': z(B, ML_HEADS, HEAD_DIM), 'ml_m': z(B, ML_HEADS),
              'nsa_cmp': None, 'nsa_sel': None, 'nsa_win': None,
              'mem_kv': _mem_kv(mem, g[3], W['mem_w_kv'], W['mem_qk_g'][1])}
    o_rw, rw_shift, rw_S = _rwkv7(p_rw, st['rw_shift'], st['rw_S'], W['rw_mu'], W['rw_w0'], W['rw_w2'],
                                  W['rw_a0'], W['rw_a2'], W['rw_g2'], W['rw_kk'], W['rw_ka'], W['rw_rk'],
                                  W['rw_gn_g'], W['rw_gn_b'])
    o_ml, ml_conv, ml_C, ml_n, ml_m = _mlstm(p_ml, st['ml_conv'], st['ml_C'], st['ml_n'], st['ml_m'],
                                             W['ml_conv_w'], W['ml_conv_b'], W['ml_wq'], W['ml_wk'],
                                             W['ml_gate_b'], W['ml_norm_g'], W['ml_skip'])
    o_nsa, kv_c, kv_s, win = _nsa(p_nsa, is_prompt, page_table, st['nsa_cmp'], st['nsa_sel'], st['nsa_win'],
                                  W['nsa_qk_g'], W['nsa_wpos'], W['nsa_wc'], W['nsa_gate_b'])
    x = x + jnp.concatenate([o_rw, o_ml, o_nsa], axis=-1) @ W['w_out']
    x = x + _mem_attend(_rms_norm(x, g[2]), st['mem_kv'], W['mem_w_q'], W['mem_qk_g'][0], W['mem_w_o'])
    x = x + 0.5 * _swiglu(_rms_norm(x, g[4]), W['ffb_up'], W['ffb_down'])
    new = {'nsa_cmp': kv_c.astype(dt), 'nsa_sel': kv_s.astype(dt), 'nsa_win': win.astype(dt),
           'rw_shift': rw_shift.astype(dt), 'rw_S': rw_S.astype(dt), 'ml_conv': ml_conv.astype(dt),
           'ml_C': ml_C.astype(dt), 'ml_n': ml_n.astype(dt), 'ml_m': ml_m.astype(dt)}
    if is_prompt:
        new['mem_kv'] = st['mem_kv'].astype(dt)
    return x, new

def setup_inputs(seed: int = 0) -> dict:
    key = jax.random.key(seed)
    keys = iter(jax.random.split(key, 80))

    def nrm(shape, scale=1.0):
        return scale * jax.random.normal(next(keys), shape, jnp.float32)

    def gain(shape):
        return 1.0 + 0.02 * nrm(shape)

    L, G, dh = DEPTH, NSA_KV_HEADS, HEAD_DIM
    n_pages = PAST_LEN // PAGE_SIZE
    n_used = DEC_BATCH * n_pages
    n_phys = n_used + (n_used + 3) // 4
    wb = min(NSA_WINDOW, PAST_LEN)
    page_table = jax.random.permutation(next(keys), n_phys)[:n_used].reshape(DEC_BATCH, n_pages).astype(jnp.int32)
    return {
        'x_prompt': nrm((BATCH, SEQ, D_MODEL)),
        'x_sample': nrm((DEC_BATCH, DEC_SEQ, D_MODEL)),
        'cache_nsa_cmp': nrm((L, n_phys, PAGE_SIZE, 2, G, dh)),
        'cache_nsa_sel': nrm((L, n_phys, PAGE_SIZE, 2, G, dh)),
        'cache_nsa_win': nrm((L, DEC_BATCH, wb, 2, G, dh)),
        'cache_mem_kv': nrm((L, DEC_BATCH, MEM_LEN, 2, MEM_HEADS, dh)),
        'state_rwkv_shift': nrm((L, DEC_BATCH, 1, RW_SHIFT_COLS)),
        'state_rwkv_S': nrm((L, DEC_BATCH, RW_HEADS, dh, dh), 0.5),
        'state_mlstm_conv': nrm((L, DEC_BATCH, ML_CONV - 1, ML_WIDTH)),
        'state_mlstm_C': nrm((L, DEC_BATCH, ML_HEADS, dh, dh), 0.5),
        'state_mlstm_n': nrm((L, DEC_BATCH, ML_HEADS, dh), 0.5),
        'state_mlstm_m': nrm((L, DEC_BATCH, ML_HEADS)),
        'page_table': page_table,
        'mem_prompt': nrm((BATCH, MEM_LEN, D_MODEL)),
        'norm_g': gain((L, 5, D_MODEL)),
        'ffa_up': nrm((L, D_MODEL, 2 * D_FF), D_MODEL ** -0.5),
        'ffa_down': nrm((L, D_FF, D_MODEL), D_FF ** -0.5),
        'ffb_up': nrm((L, D_MODEL, 2 * D_FF), D_MODEL ** -0.5),
        'ffb_down': nrm((L, D_FF, D_MODEL), D_FF ** -0.5),
        'w_in': nrm((L, D_MODEL, IN_COLS), D_MODEL ** -0.5),
        'w_out': nrm((L, MIX_WIDTH, D_MODEL), MIX_WIDTH ** -0.5),
        'rw_mu': jax.random.uniform(next(keys), (L, RW_SHIFT_COLS), jnp.float32),
        'rw_w0': jax.random.uniform(next(keys), (L, RW_WIDTH), jnp.float32, -6.0, -1.0),
        'rw_w2': nrm((L, RW_W_LORA, RW_WIDTH), 0.5 * RW_W_LORA ** -0.5),
        'rw_a0': nrm((L, RW_WIDTH), 0.1),
        'rw_a2': nrm((L, RW_A_LORA, RW_WIDTH), 0.5 * RW_A_LORA ** -0.5),
        'rw_g2': nrm((L, RW_G_LORA, RW_WIDTH), RW_G_LORA ** -0.5),
        'rw_kk': 1.0 + nrm((L, RW_WIDTH), 0.1),
        'rw_ka': 1.0 + nrm((L, RW_WIDTH), 0.1),
        'rw_rk': nrm((L, RW_HEADS, dh), 0.1),
        'rw_gn_g': gain((L, RW_WIDTH)),
        'rw_gn_b': nrm((L, RW_WIDTH), 0.02),
        'ml_conv_w': nrm((L, ML_CONV, ML_WIDTH), 0.5),
        'ml_conv_b': nrm((L, ML_WIDTH), 0.02),
        'ml_wq': nrm((L, ML_HEADS, dh, dh), dh ** -0.5),
        'ml_wk': nrm((L, ML_HEADS, dh, dh), dh ** -0.5),
        'ml_gate_b': jnp.stack([nrm((L, ML_HEADS), 0.1),
                                jnp.linspace(3.0, 6.0, ML_HEADS)[None, :] + nrm((L, ML_HEADS), 0.1)], axis=1),
        'ml_norm_g': gain((L, ML_WIDTH)),
        'ml_skip': 1.0 + nrm((L, ML_WIDTH), 0.1),
        'nsa_qk_g': gain((L, 4, dh)),
        'nsa_wpos': NSA_BLOCK ** -0.5 * (1.0 + nrm((L, NSA_BLOCK, 2, G, dh), 0.3)),
        'nsa_wc': nrm((L, 2, G, dh, dh), dh ** -0.5),
        'nsa_gate_b': nrm((L, 3 * NSA_HEADS), 0.1),
        'mem_w_q': nrm((L, D_MODEL, MEM_WIDTH), D_MODEL ** -0.5),
        'mem_w_kv': nrm((L, D_MODEL, 2 * MEM_WIDTH), D_MODEL ** -0.5),
        'mem_qk_g': gain((L, 2, dh)),
        'mem_w_o': nrm((L, MEM_WIDTH, D_MODEL), MEM_WIDTH ** -0.5),
    }

def reference(x_prompt, x_sample, cache_nsa_cmp, cache_nsa_sel, cache_nsa_win, cache_mem_kv,
              state_rwkv_shift, state_rwkv_S, state_mlstm_conv, state_mlstm_C, state_mlstm_n, state_mlstm_m,
              page_table, mem_prompt, norm_g, ffa_up, ffa_down, ffb_up, ffb_down, w_in, w_out,
              rw_mu, rw_w0, rw_w2, rw_a0, rw_a2, rw_g2, rw_kk, rw_ka, rw_rk, rw_gn_g, rw_gn_b,
              ml_conv_w, ml_conv_b, ml_wq, ml_wk, ml_gate_b, ml_norm_g, ml_skip,
              nsa_qk_g, nsa_wpos, nsa_wc, nsa_gate_b, mem_w_q, mem_w_kv, mem_qk_g, mem_w_o):
    y_p, y_s = x_prompt, x_sample
    new_p, new_s = [], []
    for l in range(DEPTH):
        W = {'norm_g': norm_g[l], 'ffa_up': ffa_up[l], 'ffa_down': ffa_down[l], 'ffb_up': ffb_up[l],
             'ffb_down': ffb_down[l], 'w_in': w_in[l], 'w_out': w_out[l], 'rw_mu': rw_mu[l], 'rw_w0': rw_w0[l],
             'rw_w2': rw_w2[l], 'rw_a0': rw_a0[l], 'rw_a2': rw_a2[l], 'rw_g2': rw_g2[l], 'rw_kk': rw_kk[l],
             'rw_ka': rw_ka[l], 'rw_rk': rw_rk[l], 'rw_gn_g': rw_gn_g[l], 'rw_gn_b': rw_gn_b[l],
             'ml_conv_w': ml_conv_w[l], 'ml_conv_b': ml_conv_b[l], 'ml_wq': ml_wq[l], 'ml_wk': ml_wk[l],
             'ml_gate_b': ml_gate_b[l], 'ml_norm_g': ml_norm_g[l], 'ml_skip': ml_skip[l],
             'nsa_qk_g': nsa_qk_g[l], 'nsa_wpos': nsa_wpos[l], 'nsa_wc': nsa_wc[l], 'nsa_gate_b': nsa_gate_b[l],
             'mem_w_q': mem_w_q[l], 'mem_w_kv': mem_w_kv[l], 'mem_qk_g': mem_qk_g[l], 'mem_w_o': mem_w_o[l]}
        st = {'nsa_cmp': cache_nsa_cmp[l], 'nsa_sel': cache_nsa_sel[l], 'nsa_win': cache_nsa_win[l],
              'mem_kv': cache_mem_kv[l], 'rw_shift': state_rwkv_shift[l], 'rw_S': state_rwkv_S[l],
              'ml_conv': state_mlstm_conv[l], 'ml_C': state_mlstm_C[l], 'ml_n': state_mlstm_n[l],
              'ml_m': state_mlstm_m[l]}
        y_p, sp = _layer(y_p, W, None, True, None, mem_prompt)
        y_s, ss = _layer(y_s, W, st, False, page_table, None)
        new_p.append(sp)
        new_s.append(ss)
    P = lambda name: jnp.stack([d[name] for d in new_p])
    S = lambda name: jnp.stack([d[name] for d in new_s])
    return (y_p, y_s,
            P('nsa_cmp'), S('nsa_cmp'), P('nsa_sel'), S('nsa_sel'), P('nsa_win'), S('nsa_win'),
            P('mem_kv'),
            P('rw_shift'), S('rw_shift'), P('rw_S'), S('rw_S'),
            P('ml_conv'), S('ml_conv'), P('ml_C'), S('ml_C'), P('ml_n'), S('ml_n'), P('ml_m'), S('ml_m'))


_drawn_inputs = setup_inputs


def setup_inputs(seed=0):
    import zlib

    import numpy as np

    out = dict(_drawn_inputs(seed))
    spreads = {}
    factors = {'rw_gn_g': 8.0,
     'rw_gn_b': 8.0,
     'ml_norm_g': 8.0,
     'ml_skip': 3.719,
     'nsa_qk_g': 3.175,
     'nsa_gate_b': 6.493,
     'mem_qk_g': 3.918}
    for name, (base, spread) in spreads.items():
        noise = np.random.default_rng([zlib.crc32(name.encode()), seed]).standard_normal(out[name].shape)
        drawn = base * np.exp(spread * noise) if base else spread * noise
        out[name] = __import__('jax').numpy.asarray(drawn.astype(out[name].dtype))
    for name, factor in factors.items():
        out[name] = (out[name] * factor).astype(out[name].dtype)
    return out
```

```python
from contextlib import ExitStack

import numpy as np
import concourse.bass as bass
from concourse import mybir

F32 = mybir.dt.float32
I32 = mybir.dt.int32
U32 = mybir.dt.uint32
ALU = mybir.AluOpType
ACT = mybir.ActivationFunctionType
AX = mybir.AxisListType

P = 128
BANK = 512
D = 1024
KD = D // P
TP = 1024
NB = 8
TS = 8
R = TP + NB * TS
DH = 64
FF = 2816
FT = FF // P
CHUNKS = [(0, 512), (512, 512), (1024, 64)]
ROWT = [(i * P, P) for i in range(TP // P)] + [(TP, NB * TS)]
EPS = 1e-6
SCALE = DH ** -0.5
NEG = -1e30
PAST = 4096
PAGE = 128
NPG = PAST // PAGE
MEM = 256
WIN = 512
ML0 = 1024
NS0 = ML0 + 3 * 256 + 8
T_COLS = [128 * j for j in range(8)] + [ML0, ML0 + 128] + [ML0 + 512, ML0 + 640] + [NS0 + 128 * j for j in range(4)]
PT_QK, PT_O, PT_Q, PT_IF = 1024, 1280, 1536, 2048
PR_V, PR_KC, PR_VC, PR_KS, PR_VS, PR_KW, PR_VW, PR_G = 0, 256, 384, 512, 640, 768, 896, 1024
PR_W = 1048
R_GROUPS = [(ML0 + 256, 0, 256), (NS0 + 512, 256, 512), (NS0 + 1024, 768, 280)]


class Arena:
    def __init__(self, array, size):
        self.array, self.size, self.at = array, size, 0

    def take(self, parts, *dims):
        n = int(np.prod(dims))
        assert self.at + n <= self.size, (self.at, n, self.size)
        v = self.array[0:parts, self.at:self.at + n]
        self.at += n
        if len(dims) == 1:
            return v
        names = "abcd"[:len(dims)]
        return v.rearrange(f"p ({' '.join(names)}) -> p {' '.join(names)}", **dict(zip(names, dims)))


class Engine:
    def __init__(self, eng, psum, for_vector, for_scalar):
        self.eng, self.wait_ge = eng, eng.wait_ge
        self.counts, self.stages = {}, 0
        self.rv = Banks(psum, 0, 4, *for_vector)
        self.ra = Banks(psum, 4, 4, *for_scalar)

    def due(self, semaphore, n=1):
        self.counts[semaphore.name] = self.counts.get(semaphore.name, 0) + n
        return self.counts[semaphore.name]

    def done(self, semaphore):
        return self.due(semaphore)

    def one(self, semaphore):
        self.due(semaphore)
        return 1

    def met(self):
        self.stages += 1
        return 5 * self.stages


class Banks:
    def __init__(self, psum, first, banks, full, read):
        self.psum, self.first, self.banks, self.n = psum, first, banks, 0
        self.full, self.read = full, read

    def next(self):
        b = self.first + self.n % self.banks
        self.n += 1
        return self.psum[:, b * BANK:(b + 1) * BANK]

    def freed(self):
        return max(0, self.n - self.banks + 1)


def build(nc, I, O):
    ctx = ExitStack()
    with ctx:
        size = 52000
        arena = Arena(ctx.enter_context(nc.sbuf_tensor("arena", [P, size], F32)), size)
        psum = ctx.enter_context(nc.psum_tensor("psum", [P, 8 * BANK], F32))
        def sem(name):
            return ctx.enter_context(nc.semaphore(name))

        bank_full_v, bank_read_v = sem("bank_full_v"), sem("bank_read_v")
        bank_full_a, bank_read_a = sem("bank_full_a"), sem("bank_read_a")
        vector_done, scalar_done, gpsimd_done = sem("vector_done"), sem("scalar_done"), sem("gpsimd_done")
        vector_for_tensor, vector_for_scalar = sem("vector_for_tensor"), sem("vector_for_scalar")
        vector_for_gpsimd, vector_for_sync = sem("vector_for_gpsimd"), sem("vector_for_sync")
        scalar_for_tensor, scalar_for_vector = sem("scalar_for_tensor"), sem("scalar_for_vector")
        scalar_for_sync, gpsimd_for_vector = sem("scalar_for_sync"), sem("gpsimd_for_vector")
        gpsimd_for_tensor, gpsimd_for_sync = sem("gpsimd_for_tensor"), sem("gpsimd_for_sync")
        sync_for_vector, sync_for_scalar, sync_for_tensor = sem("sync_for_vector"), sem("sync_for_scalar"), sem("sync_for_tensor")
        loads_for_vector, loads_for_scalar = sem("loads_for_vector"), sem("loads_for_scalar")
        loads_for_tensor = sem("loads_for_tensor")
        weights_in = [sem(f"weights_in{i}") for i in range(3)]
        weights_used = sem("weights_used")
        rows_stored, outputs_stored, heads_moved = sem("rows_stored"), sem("outputs_stored"), sem("heads_moved")
        slot_stored = [sem(f"slot_stored{i}") for i in range(2)]
        pages_in = [sem(f"pages_in{i}") for i in range(4)]
        cache_in = [sem(f"cache_in{i}") for i in range(4)]
        blocks_pooled, scalar_turned = sem("blocks_pooled"), sem("scalar_turned")
        stage_ends = sem("stage_ends")
        pT = nc.dram_tensor("pT", [2056, R], F32, kind="Internal").ap()
        pR = nc.dram_tensor("pR", [R, PR_W], F32, kind="Internal").ap()
        pooled = nc.dram_tensor("pooled", [64, 4, NB * PAST // 64], F32, kind="Internal").ap()
        mixT = nc.dram_tensor("mixT", [D, R], F32, kind="Internal").ap()

        def engine(eng):
            return Engine(eng, psum, (bank_full_v, bank_read_v), (bank_full_a, bank_read_a))

        ident = arena.take(P, P)
        ones = arena.take(P, P)
        blk = arena.take(P, P)
        norm_g = arena.take(P, 5, KD)
        eps = arena.take(P, 1)
        gneps = arena.take(P, 1)
        incl64, strict64, incl8, strict8 = (arena.take(P, P) for _ in range(4))
        neg64, neg8 = arena.take(P, P), arena.take(P, P)
        lm = arena.take(P, 6, P)
        bmask = arena.take(64, NB)
        sel4 = arena.take(4, 4, P)
        IDX = arena.take(P, NB * NPG)
        idx_u = IDX.bitcast(U32)
        bsel = arena.take(P, 2)
        xT = arena.take(P, KD, R)
        base = arena.at

        xin = arena.take(P, 3, D)
        same = arena.take(P, 7, P)
        ptab_i = arena.take(P, NB * NPG).bitcast(I32)
        prow = arena.take(P, 1)

        def setup_sp(sp):
            sp.eng.dma_start(norm_g, I["norm_g"].rearrange("l n (k p) -> p (l n) k", p=P),
                             allow_slow_non_contiguous=True).then_inc(loads_for_vector, 16)
            sp.eng.dma_start(ptab_i, I["page_table"].rearrange("(o b) p -> o (b p)", o=1).broadcast_to([P, NB * NPG]),
                             allow_slow_non_contiguous=True).then_inc(loads_for_vector, 16)
            xp, xs = I["x_prompt"][0], I["x_sample"].rearrange("b t d -> (b t) d")
            for i, (r0, n) in enumerate(ROWT):
                if i >= 3:
                    sp.wait_ge(weights_used, sp.due(weights_used))
                src = xp[r0:r0 + n] if r0 < TP else xs
                sp.eng.dma_start(xin[0:n, i % 3], src,
                                 allow_slow_non_contiguous=True).then_inc(weights_in[i % 3], 16)
            sp.wait_ge(weights_used, sp.due(weights_used, 3))

        def setup_gp(gp):
            g = gp.eng
            g.memset(ident, 0.0).then_inc(gpsimd_done, 1)
            gp.wait_ge(gpsimd_done, gp.done(gpsimd_done))
            g.affine_select(out=ident, in_=ident, compare_op=ALU.not_equal, fill=1.0, base=0,
                                  pattern=[[-1, P]], channel_multiplier=1).then_inc(gpsimd_done, 1)
            gp.wait_ge(gpsimd_done, gp.done(gpsimd_done))
            g.memset(ones, 1.0).then_inc(gpsimd_done, 1)
            gp.wait_ge(gpsimd_done, gp.done(gpsimd_done))
            g.memset(blk, 1.0).then_inc(gpsimd_done, 1)
            gp.wait_ge(gpsimd_done, gp.done(gpsimd_done))
            g.affine_select(out=blk[:, 0:64], in_=blk[:, 0:64], compare_op=ALU.is_ge, fill=0.0, base=63,
                                  pattern=[[0, 64]], channel_multiplier=-1).then_inc(gpsimd_done, 1)
            gp.wait_ge(gpsimd_done, gp.done(gpsimd_done))
            g.affine_select(out=blk[:, 64:128], in_=blk[:, 64:128], compare_op=ALU.is_ge, fill=0.0, base=-64,
                                  pattern=[[0, 64]], channel_multiplier=1).then_inc(gpsimd_done, 1)
            gp.wait_ge(gpsimd_done, gp.done(gpsimd_done))
            g.memset(eps, EPS).then_inc(gpsimd_done, 1)
            gp.wait_ge(gpsimd_done, gp.done(gpsimd_done))
            g.memset(gneps, 64e-5).then_inc(gpsimd_done, 1)
            gp.wait_ge(gpsimd_done, gp.done(gpsimd_done))

            def keep(m, op, by, step, b0, *dims):
                g.affine_select(out=m, in_=m, compare_op=op, fill=0.0, base=b0, pattern=step,
                                      channel_multiplier=by).then_inc(gpsimd_done, 1)
                gp.wait_ge(gpsimd_done, gp.done(gpsimd_done))

            for l in range(7):
                s, m = 2 ** l, same[:, l]
                g.memset(m, 1.0).then_inc(gpsimd_done, 1)
                gp.wait_ge(gpsimd_done, gp.done(gpsimd_done))
                keep(m, ALU.is_ge, 1, [[-s, P // s], [0, s]], 0)
                keep(m, ALU.is_ge, -1, [[s, P // s], [0, s]], s - 1)
            for l in range(6):
                g.tensor_tensor(lm[:, l], same[:, l + 1], same[:, l], ALU.subtract).then_inc(gpsimd_done, 1)
                gp.wait_ge(gpsimd_done, gp.done(gpsimd_done))
                keep(lm[:, l], ALU.is_gt, -1, [[1, P]], 0)
            for incl, strict, neg, l in ((incl64, strict64, neg64, 6), (incl8, strict8, neg8, 3)):
                g.tensor_copy(incl, same[:, l]).then_inc(gpsimd_done, 1)
                gp.wait_ge(gpsimd_done, gp.done(gpsimd_done))
                g.tensor_copy(strict, same[:, l]).then_inc(gpsimd_done, 1)
                gp.wait_ge(gpsimd_done, gp.done(gpsimd_done))
                keep(incl, ALU.is_ge, -1, [[1, P]], 0)
                keep(strict, ALU.is_gt, -1, [[1, P]], 0)
                g.tensor_scalar(neg, incl, -1.0, -NEG, ALU.add, ALU.mult).then_inc(gpsimd_done, 1)
                gp.wait_ge(gpsimd_done, gp.done(gpsimd_done))
            g.memset(bmask, 1.0).then_inc(gpsimd_done, 1)
            gp.wait_ge(gpsimd_done, gp.done(gpsimd_done))
            keep(bmask, ALU.is_ge, 1, [[-TS, NB]], 0)
            keep(bmask, ALU.is_ge, -1, [[TS, NB]], TS - 1)
            g.memset(sel4, 1.0).then_inc(gpsimd_done, 1)
            gp.wait_ge(gpsimd_done, gp.done(gpsimd_done))
            keep(sel4, ALU.is_equal, 1, [[-1, 4], [0, P]], 0)
            g.iota(prow, pattern=[[0, 1]], base=0, channel_multiplier=1, allow_small_or_imprecise_dtypes=True).then_inc(gpsimd_done, 1)
            gp.wait_ge(gpsimd_done, gp.done(gpsimd_done))
            g.memset(bsel, 1.0).then_inc(gpsimd_done, 1)
            gp.wait_ge(gpsimd_done, gp.done(gpsimd_done))
            keep(bsel[:, 0:1], ALU.is_ge, -1, [[0, 1]], 63)
            keep(bsel[:, 1:2], ALU.is_ge, 1, [[0, 1]], -64)
            gp.eng.sem_inc(gpsimd_for_tensor, gp.one(gpsimd_for_tensor))
            gp.eng.sem_inc(gpsimd_for_vector, gp.one(gpsimd_for_vector))

        def turn_pe(pe, i, src, n):
            pe.wait_ge(weights_in[i % 3], pe.due(weights_in[i % 3], 16))
            for ring, k0 in ((pe.rv, 0), (pe.ra, 4)):
                pe.wait_ge(ring.read, ring.freed())
                b = ring.next()
                for k in range(4):
                    ins = pe.eng.transpose(b[:, k * P:k * P + n], src[0:n, (k0 + k) * P:(k0 + k + 1) * P],
                                           ident[0:n, 0:n])
                ins.then_inc(ring.full, 1)

        def setup_pe(pe):
            pe.wait_ge(gpsimd_for_tensor, pe.due(gpsimd_for_tensor))
            for i, (r0, n) in enumerate(ROWT):
                turn_pe(pe, i, xin[:, i % 3], n)

        def four(b, n):
            return b.rearrange("p (k c) -> p k c", k=4)[:, :, 0:n]

        def setup_act(act):
            for i, (r0, n) in enumerate(ROWT):
                act.wait_ge(bank_full_a, act.due(bank_full_a))
                b = act.ra.next()
                act.eng.copy(xT[:, 4:8, r0:r0 + n], four(b, n)).then_inc(bank_read_a, 1)
                act.wait_ge(bank_read_a, act.done(bank_read_a))
                act.eng.sem_inc(scalar_for_vector, act.one(scalar_for_vector))

        def setup_dve(v):
            v.wait_ge(loads_for_vector, v.due(loads_for_vector, 32))
            v.wait_ge(gpsimd_for_vector, v.due(gpsimd_for_vector))
            v.eng.tensor_copy(IDX, ptab_i).then_inc(vector_done, 1)
            v.wait_ge(vector_done, v.done(vector_done))
            v.eng.tensor_scalar(IDX, IDX, float(PAGE), prow[:, 0:1], ALU.mult, ALU.add).then_inc(vector_done, 1)
            v.wait_ge(vector_done, v.done(vector_done))
            v.eng.tensor_copy(idx_u, IDX).then_inc(vector_done, 1)
            v.wait_ge(vector_done, v.done(vector_done))
            for i, (r0, n) in enumerate(ROWT):
                v.wait_ge(bank_full_v, v.due(bank_full_v))
                b = v.rv.next()
                v.eng.tensor_copy(xT[:, 0:4, r0:r0 + n], four(b, n)).then_inc(bank_read_v, 1)
                v.wait_ge(bank_read_v, v.done(bank_read_v))
                v.wait_ge(scalar_for_vector, v.due(scalar_for_vector))
                v.eng.sem_inc(weights_used, v.one(weights_used))

        arena.at = base

        hT = arena.take(P, KD, R)
        after_h = arena.at
        sq = arena.take(P, 2, KD, 256)
        rs = arena.take(P, 2, 256)
        after_norm = arena.at

        NCH = [(c, 256) for c in range(0, TP, 256)] + [(TP, R - TP)]

        def norm_dve(v, gi, src=None, dst=None, chunks=NCH):
            src = xT if src is None else src
            dst = hT if dst is None else dst

            def squares(k):
                c0, n = chunks[k]
                v.eng.tensor_tensor(sq[:, k % 2, :, 0:n], src[:, :, c0:c0 + n], src[:, :, c0:c0 + n], ALU.mult).then_inc(vector_for_tensor, 1)
                v.wait_ge(vector_for_tensor, v.done(vector_for_tensor))
            squares(0)
            for i, (c0, n) in enumerate(chunks):
                if i + 1 < len(chunks):
                    squares(i + 1)
                v.wait_ge(scalar_for_vector, v.due(scalar_for_vector))
                r = rs[:, i % 2, 0:n]
                v.eng.reciprocal(r, r).then_inc(vector_done, 1)
                v.wait_ge(vector_done, v.done(vector_done))
                for k in range(KD):
                    v.eng.scalar_tensor_tensor(out=dst[:, k, c0:c0 + n], in0=src[:, k, c0:c0 + n],
                                                    scalar=norm_g[:, gi, k:k + 1], in1=r,
                                                    op0=ALU.mult, op1=ALU.mult).then_inc(vector_done, 1)
                    v.wait_ge(vector_done, v.done(vector_done))
                v.eng.sem_inc(vector_for_scalar, v.one(vector_for_scalar))

        def norm_pe(pe, chunks=NCH):
            for i, (c0, n) in enumerate(chunks):
                pe.wait_ge(vector_for_tensor, pe.due(vector_for_tensor))
                pe.wait_ge(bank_read_a, pe.ra.freed())
                b = pe.ra.next()
                for k in range(KD):
                    ins = pe.eng.matmul(b[:, 0:n], ones, sq[:, i % 2, k, 0:n], start=(k == 0), stop=(k == KD - 1))
                ins.then_inc(bank_full_a, 1)

        def norm_act(act, chunks=NCH):
            for i, (c0, n) in enumerate(chunks):
                act.wait_ge(bank_full_a, act.due(bank_full_a))
                b = act.ra.next()
                if i >= 2:
                    act.wait_ge(vector_for_scalar, act.due(vector_for_scalar))
                act.eng.activation(rs[:, i % 2, 0:n], b[:, 0:n], ACT.Sqrt, bias=eps[:, 0:1], scale=1.0 / D).then_inc(bank_read_a, 1)
                act.wait_ge(bank_read_a, act.done(bank_read_a))
                act.eng.sem_inc(scalar_for_vector, act.one(scalar_for_vector))
            act.wait_ge(vector_for_scalar, act.due(vector_for_scalar, min(2, len(chunks))))

        arena.at = after_h
        actT = arena.take(P, FT, R)
        ff_tail = arena.at
        wup = arena.take(P, 2, 2, KD, P)
        sg = arena.take(P, 2, BANK)
        wdn = arena.array[:, base:base + 3 * FT * P].rearrange("p (s k c) -> p s k c", s=3, k=FT)
        assert base + 3 * FT * P <= after_h or True
        wdn = arena.array[:, base:base + 2 * FT * P].rearrange("p (s k c) -> p s k c", s=2, k=FT)
        assert base + 2 * FT * P <= after_h

        PPS = 4
        PSTEPS = NB * NPG // PPS
        SPB = NPG // PPS
        gbuf = arena.take(P, PPS, 256)
        wbuf = arena.take(P, PPS, 256)
        WP = arena.take(P, 256)
        CTb = arena.take(64, 4, 2 * NPG)

        def ff_first_sp(sp, w, pages=False):
            for f in range(2):
                ff_load(sp, w, f)
            if pages:
                for k in range(2):
                    sp.eng.dma_start(WP[64 * k:64 * k + 64], I["nsa_wpos"][0].rearrange("l c g d -> l (c g d)"),
                                     allow_slow_non_contiguous=True).then_inc(loads_for_vector, 16)

        def ff_load(sp, w, f):
            cols = w[0].rearrange("(k p) c -> p k c", p=P)
            for half in range(2):
                sp.eng.dma_start(wup[:, f % 2, half], cols[:, :, half * FF + f * P:half * FF + (f + 1) * P],
                                 allow_slow_non_contiguous=True).then_inc(weights_in[f % 2], 16)

        def ff_up_sp(sp, w):
            for f in range(2, FT):
                sp.wait_ge(weights_used, sp.due(weights_used))
                ff_load(sp, w, f)
            sp.wait_ge(weights_used, sp.due(weights_used, 2))

        def ff_up_pe(pe, pages=False):
            for f in range(FT):
                pe.wait_ge(weights_in[f % 2], pe.due(weights_in[f % 2], 32))
                for ci, (c0, n) in enumerate(CHUNKS):
                    for ring, half in ((pe.ra, 0), (pe.rv, 1)):
                        pe.wait_ge(ring.read, ring.freed())
                        b = ring.next()
                        for k in range(KD):
                            ins = pe.eng.matmul(b[:, 0:n], wup[:, f % 2, half, k], hT[:, k, c0:c0 + n],
                                                start=(k == 0), stop=(k == KD - 1))
                        ins.then_inc(ring.full, 1)
                    if pages and 3 * f + ci < PSTEPS:
                        pe.wait_ge(vector_for_tensor, pe.due(vector_for_tensor))
                        pe.wait_ge(bank_read_v, pe.rv.freed())
                        b = pe.rv.next()
                        for q in range(4):
                            for s in range(PPS):
                                o = (q * PPS + s) * 2
                                ins = pe.eng.matmul(b[0:64, o:o + 2], wbuf[:, s, q * 64:(q + 1) * 64], bsel,
                                                    start=True, stop=True)
                        ins.then_inc(bank_full_v, 1)

        def ff_up_act(act):
            for i in range(FT * len(CHUNKS)):
                c0, n = CHUNKS[i % 3]
                if i >= 2:
                    act.wait_ge(vector_for_scalar, act.due(vector_for_scalar))
                act.wait_ge(bank_full_a, act.due(bank_full_a))
                b = act.ra.next()
                act.eng.activation(sg[:, i % 2, 0:n], b[:, 0:n], ACT.Silu).then_inc(bank_read_a, 1)
                act.wait_ge(bank_read_a, act.done(bank_read_a))
                act.eng.sem_inc(scalar_for_vector, act.one(scalar_for_vector))
            act.wait_ge(vector_for_scalar, act.due(vector_for_scalar, 2))

        def ff_up_dve(v, pages=False):
            if pages:
                v.wait_ge(loads_for_vector, v.due(loads_for_vector, 32))
            for i in range(FT * len(CHUNKS)):
                c0, n = CHUNKS[i % 3]
                if pages and i < PSTEPS:
                    for s in range(PPS):
                        v.wait_ge(pages_in[s], v.due(pages_in[s], 16))
                    v.eng.tensor_tensor(wbuf, gbuf, WP.unsqueeze(1).broadcast_to([P, PPS, 256]), ALU.mult).then_inc(vector_for_tensor, 1)
                    v.wait_ge(vector_for_tensor, v.done(vector_for_tensor))
                    v.eng.sem_inc(vector_for_gpsimd, v.one(vector_for_gpsimd))
                v.wait_ge(bank_full_v, v.due(bank_full_v))
                b = v.rv.next()
                v.wait_ge(scalar_for_vector, v.due(scalar_for_vector))
                v.eng.tensor_tensor(actT[:, i // 3, c0:c0 + n], b[:, 0:n], sg[:, i % 2, 0:n], ALU.mult).then_inc(bank_read_v, 1)
                v.wait_ge(bank_read_v, v.done(bank_read_v))
                v.eng.sem_inc(vector_for_scalar, v.one(vector_for_scalar))
                if i % 3 == 2:
                    v.eng.sem_inc(weights_used, v.one(weights_used))
                if pages and i < PSTEPS:
                    v.wait_ge(bank_full_v, v.due(bank_full_v))
                    b = v.rv.next()
                    if i % SPB == 0 and i:
                        v.wait_ge(gpsimd_for_vector, v.due(gpsimd_for_vector))
                    k = i % SPB * 2 * PPS
                    v.eng.tensor_copy(CTb[:, :, k:k + 2 * PPS],
                                                   b[0:64, 0:8 * PPS].rearrange("p (q k) -> p q k", q=4)).then_inc(bank_read_v, 1)
                    v.wait_ge(bank_read_v, v.done(bank_read_v))
                    if i % SPB == SPB - 1:
                        v.eng.sem_inc(blocks_pooled, v.one(blocks_pooled))
            if pages:
                v.wait_ge(gpsimd_for_vector, v.due(gpsimd_for_vector))

        def pages_gp(gp):
            g = gp.eng
            for i in range(PSTEPS):
                if i:
                    gp.wait_ge(vector_for_gpsimd, gp.due(vector_for_gpsimd))
                for s in range(PPS):
                    n = i * PPS + s
                    g.indirect_dma_start(out=gbuf[:, s], out_offset=None, in_=rows_of(I["cache_nsa_cmp"]),
                                                 in_offset=bass.IndirectOffsetOnAxis(ap=idx_u[:, n:n + 1], axis=0)).then_inc(pages_in[s], 16)
                if i % SPB == 1 and i > SPB:
                    store_pooled(gp, i // SPB - 1)
            gp.wait_ge(vector_for_gpsimd, gp.due(vector_for_gpsimd))
            store_pooled(gp, NB - 1)

        def store_pooled(gp, q):
            gp.wait_ge(blocks_pooled, gp.due(blocks_pooled))
            gp.eng.dma_start(pooled[:, :, q * 2 * NPG:(q + 1) * 2 * NPG], CTb,
                             allow_slow_non_contiguous=True).then_inc(rows_stored, 16)
            gp.wait_ge(rows_stored, gp.due(rows_stored, 16))
            gp.eng.sem_inc(gpsimd_for_vector, gp.one(gpsimd_for_vector))

        def rows_of(cache):
            return cache[0].rearrange("p l c g d -> (p l) (c g d)")

        def ff_down_sp(sp, w):
            cols = w[0].rearrange("(k p) c -> p k c", p=P)
            for d in range(KD):
                if d >= 2:
                    sp.wait_ge(weights_used, sp.due(weights_used))
                sp.eng.dma_start(wdn[:, d % 2], cols[:, :, d * P:(d + 1) * P],
                                 allow_slow_non_contiguous=True).then_inc(weights_in[d % 2], 16)
            sp.wait_ge(weights_used, sp.due(weights_used, 2))

        def ff_down_pe(pe):
            for d in range(KD):
                pe.wait_ge(weights_in[d % 2], pe.due(weights_in[d % 2], 16))
                for c0, n in CHUNKS:
                    pe.wait_ge(bank_read_v, pe.rv.freed())
                    b = pe.rv.next()
                    for k in range(FT):
                        ins = pe.eng.matmul(b[:, 0:n], wdn[:, d % 2, k], actT[:, k, c0:c0 + n],
                                            start=(k == 0), stop=(k == FT - 1))
                    ins.then_inc(bank_full_v, 1)

        def ff_down_dve(v):
            for d in range(KD):
                for c0, n in CHUNKS:
                    v.wait_ge(bank_full_v, v.due(bank_full_v))
                    b = v.rv.next()
                    v.eng.scalar_tensor_tensor(out=xT[:, d, c0:c0 + n], in0=b[:, 0:n], scalar=0.5,
                                                            in1=xT[:, d, c0:c0 + n], op0=ALU.mult, op1=ALU.add).then_inc(bank_read_v, 1)
                    v.wait_ge(bank_read_v, v.done(bank_read_v))
                v.eng.sem_inc(weights_used, v.one(weights_used))

        arena.at = after_norm
        wt = arena.take(P, 3, KD, P)
        wr = arena.take(P, KD, 1048)
        wif = arena.take(P, KD, 8)
        stg = arena.take(P, 2, R)
        stgr = arena.take(P, 2, PR_W)

        def proj_first_sp(sp):
            cols = I["w_in"][0].rearrange("(k p) c -> p k c", p=P)
            for j in range(3):
                sp.eng.dma_start(wt[:, j], cols[:, :, T_COLS[j]:T_COLS[j] + P],
                                 allow_slow_non_contiguous=True).then_inc(weights_in[j], 16)
            sp.eng.dma_start(wif, cols[:, :, ML0 + 768:ML0 + 776],
                             allow_slow_non_contiguous=True).then_inc(loads_for_tensor, 16)
            for c, o, n in R_GROUPS:
                sp.eng.dma_start(wr[:, :, o:o + n], cols[:, :, c:c + n],
                                 allow_slow_non_contiguous=True).then_inc(loads_for_tensor, 16)

        def proj_sp(sp):
            cols = I["w_in"][0].rearrange("(k p) c -> p k c", p=P)
            for j, c in enumerate(T_COLS):
                if j < 3:
                    continue
                sp.wait_ge(weights_used, sp.due(weights_used))
                sp.eng.dma_start(wt[:, j % 3], cols[:, :, c:c + P],
                                 allow_slow_non_contiguous=True).then_inc(weights_in[j % 3], 16)
            sp.wait_ge(weights_used, sp.due(weights_used, 3))

        def proj_pe(pe):
            for j in range(len(T_COLS) + 1):
                if j < len(T_COLS):
                    pe.wait_ge(weights_in[j % 3], pe.due(weights_in[j % 3], 16))
                else:
                    pe.wait_ge(loads_for_tensor, pe.due(loads_for_tensor, 64))
                for c0, n in CHUNKS:
                    pe.wait_ge(bank_read_a, pe.ra.freed())
                    b = pe.ra.next()
                    for k in range(KD):
                        w = wt[:, j % 3, k] if j < len(T_COLS) else wif[:, k]
                        m = P if j < len(T_COLS) else 8
                        ins = pe.eng.matmul(b[0:m, 0:n], w, hT[:, k, c0:c0 + n], start=(k == 0), stop=(k == KD - 1))
                    ins.then_inc(bank_full_a, 1)
            for r0, m in ROWT:
                for _, o, n in R_GROUPS:
                    pe.wait_ge(bank_read_v, pe.rv.freed())
                    b = pe.rv.next()
                    for k in range(KD):
                        ins = pe.eng.matmul(b[0:m, 0:n], hT[:, k, r0:r0 + m], wr[:, k, o:o + n],
                                            start=(k == 0), stop=(k == KD - 1))
                    ins.then_inc(bank_full_v, 1)

        def proj_act(act):
            for j in range(len(T_COLS) + 1):
                if j >= 2:
                    act.wait_ge(slot_stored[j % 2], act.due(slot_stored[j % 2], 16))
                m = P if j < len(T_COLS) else 8
                for c0, n in CHUNKS:
                    act.wait_ge(bank_full_a, act.due(bank_full_a))
                    b = act.ra.next()
                    act.eng.copy(stg[0:m, j % 2, c0:c0 + n], b[0:m, 0:n]).then_inc(bank_read_a, 1)
                    act.wait_ge(bank_read_a, act.done(bank_read_a))
                if j < len(T_COLS):
                    act.eng.sem_inc(weights_used, act.one(weights_used))
                act.eng.dma_start(pT[j * P:j * P + m], stg[0:m, j % 2],
                                 allow_slow_non_contiguous=True).then_inc(slot_stored[j % 2], 16)
            act.wait_ge(slot_stored[0], act.due(slot_stored[0], 16))
            act.wait_ge(slot_stored[1], act.due(slot_stored[1], 16))

        def proj_dve(v):
            for i, (r0, m) in enumerate(ROWT):
                if i >= 2:
                    v.wait_ge(sync_for_vector, v.due(sync_for_vector))
                for _, o, n in R_GROUPS:
                    v.wait_ge(bank_full_v, v.due(bank_full_v))
                    b = v.rv.next()
                    v.eng.tensor_copy(stgr[0:m, i % 2, o:o + n], b[0:m, 0:n]).then_inc(bank_read_v, 1)
                    v.wait_ge(bank_read_v, v.done(bank_read_v))
                v.eng.sem_inc(vector_for_gpsimd, v.one(vector_for_gpsimd))
            v.wait_ge(sync_for_vector, v.due(sync_for_vector, 2))

        def proj_gp(gp):
            for i, (r0, m) in enumerate(ROWT):
                gp.wait_ge(vector_for_gpsimd, gp.due(vector_for_gpsimd))
                gp.eng.dma_start(pR[r0:r0 + m], stgr[0:m, i % 2],
                                 allow_slow_non_contiguous=True).then_inc(rows_stored, 16)
                gp.wait_ge(rows_stored, gp.due(rows_stored, 16))
                gp.eng.sem_inc(sync_for_vector, gp.one(sync_for_vector))

        arena.at = base
        yrow = arena.take(P, 2, D)

        def final_pe(pe):
            for i, (r0, m) in enumerate(ROWT):
                for ring, k0 in ((pe.rv, 0), (pe.ra, 4)):
                    pe.wait_ge(ring.read, ring.freed())
                    b = ring.next()
                    for k in range(4):
                        ins = pe.eng.transpose(b[0:m, k * P:(k + 1) * P], xT[:, k0 + k, r0:r0 + m], ident)
                    ins.then_inc(ring.full, 1)

        def final_dve(v):
            for i, (r0, m) in enumerate(ROWT):
                if i >= 2:
                    v.wait_ge(sync_for_vector, v.due(sync_for_vector))
                v.wait_ge(bank_full_v, v.due(bank_full_v))
                b = v.rv.next()
                v.eng.tensor_copy(yrow[0:m, i % 2, 0:512], b[0:m]).then_inc(bank_read_v, 1)
                v.wait_ge(bank_read_v, v.done(bank_read_v))
                v.eng.sem_inc(vector_for_sync, v.one(vector_for_sync))
            v.wait_ge(sync_for_vector, v.due(sync_for_vector, 2))

        def final_act(act):
            for i, (r0, m) in enumerate(ROWT):
                if i >= 2:
                    act.wait_ge(sync_for_scalar, act.due(sync_for_scalar))
                act.wait_ge(bank_full_a, act.due(bank_full_a))
                b = act.ra.next()
                act.eng.copy(yrow[0:m, i % 2, 512:1024], b[0:m]).then_inc(bank_read_a, 1)
                act.wait_ge(bank_read_a, act.done(bank_read_a))
                act.eng.sem_inc(scalar_for_sync, act.one(scalar_for_sync))
            act.wait_ge(sync_for_scalar, act.due(sync_for_scalar, 2))

        def final_sp(sp):
            yp, ys = O["y_prompt"][0], O["y_sample"].rearrange("b t d -> (b t) d")
            for i, (r0, m) in enumerate(ROWT):
                sp.wait_ge(vector_for_sync, sp.due(vector_for_sync))
                sp.wait_ge(scalar_for_sync, sp.due(scalar_for_sync))
                sp.eng.dma_start(yp[r0:r0 + m] if r0 < TP else ys, yrow[0:m, i % 2],
                                 allow_slow_non_contiguous=True).then_inc(outputs_stored, 16)
                sp.wait_ge(outputs_stored, sp.due(outputs_stored, 16))
                sp.eng.sem_inc(sync_for_vector, sp.one(sync_for_vector))
                sp.eng.sem_inc(sync_for_scalar, sp.one(sync_for_scalar))

        arena.at = base
        PX = arena.take(P, 8, R)
        PV = arena.take(P, 8, R)
        rR, rK, rV, rB = PX[:, 0:2], PX[:, 2:4], PX[:, 4:6], PX[:, 6:8]
        LD, AA, KK, CC = PV[:, 0:2], PV[:, 2:4], PV[:, 4:6], PV[:, 6:8]
        rwG = arena.take(P, 2, R)
        BON = arena.take(P, 2, R)
        rw_free = arena.at
        TT2 = arena.take(P, 2, R)
        WW = arena.take(P, 2, R)
        A64 = arena.array[0:64, base + 8 * R:base + 12 * R].rearrange("p (h c) -> p h c", h=4)
        B64 = arena.array[0:64, base + 12 * R:base + 16 * R].rearrange("p (h c) -> p h c", h=4)
        K64 = arena.take(64, 4, R)
        R64 = arena.take(64, 4, R)
        rmask = arena.array[:, arena.at - 8 * R:arena.at - 7 * R]
        th = arena.array[:, arena.at - 7 * R:arena.at - 6 * R]
        sgd = arena.array[:, arena.at - 6 * R:arena.at - 5 * R]
        rw_cols = arena.take(P, 10, 2)
        muc = arena.take(P, 8)
        WC = arena.take(64, 4, 24)
        WCp = arena.take(P, 2, 24)
        lora_at = arena.at
        w2p, a2p, g2w = (arena.take(P, 256) for _ in range(3))
        rw_tail = arena.at
        C_W0, C_A0, C_KK, C_KA, C_RK, C_GG, C_GB, C_OK = range(8)

        def col(i, j):
            return rw_cols[:, i, j:j + 1]

        def rwkv_sp(sp):
            sp.eng.dma_start(PX, pT[0:1024].rearrange("(j p) r -> p j r", p=P),
                             allow_slow_non_contiguous=True).then_inc(loads_for_vector, 16)
            pv = pT[0:1024].rearrange("(j p) r -> p j r", p=P)
            sp.eng.dma_start(PV[:, :, 1:TP], pv[:, :, 0:TP - 1],
                             allow_slow_non_contiguous=True).then_inc(loads_for_vector, 16)
            for j in range(8):
                sp.eng.dma_start(PV[:, j, TP:R].rearrange("p (b t) -> p b t", b=NB)[:, :, 1:TS], pv[:, j, TP:R].rearrange("p (b t) -> p b t", b=NB)[:, :, 0:TS - 1],
                                 allow_slow_non_contiguous=True).then_inc(loads_for_vector, 16)
                sp.eng.dma_start(PV[:, j, TP:R:TS], I["state_rwkv_shift"][0, :, 0, j * P:(j + 1) * P].rearrange("b p -> p b"),
                                 allow_slow_non_contiguous=True).then_inc(loads_for_vector, 16)
            for i, name in enumerate(("rw_w0", "rw_a0", "rw_kk", "rw_ka", "rw_rk", "rw_gn_g", "rw_gn_b")):
                src = I[name][0].rearrange("h d -> (h d)") if name == "rw_rk" else I[name][0]
                sp.eng.dma_start(rw_cols[:, i], src.rearrange("(j p) -> p j", p=P),
                                 allow_slow_non_contiguous=True).then_inc(loads_for_vector, 16)
            sp.eng.dma_start(muc, I["rw_mu"][0].rearrange("(j p) -> p j", p=P),
                             allow_slow_non_contiguous=True).then_inc(loads_for_vector, 16)
            sp.wait_ge(gpsimd_for_sync, sp.due(gpsimd_for_sync))
            sp.eng.dma_start(w2p[0:64], I["rw_w2"][0],
                             allow_slow_non_contiguous=True).then_inc(loads_for_tensor, 16)
            sp.eng.dma_start(a2p[64:128], I["rw_a2"][0],
                             allow_slow_non_contiguous=True).then_inc(loads_for_tensor, 16)
            sp.eng.dma_start(g2w, I["rw_g2"][0],
                             allow_slow_non_contiguous=True).then_inc(loads_for_tensor, 16)
            sp.eng.dma_start(O["shift_p"][0, 0, 0].rearrange("(c o) -> c o", o=1), pT[0:1024, TP - 1:TP],
                             allow_slow_non_contiguous=True).then_inc(outputs_stored, 16)
            for b in range(NB):
                t = TP + b * TS + TS - 1
                sp.eng.dma_start(O["shift_s"][0, b, 0].rearrange("(c o) -> c o", o=1), pT[0:1024, t:t + 1],
                                 allow_slow_non_contiguous=True).then_inc(outputs_stored, 16)
            sp.wait_ge(vector_for_sync, sp.due(vector_for_sync))
            for dst, src in ((A64, TT2), (B64, rB), (K64, rK), (R64, rR), (WC, WCp)):
                for e in range(2):
                    sp.eng.dma_start(dst[:, e:4:2], src[64 * e:64 * e + 64],
                                     allow_slow_non_contiguous=True).then_inc(heads_moved, 16)
            sp.wait_ge(heads_moved, sp.due(heads_moved, 160))
            sp.wait_ge(outputs_stored, sp.due(outputs_stored, 16 * 9))

        IN_RW = 16 * (2 + 16 + 7 + 1)

        def rwkv_gp(gp):
            g = gp.eng
            g.memset(PV[:, :, 0:1], 0.0).then_inc(gpsimd_done, 1)
            gp.wait_ge(gpsimd_done, gp.done(gpsimd_done))
            g.memset(w2p, 0.0).then_inc(gpsimd_done, 1)
            gp.wait_ge(gpsimd_done, gp.done(gpsimd_done))
            g.memset(a2p, 0.0).then_inc(gpsimd_done, 1)
            gp.wait_ge(gpsimd_done, gp.done(gpsimd_done))
            g.memset(rmask, 1.0).then_inc(gpsimd_done, 1)
            gp.wait_ge(gpsimd_done, gp.done(gpsimd_done))
            g.memset(rmask[:, 0:TP:64], 0.0).then_inc(gpsimd_done, 1)
            gp.wait_ge(gpsimd_done, gp.done(gpsimd_done))
            g.memset(rmask[:, TP:R:TS], 0.0).then_inc(gpsimd_done, 1)
            gp.wait_ge(gpsimd_done, gp.done(gpsimd_done))
            gp.eng.sem_inc(gpsimd_for_sync, gp.one(gpsimd_for_sync))
            gp.eng.sem_inc(gpsimd_for_vector, gp.one(gpsimd_for_vector))

        def rwkv_dve(v):
            e = v.eng
            v.wait_ge(loads_for_vector, v.due(loads_for_vector, IN_RW))
            v.wait_ge(gpsimd_for_vector, v.due(gpsimd_for_vector))
            e.tensor_tensor(PV, PV, PX, ALU.subtract).then_inc(vector_done, 1)
            v.wait_ge(vector_done, v.done(vector_done))
            for j in range(8):
                e.scalar_tensor_tensor(out=PX[:, j], in0=PV[:, j], scalar=muc[:, j:j + 1], in1=PX[:, j],
                                            op0=ALU.mult, op1=ALU.add).then_inc(vector_done, 1)
                v.wait_ge(vector_done, v.done(vector_done))
            v.eng.sem_inc(vector_for_scalar, v.one(vector_for_scalar))
            for j in range(2):
                e.tensor_scalar(KK[:, j], rK[:, j], col(C_KK, j), None, ALU.mult).then_inc(vector_done, 1)
                v.wait_ge(vector_done, v.done(vector_done))
                e.tensor_scalar(col(C_OK, j), col(C_KA, j), -1.0, 1.0, ALU.mult, ALU.add).then_inc(vector_done, 1)
                v.wait_ge(vector_done, v.done(vector_done))
            e.tensor_tensor(TT2, KK, KK, ALU.mult).then_inc(vector_for_tensor, 1)
            v.wait_ge(vector_for_tensor, v.done(vector_for_tensor))
            v.wait_ge(scalar_for_vector, v.due(scalar_for_vector))
            e.tensor_scalar(LD, LD, -float(np.exp(-0.5)), None, ALU.mult).then_inc(vector_done, 1)
            v.wait_ge(vector_done, v.done(vector_done))
            e.tensor_scalar(WW, WW, 1e-12, None, ALU.max).then_inc(vector_done, 1)
            v.wait_ge(vector_done, v.done(vector_done))
            e.reciprocal(WW, WW).then_inc(vector_done, 1)
            v.wait_ge(vector_done, v.done(vector_done))
            e.tensor_tensor(KK, KK, WW, ALU.mult).then_inc(vector_done, 1)
            v.wait_ge(vector_done, v.done(vector_done))
            for j in range(2):
                e.tensor_scalar(TT2[:, j], AA[:, j], col(C_KA, j), col(C_OK, j), ALU.mult, ALU.add).then_inc(vector_done, 1)
                v.wait_ge(vector_done, v.done(vector_done))
            e.tensor_tensor(rK, rK, TT2, ALU.mult).then_inc(vector_done, 1)
            v.wait_ge(vector_done, v.done(vector_done))
            for j in range(2):
                e.scalar_tensor_tensor(out=TT2[:, j], in0=rR[:, j], scalar=col(C_RK, j), in1=rK[:, j],
                                            op0=ALU.mult, op1=ALU.mult).then_inc(vector_done, 1)
                v.wait_ge(vector_done, v.done(vector_done))
            v.eng.sem_inc(vector_for_tensor, v.one(vector_for_tensor))
            for j in range(2):
                for c0, n in CHUNKS:
                    v.wait_ge(bank_full_v, v.due(bank_full_v))
                    b = v.rv.next()
                    e.tensor_tensor(BON[:, j, c0:c0 + n], b[:, 0:n], rV[:, j, c0:c0 + n], ALU.mult).then_inc(bank_read_v, 1)
                    v.wait_ge(bank_read_v, v.done(bank_read_v))
            for j in range(2):
                e.tensor_tensor_scan(CC[:, j], rmask, LD[:, j], 0.0, ALU.mult, ALU.add).then_inc(vector_done, 1)
                v.wait_ge(vector_done, v.done(vector_done))
            e.tensor_tensor(LD, CC, LD, ALU.subtract).then_inc(vector_for_scalar, 1)
            v.wait_ge(vector_for_scalar, v.done(vector_for_scalar))
            v.wait_ge(scalar_for_vector, v.due(scalar_for_vector))
            e.tensor_copy(WCp[:, :, 0:16], WW[:, :, 63:TP:64]).then_inc(vector_done, 1)
            v.wait_ge(vector_done, v.done(vector_done))
            e.tensor_copy(WCp[:, :, 16:24], WW[:, :, TP + TS - 1:R:TS]).then_inc(vector_done, 1)
            v.wait_ge(vector_done, v.done(vector_done))
            e.tensor_tensor(rR, rR, WW, ALU.mult).then_inc(vector_done, 1)
            v.wait_ge(vector_done, v.done(vector_done))
            e.tensor_tensor(TT2, KK, LD, ALU.mult).then_inc(vector_done, 1)
            v.wait_ge(vector_done, v.done(vector_done))
            e.tensor_tensor(rB, KK, AA, ALU.mult).then_inc(vector_done, 1)
            v.wait_ge(vector_done, v.done(vector_done))
            e.tensor_tensor(rB, rB, CC, ALU.mult).then_inc(vector_done, 1)
            v.wait_ge(vector_done, v.done(vector_done))
            e.tensor_tensor(rK, rK, CC, ALU.mult).then_inc(vector_done, 1)
            v.wait_ge(vector_done, v.done(vector_done))
            v.eng.sem_inc(vector_for_sync, v.one(vector_for_sync))

        def rwkv_act(act):
            a = act.eng
            act.wait_ge(vector_for_scalar, act.due(vector_for_scalar))
            a.activation(th, PX[:, 6], ACT.Tanh).then_inc(scalar_done, 1)
            act.wait_ge(scalar_done, act.done(scalar_done))
            a.activation(sgd, PX[:, 7], ACT.Sigmoid).then_inc(scalar_done, 1)
            act.wait_ge(scalar_done, act.done(scalar_done))
            act.eng.sem_inc(scalar_for_tensor, act.one(scalar_for_tensor))
            for j in range(2):
                for c0, n in CHUNKS:
                    act.wait_ge(bank_full_a, act.due(bank_full_a))
                    b = act.ra.next()
                    a.activation(LD[:, j, c0:c0 + n], b[:, 0:n], ACT.Sigmoid, bias=col(C_W0, j)).then_inc(bank_read_a, 1)
                    act.wait_ge(bank_read_a, act.done(bank_read_a))
                    act.wait_ge(bank_full_a, act.due(bank_full_a))
                    b = act.ra.next()
                    a.activation(AA[:, j, c0:c0 + n], b[:, 0:n], ACT.Sigmoid, bias=col(C_A0, j)).then_inc(bank_read_a, 1)
                    act.wait_ge(bank_read_a, act.done(bank_read_a))
                    act.wait_ge(bank_full_a, act.due(bank_full_a))
                    b = act.ra.next()
                    a.copy(rwG[:, j, c0:c0 + n], b[:, 0:n]).then_inc(bank_read_a, 1)
                    act.wait_ge(bank_read_a, act.done(bank_read_a))
            for j in range(2):
                for c0, n in CHUNKS:
                    act.wait_ge(bank_full_a, act.due(bank_full_a))
                    b = act.ra.next()
                    a.activation(WW[:, j, c0:c0 + n], b[:, 0:n], ACT.Sqrt).then_inc(bank_read_a, 1)
                    act.wait_ge(bank_read_a, act.done(bank_read_a))
            act.eng.sem_inc(scalar_for_vector, act.one(scalar_for_vector))
            act.wait_ge(vector_for_scalar, act.due(vector_for_scalar))
            a.activation(WW, CC, ACT.Exp).then_inc(scalar_done, 1)
            act.wait_ge(scalar_done, act.done(scalar_done))
            a.activation(CC, CC, ACT.Exp, scale=-1.0).then_inc(scalar_done, 1)
            act.wait_ge(scalar_done, act.done(scalar_done))
            a.activation(LD, LD, ACT.Exp).then_inc(scalar_done, 1)
            act.wait_ge(scalar_done, act.done(scalar_done))
            act.eng.sem_inc(scalar_for_vector, act.one(scalar_for_vector))

        def rwkv_pe(pe):
            pe.wait_ge(loads_for_tensor, pe.due(loads_for_tensor, 48))
            pe.wait_ge(scalar_for_tensor, pe.due(scalar_for_tensor))
            for j in range(2):
                for c0, n in CHUNKS:
                    for w, x in ((w2p, th), (a2p, PX[:, 6]), (g2w, sgd)):
                        pe.wait_ge(bank_read_a, pe.ra.freed())
                        b = pe.ra.next()
                        pe.eng.matmul(b[:, 0:n], w[:, j * P:(j + 1) * P], x[:, c0:c0 + n],
                                                      start=True, stop=True).then_inc(bank_full_a, 1)
            for ring in (pe.ra, pe.rv):
                pe.wait_ge(vector_for_tensor, pe.due(vector_for_tensor))
                for j in range(2):
                    for c0, n in CHUNKS:
                        pe.wait_ge(ring.read, ring.freed())
                        b = ring.next()
                        pe.eng.matmul(b[:, 0:n], blk, TT2[:, j, c0:c0 + n], start=True, stop=True).then_inc(ring.full, 1)

        arena.at = rw_tail
        YP = rR
        spare = arena.array[:, rw_free:rw_free + 4 * R]
        work = Arena(spare, 4 * R)
        tail = Arena(arena.array[:, rw_tail:size], size - rw_tail)
        MT, NT, E1, E2 = (work.take(P, 4, P) for _ in range(4))
        TM, TT = work.take(P, 4, P), work.take(P, 4, P)
        XL, ML = work.take(P, 4, P), tail.take(P, 4, P)
        BKr = work.take(P, 2, 256)
        Yt = tail.take(64, 4, P)
        tail_at = tail.at
        VP = tail.take(P, 2, 256)
        SAP = tail.take(P, 2, 256)
        X2 = tail.take(P, 256)
        Z = tail.take(64, 4, 64)
        Zo = tail.take(64, 4, 64)

        def hv(b, n, m=P):
            return b[0:m, 0:4 * n].rearrange("p (h c) -> p h c", h=4)

        def bc4(m, n):
            return m[0:n, 0:n].unsqueeze(1).broadcast_to([n, 4, n])

        def tile_matrices_pe(pe, t0, n):
            for e, srcs in ((0, (rB, rK)), (1, (rV,))):
                pe.wait_ge(bank_read_v, pe.rv.freed())
                b = pe.rv.next()
                for i, src in enumerate(srcs):
                    for j in range(2):
                        ins = pe.eng.transpose(b[0:n, i * 256 + j * P:i * 256 + (j + 1) * P], src[:, j, t0:t0 + n], ident)
                ins.then_inc(bank_full_v, 1)
            for lhs, rhs in ((B64, A64), (K64, A64), (B64, R64), (K64, R64)):
                pe.wait_ge(bank_read_v, pe.rv.freed())
                b = pe.rv.next()
                for h in range(4):
                    ins = pe.eng.matmul(b[0:n, h * n:(h + 1) * n], lhs[:, h, t0:t0 + n], rhs[:, h, t0:t0 + n],
                                        start=True, stop=True)
                ins.then_inc(bank_full_v, 1)

        def tile_matrices_dve(v, n, incl, strict, M, v_rows):
            e = v.eng
            v.wait_ge(bank_full_v, v.due(bank_full_v))
            b = v.rv.next()
            e.tensor_copy(M["BK"], b[0:n].rearrange("p (i c) -> p i c", i=2)).then_inc(bank_read_v, 1)
            v.wait_ge(bank_read_v, v.done(bank_read_v))
            v_rows(v)
            for i, (m, mask) in enumerate(((M["MT"], None), (M["NT"], strict), (M["E1"], incl), (M["E2"], incl))):
                v.wait_ge(bank_full_v, v.due(bank_full_v))
                b = v.rv.next()
                if mask is None:
                    e.tensor_copy(m, hv(b, n, n)).then_inc(bank_read_v, 1)
                    v.wait_ge(bank_read_v, v.done(bank_read_v))
                else:
                    e.tensor_tensor(m, hv(b, n, n), bc4(mask, n), ALU.mult).then_inc(bank_read_v, 1)
                    v.wait_ge(bank_read_v, v.done(bank_read_v))
            e.tensor_copy(M["TM"], bc4(ident, n)).then_inc(vector_done, 1)
            v.wait_ge(vector_done, v.done(vector_done))
            e.tensor_copy(M["TT"], bc4(ident, n)).then_inc(vector_done, 1)
            v.wait_ge(vector_done, v.done(vector_done))

        def inverse_dve(v, n, M, levels):
            e = v.eng
            for l in range(levels):
                e.tensor_tensor(M["ML"], M["MT"], bc4(lm[:, l], n), ALU.mult).then_inc(vector_for_tensor, 1)
                v.wait_ge(vector_for_tensor, v.done(vector_for_tensor))
                v.wait_ge(bank_full_v, v.due(bank_full_v))
                b = v.rv.next()
                e.tensor_tensor(M["TM"], M["TM"], hv(b, n, n), ALU.subtract).then_inc(bank_read_v, 1)
                v.wait_ge(bank_read_v, v.done(bank_read_v))
                v.wait_ge(bank_full_v, v.due(bank_full_v))
                b = v.rv.next()
                e.tensor_tensor(M["TT"], M["TT"], hv(b, n, n), ALU.subtract).then_inc(bank_read_v, 1)
                v.wait_ge(bank_read_v, v.done(bank_read_v))

        def inverse_act(act, n, M, levels):
            for l in range(levels):
                act.wait_ge(bank_full_a, act.due(bank_full_a))
                b = act.ra.next()
                act.eng.copy(M["XL"], hv(b, n, n)).then_inc(bank_read_a, 1)
                act.wait_ge(bank_read_a, act.done(bank_read_a))
                act.eng.sem_inc(scalar_for_tensor, act.one(scalar_for_tensor))

        def inverse_pe(pe, n, M, levels):
            def four_heads(ring, lhs, rhs):
                pe.wait_ge(ring.read, ring.freed())
                b = ring.next()
                for h in range(4):
                    ins = pe.eng.matmul(b[0:n, h * n:(h + 1) * n], lhs[:, h], rhs[:, h], start=True, stop=True)
                ins.then_inc(ring.full, 1)
            for l in range(levels):
                pe.wait_ge(vector_for_tensor, pe.due(vector_for_tensor))
                four_heads(pe.ra, M["ML"], M["TM"])
                pe.wait_ge(scalar_for_tensor, pe.due(scalar_for_tensor))
                four_heads(pe.rv, M["TT"], M["XL"])
                four_heads(pe.rv, M["XL"], M["TT"])

        MP = dict(MT=MT, NT=NT, E1=E1, E2=E2, TM=TM, TT=TT, XL=XL, ML=ML, BK=BKr)

        def scan_dve(v):
            e = v.eng
            e.memset(VP, 0.0).then_inc(vector_done, 1)
            v.wait_ge(vector_done, v.done(vector_done))
            e.memset(SAP, 0.0).then_inc(vector_done, 1)
            v.wait_ge(vector_done, v.done(vector_done))
            e.memset(Z, 0.0).then_inc(vector_done, 1)
            v.wait_ge(vector_done, v.done(vector_done))
            for i in range(8):
                def v_rows(v):
                    v.wait_ge(bank_full_v, v.due(bank_full_v))
                    b = v.rv.next()
                    e.tensor_copy(VP[0:64, 0], b[0:64, 0:256]).then_inc(vector_done, 1)
                    v.wait_ge(vector_done, v.done(vector_done))
                    e.tensor_copy(VP[64:128, 1], b[64:128, 0:256]).then_inc(bank_read_v, 1)
                    v.wait_ge(bank_read_v, v.done(bank_read_v))
                tile_matrices_dve(v, P, incl64, strict64, MP, v_rows)
                inverse_dve(v, P, MP, 6)
                v.eng.sem_inc(vector_for_tensor, v.one(vector_for_tensor))
                for c in range(2):
                    rows = slice(64 * c, 64 * c + 64)
                    v.wait_ge(bank_full_v, v.due(bank_full_v))
                    b = v.rv.next()
                    e.tensor_scalar(SAP[rows, c], b[rows, 0:256], -1.0, None, ALU.mult).then_inc(bank_read_v, 1)
                    v.wait_ge(bank_read_v, v.done(bank_read_v))
                    v.eng.sem_inc(vector_for_tensor, v.one(vector_for_tensor))
                    v.wait_ge(bank_full_v, v.due(bank_full_v))
                    b = v.rv.next()
                    e.tensor_tensor(Z, Z, hv(b, 64, 64), ALU.add).then_inc(bank_read_v, 1)
                    v.wait_ge(bank_read_v, v.done(bank_read_v))
                    w = WC[:, :, 2 * i + c:2 * i + c + 1].broadcast_to([64, 4, 64])
                    e.tensor_tensor(Z, Z, w, ALU.mult).then_inc(vector_for_tensor, 1)
                    v.wait_ge(vector_for_tensor, v.done(vector_for_tensor))
            v.wait_ge(bank_full_v, v.due(bank_full_v))
            b = v.rv.next()
            e.tensor_copy(Zo, hv(b, 64, 64)).then_inc(bank_read_v, 1)
            v.wait_ge(bank_read_v, v.done(bank_read_v))
            v.eng.sem_inc(vector_for_sync, v.one(vector_for_sync))

        def scan_act(act):
            a = act.eng
            for i in range(8):
                inverse_act(act, P, MP, 6)
                for c in range(2):
                    act.wait_ge(bank_full_a, act.due(bank_full_a))
                    b = act.ra.next()
                    a.copy(X2, b[:, 0:256]).then_inc(bank_read_a, 1)
                    act.wait_ge(bank_read_a, act.done(bank_read_a))
                    act.eng.sem_inc(scalar_for_tensor, act.one(scalar_for_tensor))
                    act.wait_ge(bank_full_a, act.due(bank_full_a))
                    b = act.ra.next()
                    if i and not c:
                        act.wait_ge(sync_for_scalar, act.due(sync_for_scalar))
                    a.copy(Yt[:, :, 64 * c:64 * c + 64], hv(b, 64, 64)).then_inc(bank_read_a, 1)
                    act.wait_ge(bank_read_a, act.done(bank_read_a))
                act.eng.sem_inc(scalar_for_sync, act.one(scalar_for_sync))
            act.wait_ge(sync_for_scalar, act.due(sync_for_scalar))

        def scan_sp(sp):
            for i in range(8):
                sp.wait_ge(scalar_for_sync, sp.due(scalar_for_sync))
                for e in range(2):
                    sp.eng.dma_start(YP[64 * e:64 * e + 64, :, i * P:(i + 1) * P], Yt[:, e:4:2],
                                     allow_slow_non_contiguous=True).then_inc(heads_moved, 16)
                sp.wait_ge(heads_moved, sp.due(heads_moved, 32))
                sp.eng.sem_inc(sync_for_scalar, sp.one(sync_for_scalar))
            sp.wait_ge(vector_for_sync, sp.due(vector_for_sync))
            sp.eng.dma_start(O["S_p"][0, 0].rearrange("h i j -> i h j"), Zo,
                             allow_slow_non_contiguous=True).then_inc(outputs_stored, 16)
            sp.wait_ge(outputs_stored, sp.due(outputs_stored, 16))

        def scan_pe(pe):
            mm = pe.eng.matmul
            for i in range(8):
                t0 = i * P
                tile_matrices_pe(pe, t0, P)
                inverse_pe(pe, P, MP, 6)
                pe.wait_ge(vector_for_tensor, pe.due(vector_for_tensor))
                for c in range(2):
                    tc = slice(t0 + 64 * c, t0 + 64 * c + 64)
                    pe.wait_ge(bank_read_a, pe.ra.freed())
                    b = pe.ra.next()
                    for h in range(4):
                        o = b[:, h * 64:(h + 1) * 64]
                        mm(o, A64[:, h, t0:t0 + P], Z[:, h], start=True, stop=False)
                        ins = mm(o, NT[:, h], VP[:, c, h * 64:(h + 1) * 64], start=False, stop=True)
                    ins.then_inc(bank_full_a, 1)
                    pe.wait_ge(scalar_for_tensor, pe.due(scalar_for_tensor))
                    pe.wait_ge(bank_read_v, pe.rv.freed())
                    b = pe.rv.next()
                    for h in range(4):
                        ins = mm(b[:, h * 64:(h + 1) * 64], TT[:, h], X2[:, h * 64:(h + 1) * 64], start=True, stop=True)
                    ins.then_inc(bank_full_v, 1)
                    pe.wait_ge(vector_for_tensor, pe.due(vector_for_tensor))
                    pe.wait_ge(bank_read_a, pe.ra.freed())
                    b = pe.ra.next()
                    for h in range(4):
                        o, hs = b[0:64, h * 64:(h + 1) * 64], slice(h * 64, (h + 1) * 64)
                        mm(o, Z[:, h], R64[:, h, tc], start=True, stop=False)
                        mm(o, SAP[:, c, hs], E1[:, h, 64 * c:64 * c + 64], start=False, stop=False)
                        ins = mm(o, VP[:, c, hs], E2[:, h, 64 * c:64 * c + 64], start=False, stop=True)
                    ins.then_inc(bank_full_a, 1)
                    pe.wait_ge(bank_read_v, pe.rv.freed())
                    b = pe.rv.next()
                    for h in range(4):
                        o, hs = b[0:64, h * 64:(h + 1) * 64], slice(h * 64, (h + 1) * 64)
                        mm(o, BKr[:, 0, hs], SAP[:, c, hs], start=True, stop=False)
                        ins = mm(o, BKr[:, 1, hs], VP[:, c, hs], start=False, stop=True)
                    ins.then_inc(bank_full_v, 1)
                    pe.wait_ge(vector_for_tensor, pe.due(vector_for_tensor))
            pe.wait_ge(bank_read_v, pe.rv.freed())
            b = pe.rv.next()
            for h in range(4):
                ins = pe.eng.transpose(b[0:64, h * 64:(h + 1) * 64], Z[:, h], ident[0:64, 0:64])
            ins.then_inc(bank_full_v, 1)

        work = Arena(spare, 4 * R)
        tail = Arena(arena.array[:, rw_tail:size], size - rw_tail)
        MS = {k: work.take(64, 4, 64) for k in ("MT", "NT", "E1", "E2", "TM", "TT", "XL", "ML")}
        MS["BK"] = work.take(64, 2, 256)
        sV, sXT, sXr, sSA, sY = (work.take(64, 4, 64) for _ in range(5))
        sXP = [arena.array[0:64, lora_at:lora_at + 512].rearrange("p (q i) -> p q i", q=NB),
               tail.take(64, NB, 64)]
        ZS = tail.take(64, 4, NB, 64)
        S0r = tail.take(64, 4, NB, 64)
        nT = R - TP

        def scan_s_sp(sp):
            for h in range(4):
                sp.eng.dma_start(S0r[:, h], I["state_rwkv_S"][0, :, h].rearrange("b i j -> i b j"),
                                 allow_slow_non_contiguous=True).then_inc(loads_for_tensor, 16)
            sp.wait_ge(vector_for_sync, sp.due(vector_for_sync))
            for e in range(2):
                sp.eng.dma_start(YP[64 * e:64 * e + 64, :, TP:R], sY[:, e:4:2],
                                 allow_slow_non_contiguous=True).then_inc(heads_moved, 16)
            sp.wait_ge(vector_for_sync, sp.due(vector_for_sync))
            for h in range(4):
                sp.eng.dma_start(O["S_s"][0, :, h].rearrange("b i j -> i b j"), S0r[:, h],
                                 allow_slow_non_contiguous=True).then_inc(outputs_stored, 16)
            sp.wait_ge(heads_moved, sp.due(heads_moved, 32))
            sp.wait_ge(outputs_stored, sp.due(outputs_stored, 64))

        def state_turn_pe(pe, src):
            for h in range(4):
                pe.wait_ge(bank_read_v, pe.rv.freed())
                b = pe.rv.next()
                for q in range(NB):
                    ins = pe.eng.transpose(b[0:64, q * 64:(q + 1) * 64], src[:, h, q], ident[0:64, 0:64])
                ins.then_inc(bank_full_v, 1)

        def state_turn_dve(v, dst):
            for h in range(4):
                v.wait_ge(bank_full_v, v.due(bank_full_v))
                b = v.rv.next()
                v.eng.tensor_copy(dst[:, h], b[0:64].rearrange("p (q i) -> p q i", q=NB)).then_inc(bank_read_v, 1)
                v.wait_ge(bank_read_v, v.done(bank_read_v))

        def per_seq_pe(pe, x):
            pe.wait_ge(bank_read_v, pe.rv.freed())
            b = pe.rv.next()
            for h in range(4):
                for q in range(NB):
                    ins = pe.eng.matmul(b[0:64, h * 64 + q * TS:h * 64 + (q + 1) * TS], ZS[:, h, q],
                                        x[:, h, TP + q * TS:TP + (q + 1) * TS], start=True, stop=True)
            ins.then_inc(bank_full_v, 1)

        def heads_pe(pe, *pairs):
            pe.wait_ge(bank_read_v, pe.rv.freed())
            b = pe.rv.next()
            for h in range(4):
                for i, (lhs, rhs) in enumerate(pairs):
                    ins = pe.eng.matmul(b[0:64, h * 64:(h + 1) * 64], lhs[:, h], rhs[:, h],
                                        start=(i == 0), stop=(i == len(pairs) - 1))
            ins.then_inc(bank_full_v, 1)

        def scan_s_pe(pe):
            pe.wait_ge(loads_for_tensor, pe.due(loads_for_tensor, 64))
            state_turn_pe(pe, S0r)
            tile_matrices_pe(pe, TP, nT)
            inverse_pe(pe, nT, MS, 3)
            pe.wait_ge(vector_for_tensor, pe.due(vector_for_tensor))
            heads_pe(pe, (sV, MS["NT"]))
            per_seq_pe(pe, A64)
            pe.wait_ge(vector_for_tensor, pe.due(vector_for_tensor))
            pe.wait_ge(bank_read_v, pe.rv.freed())
            b = pe.rv.next()
            for h in range(4):
                ins = pe.eng.transpose(b[0:64, h * 64:(h + 1) * 64], sXT[:, h], ident[0:64, 0:64])
            ins.then_inc(bank_full_v, 1)
            pe.wait_ge(vector_for_tensor, pe.due(vector_for_tensor))
            heads_pe(pe, (MS["TT"], sXr))
            pe.wait_ge(vector_for_tensor, pe.due(vector_for_tensor))
            heads_pe(pe, (sSA, MS["E1"]), (sV, MS["E2"]))
            per_seq_pe(pe, R64)
            for h in range(4):
                pe.wait_ge(vector_for_tensor, pe.due(vector_for_tensor))
                pe.wait_ge(bank_read_v, pe.rv.freed())
                b = pe.rv.next()
                for i in range(2):
                    ins = pe.eng.matmul(b[0:64], MS["BK"][:, i, h * 64:(h + 1) * 64],
                                        sXP[i].rearrange("p q i -> p (q i)"), start=(i == 0), stop=(i == 1))
                ins.then_inc(bank_full_v, 1)
            pe.wait_ge(vector_for_tensor, pe.due(vector_for_tensor))
            state_turn_pe(pe, ZS)

        def scan_s_dve(v):
            e = v.eng
            state_turn_dve(v, ZS)

            def v_rows(v):
                v.wait_ge(bank_full_v, v.due(bank_full_v))
                b = v.rv.next()
                e.tensor_copy(sV, hv(b, 64, 64)).then_inc(bank_read_v, 1)
                v.wait_ge(bank_read_v, v.done(bank_read_v))
            tile_matrices_dve(v, nT, incl8, strict8, MS, v_rows)
            inverse_dve(v, nT, MS, 3)
            v.eng.sem_inc(vector_for_tensor, v.one(vector_for_tensor))

            def two_banks(dst):
                v.wait_ge(bank_full_v, v.due(bank_full_v))
                b = v.rv.next()
                e.tensor_copy(dst, hv(b, 64, 64)).then_inc(bank_read_v, 1)
                v.wait_ge(bank_read_v, v.done(bank_read_v))
                v.wait_ge(bank_full_v, v.due(bank_full_v))
                b = v.rv.next()
                e.tensor_tensor(dst, dst, hv(b, 64, 64), ALU.add).then_inc(bank_read_v, 1)
                v.wait_ge(bank_read_v, v.done(bank_read_v))
            two_banks(sXT)
            v.eng.sem_inc(vector_for_tensor, v.one(vector_for_tensor))
            v.wait_ge(bank_full_v, v.due(bank_full_v))
            b = v.rv.next()
            e.tensor_copy(sXr, hv(b, 64, 64)).then_inc(bank_read_v, 1)
            v.wait_ge(bank_read_v, v.done(bank_read_v))
            v.eng.sem_inc(vector_for_tensor, v.one(vector_for_tensor))
            v.wait_ge(bank_full_v, v.due(bank_full_v))
            b = v.rv.next()
            e.tensor_scalar(sSA, hv(b, 64, 64), -1.0, None, ALU.mult).then_inc(bank_read_v, 1)
            v.wait_ge(bank_read_v, v.done(bank_read_v))
            v.eng.sem_inc(vector_for_tensor, v.one(vector_for_tensor))
            two_banks(sY)
            v.eng.sem_inc(vector_for_sync, v.one(vector_for_sync))
            for h in range(4):
                for i, x in enumerate((sSA, sV)):
                    e.tensor_tensor(sXP[i], x[:, h].unsqueeze(1).broadcast_to([64, NB, 64]),
                                         bmask.unsqueeze(2).broadcast_to([64, NB, 64]), ALU.mult).then_inc(vector_done, 1)
                    v.wait_ge(vector_done, v.done(vector_done))
                v.eng.sem_inc(vector_for_tensor, v.one(vector_for_tensor))
                v.wait_ge(bank_full_v, v.due(bank_full_v))
                b = v.rv.next()
                e.tensor_tensor(ZS[:, h], ZS[:, h], b[0:64].rearrange("p (q i) -> p q i", q=NB), ALU.add).then_inc(bank_read_v, 1)
                v.wait_ge(bank_read_v, v.done(bank_read_v))
                e.tensor_tensor(ZS[:, h], ZS[:, h], WC[:, h, 16:24].unsqueeze(2).broadcast_to([64, NB, 64]), ALU.mult).then_inc(vector_done, 1)
                v.wait_ge(vector_done, v.done(vector_done))
            v.eng.sem_inc(vector_for_tensor, v.one(vector_for_tensor))
            state_turn_dve(v, S0r)
            v.eng.sem_inc(vector_for_sync, v.one(vector_for_sync))

        def scan_s_act(act):
            inverse_act(act, nT, MS, 3)

        GQ, GN = rB, rK

        def gn_pe(pe):
            for ring, x in ((pe.rv, YP), (pe.ra, GQ)):
                if x is GQ:
                    pe.wait_ge(vector_for_tensor, pe.due(vector_for_tensor))
                for j in range(2):
                    for c0, n in CHUNKS:
                        pe.wait_ge(ring.read, ring.freed())
                        b = ring.next()
                        pe.eng.matmul(b[:, 0:n], blk, x[:, j, c0:c0 + n], start=True, stop=True).then_inc(ring.full, 1)

        def gn_act(act):
            for j in range(2):
                for c0, n in CHUNKS:
                    act.wait_ge(bank_full_a, act.due(bank_full_a))
                    b = act.ra.next()
                    act.eng.activation(GN[:, j, c0:c0 + n], b[:, 0:n], ACT.Sqrt, bias=gneps[:, 0:1],
                                                        scale=1.0 / DH).then_inc(bank_read_a, 1)
                    act.wait_ge(bank_read_a, act.done(bank_read_a))
            act.eng.sem_inc(scalar_for_vector, act.one(scalar_for_vector))

        def gn_dve(v):
            e = v.eng
            for j in range(2):
                for c0, n in CHUNKS:
                    v.wait_ge(bank_full_v, v.due(bank_full_v))
                    b = v.rv.next()
                    y = YP[:, j, c0:c0 + n]
                    e.scalar_tensor_tensor(out=y, in0=b[:, 0:n], scalar=-1.0 / DH, in1=y,
                                                        op0=ALU.mult, op1=ALU.add).then_inc(bank_read_v, 1)
                    v.wait_ge(bank_read_v, v.done(bank_read_v))
            e.tensor_tensor(GQ, YP, YP, ALU.mult).then_inc(vector_for_tensor, 1)
            v.wait_ge(vector_for_tensor, v.done(vector_for_tensor))
            v.wait_ge(scalar_for_vector, v.due(scalar_for_vector))
            e.reciprocal(GN, GN).then_inc(vector_done, 1)
            v.wait_ge(vector_done, v.done(vector_done))
            e.tensor_tensor(YP, YP, GN, ALU.mult).then_inc(vector_done, 1)
            v.wait_ge(vector_done, v.done(vector_done))
            for j in range(2):
                e.tensor_scalar(YP[:, j], YP[:, j], col(C_GG, j), col(C_GB, j), ALU.mult, ALU.add).then_inc(vector_done, 1)
                v.wait_ge(vector_done, v.done(vector_done))
            e.tensor_tensor(YP, YP, BON, ALU.add).then_inc(vector_done, 1)
            v.wait_ge(vector_done, v.done(vector_done))
            e.tensor_tensor(YP, YP, rwG, ALU.mult).then_inc(vector_done, 1)
            v.wait_ge(vector_done, v.done(vector_done))
            v.eng.sem_inc(vector_for_sync, v.one(vector_for_sync))

        def gn_sp(sp):
            sp.wait_ge(vector_for_sync, sp.due(vector_for_sync))
            sp.eng.dma_start(mixT[0:256].rearrange("(j p) r -> p j r", p=P), YP,
                             allow_slow_non_contiguous=True).then_inc(outputs_stored, 16)
            sp.wait_ge(outputs_stored, sp.due(outputs_stored, 16))

        arena.at = base
        XC = arena.take(P, 2, 3 + TP)
        XS = arena.take(P, 2, NB, 3 + TS)
        CA = arena.take(P, 2, R)
        Q64, KM64, QS64, KW64 = (arena.take(64, 4, R) for _ in range(4))
        ml_cols = arena.take(P, 2, 7)
        gb = arena.take(4, 2)
        row_at = arena.at
        li, lf, bb, mm_, MPV, GG, NBM, tmp4 = (arena.take(4, R) for _ in range(8))
        rm4 = arena.take(4, R)
        Eb, Em, Mp, Dd, DEC4 = (arena.take(4, 24) for _ in range(5))
        DEC = arena.take(64, 4, 24)
        wqk = arena.take(64, 2, 4, 64)
        ca_at = arena.at
        CA64 = arena.take(64, 4, R)
        ml_end = arena.at
        SC4, WG4, EM4 = MPV, tmp4, rm4
        m0 = Mp[:, 16:24]

        def ml_sp(sp):
            qk = pT[PT_QK:PT_QK + 256].rearrange("(j p) r -> p j r", p=P)
            sp.eng.dma_start(XC[:, :, 3:3 + TP], qk[:, :, 0:TP],
                             allow_slow_non_contiguous=True).then_inc(loads_for_vector, 16)
            for j in range(2):
                sp.eng.dma_start(XS[:, j, :, 3:3 + TS], qk[:, j, TP:R].rearrange("p (b t) -> p b t", b=NB),
                                 allow_slow_non_contiguous=True).then_inc(loads_for_vector, 16)
                for t in range(3):
                    sp.eng.dma_start(XS[:, j, :, t], I["state_mlstm_conv"][0, :, t, j * P:(j + 1) * P].rearrange("b p -> p b"),
                                     allow_slow_non_contiguous=True).then_inc(loads_for_vector, 16)
                for t in range(4):
                    sp.eng.dma_start(ml_cols[:, j, t:t + 1], I["ml_conv_w"][0, t, j * P:(j + 1) * P].rearrange("(p o) -> p o", o=1),
                                     allow_slow_non_contiguous=True).then_inc(loads_for_vector, 16)
                for i, name in enumerate(("ml_conv_b", "ml_norm_g", "ml_skip")):
                    sp.eng.dma_start(ml_cols[:, j, 4 + i:5 + i], I[name][0, j * P:(j + 1) * P].rearrange("(p o) -> p o", o=1),
                                     allow_slow_non_contiguous=True).then_inc(loads_for_vector, 16)
            sp.eng.dma_start(li, pT[PT_IF:PT_IF + 4],
                             allow_slow_non_contiguous=True).then_inc(loads_for_vector, 16)
            sp.eng.dma_start(lf, pT[PT_IF + 4:PT_IF + 8],
                             allow_slow_non_contiguous=True).then_inc(loads_for_vector, 16)
            sp.eng.dma_start(gb, I["ml_gate_b"][0].rearrange("g h -> h g"),
                             allow_slow_non_contiguous=True).then_inc(loads_for_vector, 16)
            sp.eng.dma_start(m0, I["state_mlstm_m"][0].rearrange("b h -> h b"),
                             allow_slow_non_contiguous=True).then_inc(loads_for_vector, 16)
            sp.eng.dma_start(wqk[:, 0], I["ml_wq"][0].rearrange("h d e -> d h e"),
                             allow_slow_non_contiguous=True).then_inc(loads_for_tensor, 16)
            sp.eng.dma_start(wqk[:, 1], I["ml_wk"][0].rearrange("h d e -> d h e"),
                             allow_slow_non_contiguous=True).then_inc(loads_for_tensor, 16)
            for t in range(3):
                sp.eng.dma_start(O["conv_p"][0, 0, t].rearrange("(c o) -> c o", o=1), pT[PT_QK:PT_QK + 256, TP - 3 + t:TP - 2 + t],
                                 allow_slow_non_contiguous=True).then_inc(outputs_stored, 16)
                for b in range(NB):
                    r = TP + b * TS + TS - 3 + t
                    sp.eng.dma_start(O["conv_s"][0, b, t].rearrange("(c o) -> c o", o=1), pT[PT_QK:PT_QK + 256, r:r + 1],
                                     allow_slow_non_contiguous=True).then_inc(outputs_stored, 16)
            sp.wait_ge(scalar_for_sync, sp.due(scalar_for_sync))
            for e in range(2):
                sp.eng.dma_start(CA64[:, e:4:2], CA[64 * e:64 * e + 64],
                                 allow_slow_non_contiguous=True).then_inc(loads_for_tensor, 16)
            sp.wait_ge(outputs_stored, sp.due(outputs_stored, 16 * 27))

        IN_ML = 16 * (1 + 2 * (1 + 3 + 4 + 3) + 4)

        def ml_gp(gp):
            g = gp.eng
            g.memset(XC[:, :, 0:3], 0.0).then_inc(gpsimd_done, 1)
            gp.wait_ge(gpsimd_done, gp.done(gpsimd_done))
            g.memset(rm4, 1.0).then_inc(gpsimd_done, 1)
            gp.wait_ge(gpsimd_done, gp.done(gpsimd_done))
            g.memset(rm4[:, 0:TP:64], 0.0).then_inc(gpsimd_done, 1)
            gp.wait_ge(gpsimd_done, gp.done(gpsimd_done))
            g.memset(rm4[:, TP:R:TS], 0.0).then_inc(gpsimd_done, 1)
            gp.wait_ge(gpsimd_done, gp.done(gpsimd_done))
            gp.eng.sem_inc(gpsimd_for_vector, gp.one(gpsimd_for_vector))

        def bcr(x, n):
            return x.unsqueeze(2).broadcast_to([4, x.shape[1], n])

        def ml_dve(v):
            e = v.eng
            v.wait_ge(loads_for_vector, v.due(loads_for_vector, IN_ML))
            v.wait_ge(gpsimd_for_vector, v.due(gpsimd_for_vector))
            for j in range(2):
                CS = CA[:, j, TP:R].rearrange("p (b t) -> p b t", b=NB)
                for out, x, n in ((CA[:, j, 0:TP], XC[:, j], TP), (CS, XS[:, j], TS)):
                    def at(t):
                        return x[:, t:t + n] if n == TP else x[:, :, t:t + n]
                    e.tensor_scalar(out, at(0), ml_cols[:, j, 0:1], ml_cols[:, j, 4:5], ALU.mult, ALU.add).then_inc(vector_done, 1)
                    v.wait_ge(vector_done, v.done(vector_done))
                    for t in range(1, 4):
                        e.scalar_tensor_tensor(out=out, in0=at(t), scalar=ml_cols[:, j, t:t + 1], in1=out,
                                                    op0=ALU.mult, op1=ALU.add).then_inc(vector_done, 1)
                        v.wait_ge(vector_done, v.done(vector_done))
            e.tensor_scalar(li, li, gb[:, 0:1], None, ALU.add).then_inc(vector_done, 1)
            v.wait_ge(vector_done, v.done(vector_done))
            e.tensor_scalar(lf, lf, gb[:, 1:2], None, ALU.add).then_inc(vector_done, 1)
            v.wait_ge(vector_done, v.done(vector_done))
            e.scalar_tensor_tensor(out=tmp4, in0=lf, scalar=-1.0, in1=lf, op0=ALU.mult, op1=ALU.max).then_inc(vector_done, 1)
            v.wait_ge(vector_done, v.done(vector_done))
            v.eng.sem_inc(vector_for_scalar, v.one(vector_for_scalar))
            v.wait_ge(scalar_for_vector, v.due(scalar_for_vector))
            e.scalar_tensor_tensor(out=lf, in0=lf, scalar=0.0, in1=tmp4, op0=ALU.min, op1=ALU.subtract).then_inc(vector_done, 1)
            v.wait_ge(vector_done, v.done(vector_done))
            e.tensor_tensor_scan(mm_[:, 0:TP], lf[:, 0:TP], li[:, 0:TP], 0.0, ALU.add, ALU.max).then_inc(vector_done, 1)
            v.wait_ge(vector_done, v.done(vector_done))
            for b in range(NB):
                c = slice(TP + b * TS, TP + (b + 1) * TS)
                e.tensor_tensor_scan(mm_[:, c], lf[:, c], li[:, c], m0[:, b:b + 1], ALU.add, ALU.max).then_inc(vector_done, 1)
                v.wait_ge(vector_done, v.done(vector_done))
            e.tensor_tensor_scan(bb, rm4, lf, 0.0, ALU.mult, ALU.add).then_inc(vector_done, 1)
            v.wait_ge(vector_done, v.done(vector_done))
            e.memset(Mp[:, 0:1], 0.0).then_inc(vector_done, 1)
            v.wait_ge(vector_done, v.done(vector_done))
            e.tensor_copy(Mp[:, 1:16], mm_[:, 63:TP - 64:64]).then_inc(vector_done, 1)
            v.wait_ge(vector_done, v.done(vector_done))
            for x, y in ((Eb, bb), (Em, mm_)):
                e.tensor_copy(x[:, 0:16], y[:, 63:TP:64]).then_inc(vector_done, 1)
                v.wait_ge(vector_done, v.done(vector_done))
                e.tensor_copy(x[:, 16:24], y[:, TP + TS - 1:R:TS]).then_inc(vector_done, 1)
                v.wait_ge(vector_done, v.done(vector_done))
            e.tensor_tensor(Dd, Eb, Em, ALU.subtract).then_inc(vector_done, 1)
            v.wait_ge(vector_done, v.done(vector_done))
            e.tensor_tensor(DEC4, Dd, Mp, ALU.add).then_inc(vector_done, 1)
            v.wait_ge(vector_done, v.done(vector_done))
            e.tensor_tensor(GG, li, bb, ALU.subtract).then_inc(vector_done, 1)
            v.wait_ge(vector_done, v.done(vector_done))
            e.tensor_tensor(NBM, bb, mm_, ALU.subtract).then_inc(vector_done, 1)
            v.wait_ge(vector_done, v.done(vector_done))
            for c, n, k0, k1 in ((slice(0, TP), 64, 0, 16), (slice(TP, R), TS, 16, 24)):
                def ch(x):
                    return x[:, c].rearrange("p (k t) -> p k t", t=n)
                e.tensor_tensor(ch(SC4), ch(NBM), bcr(Mp[:, k0:k1], n), ALU.add).then_inc(vector_done, 1)
                v.wait_ge(vector_done, v.done(vector_done))
                e.tensor_tensor(ch(WG4), ch(GG), bcr(Dd[:, k0:k1], n), ALU.add).then_inc(vector_done, 1)
                v.wait_ge(vector_done, v.done(vector_done))
            v.eng.sem_inc(vector_for_scalar, v.one(vector_for_scalar))
            for dst, src in ((QS64, Q64), (KW64, KM64)):
                v.wait_ge(scalar_for_vector, v.due(scalar_for_vector))
                for h in range(4):
                    for c0, n in CHUNKS:
                        v.wait_ge(bank_full_v, v.due(bank_full_v))
                        b = v.rv.next()
                        e.tensor_tensor(dst[:, h, c0:c0 + n], b[0:64, 0:n], src[:, h, c0:c0 + n], ALU.mult).then_inc(bank_read_v, 1)
                        v.wait_ge(bank_read_v, v.done(bank_read_v))
            v.wait_ge(bank_full_v, v.due(bank_full_v))
            b = v.rv.next()
            e.tensor_copy(DEC, b[0:64, 0:96].rearrange("p (h k) -> p h k", h=4)).then_inc(bank_read_v, 1)
            v.wait_ge(bank_read_v, v.done(bank_read_v))

        def ml_act(act):
            a = act.eng
            act.wait_ge(vector_for_scalar, act.due(vector_for_scalar))
            a.activation(CA, CA, ACT.Silu).then_inc(scalar_done, 1)
            act.wait_ge(scalar_done, act.done(scalar_done))
            act.eng.sem_inc(scalar_for_sync, act.one(scalar_for_sync))
            a.activation(tmp4, tmp4, ACT.Exp, scale=-1.0).then_inc(scalar_done, 1)
            act.wait_ge(scalar_done, act.done(scalar_done))
            a.activation(tmp4, tmp4, ACT.Ln, bias=ones[0:4, 0:1]).then_inc(scalar_done, 1)
            act.wait_ge(scalar_done, act.done(scalar_done))
            act.eng.sem_inc(scalar_for_vector, act.one(scalar_for_vector))
            act.wait_ge(vector_for_scalar, act.due(vector_for_scalar))
            for x in (SC4, WG4, DEC4):
                a.activation(x, x, ACT.Exp).then_inc(scalar_done, 1)
                act.wait_ge(scalar_done, act.done(scalar_done))
            a.activation(EM4, mm_, ACT.Exp, scale=-1.0).then_inc(scalar_done, 1)
            act.wait_ge(scalar_done, act.done(scalar_done))
            act.eng.sem_inc(scalar_for_tensor, act.one(scalar_for_tensor))
            for dst, s in ((Q64, 1.0), (KM64, SCALE)):
                for h in range(4):
                    for c0, n in CHUNKS:
                        act.wait_ge(bank_full_a, act.due(bank_full_a))
                        b = act.ra.next()
                        a.mul(dst[:, h, c0:c0 + n], b[0:64, 0:n], s).then_inc(bank_read_a, 1)
                        act.wait_ge(bank_read_a, act.done(bank_read_a))
                act.eng.sem_inc(scalar_for_vector, act.one(scalar_for_vector))

        def ml_pe(pe):
            mm = pe.eng.matmul
            pe.wait_ge(loads_for_tensor, pe.due(loads_for_tensor, 64))
            for i in range(2):
                for h in range(4):
                    for c0, n in CHUNKS:
                        pe.wait_ge(bank_read_a, pe.ra.freed())
                        b = pe.ra.next()
                        mm(b[0:64, 0:n], wqk[:, i, h], CA64[:, h, c0:c0 + n], start=True, stop=True).then_inc(bank_full_a, 1)
            pe.wait_ge(scalar_for_tensor, pe.due(scalar_for_tensor))
            for x in (SC4, WG4):
                for h in range(4):
                    for c0, n in CHUNKS:
                        pe.wait_ge(bank_read_v, pe.rv.freed())
                        b = pe.rv.next()
                        mm(b[0:64, 0:n], sel4[:, h, 0:64], x[:, c0:c0 + n], start=True, stop=True).then_inc(bank_full_v, 1)
            pe.wait_ge(bank_read_v, pe.rv.freed())
            b = pe.rv.next()
            for h in range(4):
                ins = mm(b[0:64, h * 24:(h + 1) * 24], sel4[:, h, 0:64], DEC4, start=True, stop=True)
            ins.then_inc(bank_full_v, 1)

        VR = arena.array[:, base:base + 8 * 256].rearrange("p (i c) -> p i c", i=8)
        VRs = arena.array[0:64, row_at:row_at + 256]
        mw = Arena(arena.array[:, ca_at:size], size - ca_at)
        HP = arena.array[:, ml_end:ml_end + 2 * R].rearrange("p (j r) -> p j r", j=2)
        MV = mw.take(P, 2, 4, P)
        MD, MA = mw.take(P, 4, P), mw.take(P, 4, P)
        KWr = mw.take(P, 256)
        EMs, Ht = mw.take(64, 4, P), mw.take(64, 4, P)
        ND = mw.take(64, 4, 2, 64)
        ZM = mw.take(64, 4, P)
        assert mw.at <= 4 * R and ml_end + 2 * R <= size, (mw.at, ml_end)
        mZo = QS64[:, 0, 0:256].rearrange("p (h c) -> p h c", h=4)

        def ml_a_pe(pe, t0, n):
            mm = pe.eng.matmul
            pe.wait_ge(bank_read_v, pe.rv.freed())
            b = pe.rv.next()
            for h in range(4):
                ins = pe.eng.transpose(b[0:n, h * 64:(h + 1) * 64], KW64[:, h, t0:t0 + n], ident[0:64, 0:64])
            ins.then_inc(bank_full_v, 1)
            pe.wait_ge(bank_read_v, pe.rv.freed())
            b = pe.rv.next()
            for h in range(4):
                o = b[0:n, h * n:(h + 1) * n]
                mm(o, GG[:, t0:t0 + n], sel4[:, h, 0:n], start=True, stop=False)
                ins = mm(o, sel4[:, h, 0:n], NBM[:, t0:t0 + n], start=False, stop=True)
            ins.then_inc(bank_full_v, 1)
            pe.wait_ge(bank_read_v, pe.rv.freed())
            b = pe.rv.next()
            for h in range(4):
                ins = mm(b[0:n, h * n:(h + 1) * n], KM64[:, h, t0:t0 + n], Q64[:, h, t0:t0 + n], start=True, stop=True)
            ins.then_inc(bank_full_v, 1)
            pe.wait_ge(bank_read_v, pe.rv.freed())
            b = pe.rv.next()
            for h in range(4):
                ins = mm(b[0:64, h * n:(h + 1) * n], sel4[:, h, 0:64], EM4[:, t0:t0 + n], start=True, stop=True)
            ins.then_inc(bank_full_v, 1)

        def ml_a_dve(v, n, neg, kwr, d, a, ems):
            e = v.eng
            v.wait_ge(bank_full_v, v.due(bank_full_v))
            b = v.rv.next()
            e.tensor_copy(kwr, b[0:n, 0:256]).then_inc(bank_read_v, 1)
            v.wait_ge(bank_read_v, v.done(bank_read_v))
            v.wait_ge(bank_full_v, v.due(bank_full_v))
            b = v.rv.next()
            e.tensor_tensor(d, hv(b, n, n), bc4(neg, n), ALU.add).then_inc(bank_read_v, 1)
            v.wait_ge(bank_read_v, v.done(bank_read_v))
            v.eng.sem_inc(vector_for_scalar, v.one(vector_for_scalar))
            v.wait_ge(scalar_for_vector, v.due(scalar_for_vector))
            v.wait_ge(bank_full_v, v.due(bank_full_v))
            b = v.rv.next()
            e.tensor_tensor(a, hv(b, n, n), d, ALU.mult).then_inc(bank_read_v, 1)
            v.wait_ge(bank_read_v, v.done(bank_read_v))
            v.wait_ge(bank_full_v, v.due(bank_full_v))
            b = v.rv.next()
            e.tensor_copy(ems, hv(b, n, 64)).then_inc(bank_read_v, 1)
            v.wait_ge(bank_read_v, v.done(bank_read_v))

        def ml_exp_act(act, d):
            act.wait_ge(vector_for_scalar, act.due(vector_for_scalar))
            act.eng.activation(d, d, ACT.Exp).then_inc(scalar_done, 1)
            act.wait_ge(scalar_done, act.done(scalar_done))
            act.eng.sem_inc(scalar_for_vector, act.one(scalar_for_vector))

        def mlc_sp(sp):
            sp.eng.dma_start(VR, pR[0:TP, PR_V:PR_V + 256].rearrange("(i p) c -> p i c", p=P),
                             allow_slow_non_contiguous=True).then_inc(loads_for_vector, 16)
            sp.eng.dma_start(VRs, pR[TP:R, PR_V:PR_V + 256],
                             allow_slow_non_contiguous=True).then_inc(loads_for_vector, 16)
            sp.eng.dma_start(O["m_p"][0, 0].rearrange("(h o) -> h o", o=1), mm_[:, TP - 1:TP],
                             allow_slow_non_contiguous=True).then_inc(outputs_stored, 16)
            sp.eng.dma_start(O["m_s"][0].rearrange("b h -> h b"), Em[:, 16:24],
                             allow_slow_non_contiguous=True).then_inc(outputs_stored, 16)
            for i in range(8):
                sp.wait_ge(vector_for_sync, sp.due(vector_for_sync))
                for e in range(2):
                    sp.eng.dma_start(HP[64 * e:64 * e + 64, :, i * P:(i + 1) * P], Ht[:, e:4:2],
                                     allow_slow_non_contiguous=True).then_inc(heads_moved, 16)
                sp.wait_ge(heads_moved, sp.due(heads_moved, 32))
                sp.eng.sem_inc(sync_for_vector, sp.one(sync_for_vector))
            sp.wait_ge(vector_for_sync, sp.due(vector_for_sync))
            sp.eng.dma_start(O["C_p"][0, 0].rearrange("h i j -> i h j"), mZo,
                             allow_slow_non_contiguous=True).then_inc(outputs_stored, 16)
            for h in range(4):
                sp.eng.dma_start(O["n_p"][0, 0, h].rearrange("(j o) -> j o", o=1), ZM[:, h, 64:65],
                                 allow_slow_non_contiguous=True).then_inc(outputs_stored, 16)
            sp.wait_ge(outputs_stored, sp.due(outputs_stored, 16 * 7))

        def mlc_act(act):
            for i in range(8):
                ml_exp_act(act, MD)

        def mlc_pe(pe):
            mm = pe.eng.matmul
            for i in range(8):
                t0 = i * P
                ml_a_pe(pe, t0, P)
                pe.wait_ge(vector_for_tensor, pe.due(vector_for_tensor))
                for c in range(2):
                    tc = slice(t0 + 64 * c, t0 + 64 * c + 64)
                    pe.wait_ge(bank_read_v, pe.rv.freed())
                    b = pe.rv.next()
                    for h in range(4):
                        for s in range(2):
                            o, w = b[0:64, (2 * h + s) * 64:(2 * h + s + 1) * 64], slice(64 * s, 64 * s + 64)
                            mm(o, ZM[:, h, w], QS64[:, h, tc], start=True, stop=False)
                            ins = mm(o, MV[:, c, h, w], MA[:, h, 64 * c:64 * c + 64], start=False, stop=True)
                    ins.then_inc(bank_full_v, 1)
                    pe.wait_ge(bank_read_v, pe.rv.freed())
                    b = pe.rv.next()
                    for h in range(4):
                        ins = mm(b[0:64, h * P:(h + 1) * P], KWr[:, h * 64:(h + 1) * 64], MV[:, c, h], start=True, stop=True)
                    ins.then_inc(bank_full_v, 1)
                    pe.wait_ge(vector_for_tensor, pe.due(vector_for_tensor))
            pe.wait_ge(bank_read_v, pe.rv.freed())
            b = pe.rv.next()
            for h in range(4):
                ins = pe.eng.transpose(b[0:64, h * 64:(h + 1) * 64], ZM[:, h, 0:64], ident[0:64, 0:64])
            ins.then_inc(bank_full_v, 1)

        def quotient(v, num, den, ems, out):
            e = v.eng
            e.scalar_tensor_tensor(out=den, in0=den, scalar=-1.0, in1=den, op0=ALU.mult, op1=ALU.max).then_inc(vector_done, 1)
            v.wait_ge(vector_done, v.done(vector_done))
            e.tensor_tensor(den, den, ems, ALU.max).then_inc(vector_done, 1)
            v.wait_ge(vector_done, v.done(vector_done))
            e.reciprocal(den, den).then_inc(vector_done, 1)
            v.wait_ge(vector_done, v.done(vector_done))
            e.tensor_tensor(out, num, den, ALU.mult).then_inc(vector_done, 1)
            v.wait_ge(vector_done, v.done(vector_done))

        def mlc_dve(v):
            e = v.eng
            v.wait_ge(loads_for_vector, v.due(loads_for_vector, 32))
            e.memset(MV, 0.0).then_inc(vector_done, 1)
            v.wait_ge(vector_done, v.done(vector_done))
            e.memset(MV[0:64, 0, :, 64:P], 1.0).then_inc(vector_done, 1)
            v.wait_ge(vector_done, v.done(vector_done))
            e.memset(MV[64:P, 1, :, 64:P], 1.0).then_inc(vector_done, 1)
            v.wait_ge(vector_done, v.done(vector_done))
            e.memset(ZM, 0.0).then_inc(vector_done, 1)
            v.wait_ge(vector_done, v.done(vector_done))
            for i in range(8):
                for c in range(2):
                    r = slice(64 * c, 64 * c + 64)
                    e.tensor_copy(MV[r, c, :, 0:64], VR[r, i].rearrange("p (h d) -> p h d", h=4)).then_inc(vector_done, 1)
                    v.wait_ge(vector_done, v.done(vector_done))
                ml_a_dve(v, P, neg64, KWr, MD, MA, EMs)
                v.eng.sem_inc(vector_for_tensor, v.one(vector_for_tensor))
                for c in range(2):
                    cs = slice(64 * c, 64 * c + 64)
                    v.wait_ge(bank_full_v, v.due(bank_full_v))
                    b = v.rv.next()
                    e.tensor_copy(ND, b[0:64].rearrange("p (h s t) -> p h s t", h=4, s=2)).then_inc(bank_read_v, 1)
                    v.wait_ge(bank_read_v, v.done(bank_read_v))
                    if i and not c:
                        v.wait_ge(sync_for_vector, v.due(sync_for_vector))
                    quotient(v, ND[:, :, 0], ND[:, :, 1], EMs[:, :, cs], Ht[:, :, cs])
                    v.wait_ge(bank_full_v, v.due(bank_full_v))
                    b = v.rv.next()
                    w = DEC[:, :, 2 * i + c:2 * i + c + 1].broadcast_to([64, 4, P])
                    e.tensor_tensor(ZM, ZM, w, ALU.mult).then_inc(vector_done, 1)
                    v.wait_ge(vector_done, v.done(vector_done))
                    e.tensor_tensor(ZM, ZM, hv(b, P, 64), ALU.add).then_inc(bank_read_v, 1)
                    v.wait_ge(bank_read_v, v.done(bank_read_v))
                    v.eng.sem_inc(vector_for_tensor, v.one(vector_for_tensor))
                v.eng.sem_inc(vector_for_sync, v.one(vector_for_sync))
            v.wait_ge(sync_for_vector, v.due(sync_for_vector))
            v.wait_ge(bank_full_v, v.due(bank_full_v))
            b = v.rv.next()
            e.tensor_copy(mZo, hv(b, 64, 64)).then_inc(bank_read_v, 1)
            v.wait_ge(bank_read_v, v.done(bank_read_v))
            v.eng.sem_inc(vector_for_sync, v.one(vector_for_sync))

        mw = Arena(arena.array[:, ca_at:size], ml_end - ca_at)
        tD, tA, tE, tN, tDn, tH = (mw.take(64, 4, 64) for _ in range(6))
        tKr = mw.take(64, 256)
        tVx = mw.take(64, NB, 64)
        nS = mw.take(64, 4, NB)
        zS = [Q64[:, h, 0:NB * 64].rearrange("p (q i) -> p q i", q=NB) for h in range(4)]
        c0r = [KM64[:, h, 0:NB * 64].rearrange("p (q i) -> p q i", q=NB) for h in range(4)]
        nBc = [KW64[:, h, 0:NB * 64].rearrange("p (q i) -> p q i", q=NB) for h in range(4)]
        h64 = lambda x: [x[:, h] for h in range(4)]

        def mls_sp(sp):
            for h in range(4):
                sp.eng.dma_start(c0r[h], I["state_mlstm_C"][0, :, h].rearrange("b i j -> i b j"),
                                 allow_slow_non_contiguous=True).then_inc(loads_for_tensor, 16)
                sp.eng.dma_start(nS[:, h], I["state_mlstm_n"][0, :, h].rearrange("b j -> j b"),
                                 allow_slow_non_contiguous=True).then_inc(loads_for_vector, 16)
            sp.wait_ge(vector_for_sync, sp.due(vector_for_sync))
            for e in range(2):
                sp.eng.dma_start(HP[64 * e:64 * e + 64, :, TP:R], tH[:, e:4:2],
                                 allow_slow_non_contiguous=True).then_inc(heads_moved, 16)
            sp.wait_ge(vector_for_sync, sp.due(vector_for_sync))
            for h in range(4):
                sp.eng.dma_start(O["C_s"][0, :, h].rearrange("b i j -> i b j"), c0r[h],
                                 allow_slow_non_contiguous=True).then_inc(outputs_stored, 16)
                sp.eng.dma_start(O["n_s"][0, :, h].rearrange("b j -> j b"), nS[:, h],
                                 allow_slow_non_contiguous=True).then_inc(outputs_stored, 16)
            sp.wait_ge(heads_moved, sp.due(heads_moved, 32))
            sp.wait_ge(outputs_stored, sp.due(outputs_stored, 128))

        def turn8_pe(pe, src):
            for h in range(4):
                pe.wait_ge(bank_read_v, pe.rv.freed())
                b = pe.rv.next()
                for q in range(NB):
                    ins = pe.eng.transpose(b[0:64, q * 64:(q + 1) * 64], src[h][:, q], ident[0:64, 0:64])
                ins.then_inc(bank_full_v, 1)

        def turn8_dve(v, dst):
            for h in range(4):
                v.wait_ge(bank_full_v, v.due(bank_full_v))
                b = v.rv.next()
                v.eng.tensor_copy(dst[h], b[0:64].rearrange("p (q i) -> p q i", q=NB)).then_inc(bank_read_v, 1)
                v.wait_ge(bank_read_v, v.done(bank_read_v))

        def mls_pe(pe):
            mm = pe.eng.matmul
            pe.wait_ge(loads_for_tensor, pe.due(loads_for_tensor, 64))
            turn8_pe(pe, c0r)
            ml_a_pe(pe, TP, nT)
            pe.wait_ge(vector_for_tensor, pe.due(vector_for_tensor))
            for lhs, st in (([VRs[:, h * 64:(h + 1) * 64] for h in range(4)], zS), ([ones[0:64, 0:64]] * 4, nBc)):
                pe.wait_ge(bank_read_v, pe.rv.freed())
                b = pe.rv.next()
                for h in range(4):
                    ins = mm(b[0:64, h * 64:(h + 1) * 64], lhs[h], tA[:, h], start=True, stop=True)
                ins.then_inc(bank_full_v, 1)
                pe.wait_ge(bank_read_v, pe.rv.freed())
                b = pe.rv.next()
                for h in range(4):
                    for q in range(NB):
                        ins = mm(b[0:64, h * 64 + q * TS:h * 64 + (q + 1) * TS], st[h][:, q],
                                 QS64[:, h, TP + q * TS:TP + (q + 1) * TS], start=True, stop=True)
                ins.then_inc(bank_full_v, 1)
            pe.wait_ge(bank_read_v, pe.rv.freed())
            b = pe.rv.next()
            for h in range(4):
                ins = mm(b[0:64, h * NB:(h + 1) * NB], tKr[:, h * 64:(h + 1) * 64], bmask, start=True, stop=True)
            ins.then_inc(bank_full_v, 1)
            for h in range(4):
                pe.wait_ge(vector_for_tensor, pe.due(vector_for_tensor))
                pe.wait_ge(bank_read_v, pe.rv.freed())
                b = pe.rv.next()
                mm(b[0:64], tKr[:, h * 64:(h + 1) * 64], tVx.rearrange("p q i -> p (q i)"),
                                   start=True, stop=True).then_inc(bank_full_v, 1)
            pe.wait_ge(vector_for_tensor, pe.due(vector_for_tensor))
            turn8_pe(pe, zS)

        def mls_dve(v):
            e = v.eng
            turn8_dve(v, zS)
            ml_a_dve(v, nT, neg8, tKr, tD, tA, tE)
            v.wait_ge(loads_for_vector, v.due(loads_for_vector, 64))
            for h in range(4):
                e.tensor_copy(nBc[h], nS[:, h].unsqueeze(2).broadcast_to([64, NB, 64])).then_inc(vector_done, 1)
                v.wait_ge(vector_done, v.done(vector_done))
            v.eng.sem_inc(vector_for_tensor, v.one(vector_for_tensor))
            for dst in (tN, tDn):
                v.wait_ge(bank_full_v, v.due(bank_full_v))
                b = v.rv.next()
                e.tensor_copy(dst, hv(b, 64, 64)).then_inc(bank_read_v, 1)
                v.wait_ge(bank_read_v, v.done(bank_read_v))
                v.wait_ge(bank_full_v, v.due(bank_full_v))
                b = v.rv.next()
                e.tensor_tensor(dst, dst, hv(b, 64, 64), ALU.add).then_inc(bank_read_v, 1)
                v.wait_ge(bank_read_v, v.done(bank_read_v))
            quotient(v, tN, tDn, tE, tH)
            v.eng.sem_inc(vector_for_sync, v.one(vector_for_sync))
            v.wait_ge(bank_full_v, v.due(bank_full_v))
            b = v.rv.next()
            e.tensor_tensor(nS, nS, DEC[:, :, 16:24], ALU.mult).then_inc(vector_done, 1)
            v.wait_ge(vector_done, v.done(vector_done))
            e.tensor_tensor(nS, nS, b[0:64, 0:4 * NB].rearrange("p (h q) -> p h q", h=4), ALU.add).then_inc(bank_read_v, 1)
            v.wait_ge(bank_read_v, v.done(bank_read_v))
            for h in range(4):
                e.tensor_tensor(tVx, VRs[:, h * 64:(h + 1) * 64].unsqueeze(1).broadcast_to([64, NB, 64]),
                                     bmask.unsqueeze(2).broadcast_to([64, NB, 64]), ALU.mult).then_inc(vector_for_tensor, 1)
                v.wait_ge(vector_for_tensor, v.done(vector_for_tensor))
                v.wait_ge(bank_full_v, v.due(bank_full_v))
                b = v.rv.next()
                e.tensor_tensor(zS[h], zS[h], DEC[:, h, 16:24].unsqueeze(2).broadcast_to([64, NB, 64]), ALU.mult).then_inc(vector_done, 1)
                v.wait_ge(vector_done, v.done(vector_done))
                e.tensor_tensor(zS[h], zS[h], b[0:64].rearrange("p (q i) -> p q i", q=NB), ALU.add).then_inc(bank_read_v, 1)
                v.wait_ge(bank_read_v, v.done(bank_read_v))
            v.eng.sem_inc(vector_for_tensor, v.one(vector_for_tensor))
            turn8_dve(v, c0r)
            v.eng.sem_inc(vector_for_sync, v.one(vector_for_sync))

        def mls_act(act):
            ml_exp_act(act, tD)

        OG = arena.array[:, ca_at:ca_at + 2 * R].rearrange("p (j r) -> p j r", j=2)
        MQ = arena.array[:, ca_at + 2 * R:ca_at + 4 * R].rearrange("p (j r) -> p j r", j=2)

        def mlo_sp(sp):
            sp.eng.dma_start(OG, pT[PT_O:PT_O + 256].rearrange("(j p) r -> p j r", p=P),
                             allow_slow_non_contiguous=True).then_inc(loads_for_scalar, 16)
            sp.wait_ge(vector_for_sync, sp.due(vector_for_sync))
            sp.eng.dma_start(mixT[256:512].rearrange("(j p) r -> p j r", p=P), HP,
                             allow_slow_non_contiguous=True).then_inc(outputs_stored, 16)
            sp.wait_ge(outputs_stored, sp.due(outputs_stored, 16))

        def head_sums_pe(pe, x):
            pe.wait_ge(vector_for_tensor, pe.due(vector_for_tensor))
            for j in range(2):
                for c0, n in CHUNKS:
                    pe.wait_ge(bank_read_a, pe.ra.freed())
                    b = pe.ra.next()
                    pe.eng.matmul(b[:, 0:n], blk, x[:, j, c0:c0 + n], start=True, stop=True).then_inc(bank_full_a, 1)

        def head_roots_act(act, out):
            for j in range(2):
                for c0, n in CHUNKS:
                    act.wait_ge(bank_full_a, act.due(bank_full_a))
                    b = act.ra.next()
                    act.eng.activation(out[:, j, c0:c0 + n], b[:, 0:n], ACT.Sqrt, bias=eps[:, 0:1],
                                                        scale=1.0 / DH).then_inc(bank_read_a, 1)
                    act.wait_ge(bank_read_a, act.done(bank_read_a))
            act.eng.sem_inc(scalar_for_vector, act.one(scalar_for_vector))

        MN = arena.array[:, base + 2 * (TP + 3) + 2 * NB * (TS + 3) + 2 * R:][:, 0:2 * R].rearrange("p (j r) -> p j r", j=2)

        def mlo_pe(pe):
            head_sums_pe(pe, MQ)

        def mlo_act(act):
            act.wait_ge(loads_for_scalar, act.due(loads_for_scalar, 16))
            act.eng.activation(OG, OG, ACT.Sigmoid).then_inc(scalar_done, 1)
            act.wait_ge(scalar_done, act.done(scalar_done))
            head_roots_act(act, MN)

        def mlo_dve(v):
            e = v.eng
            e.tensor_tensor(MQ, HP, HP, ALU.mult).then_inc(vector_for_tensor, 1)
            v.wait_ge(vector_for_tensor, v.done(vector_for_tensor))
            v.wait_ge(scalar_for_vector, v.due(scalar_for_vector))
            e.reciprocal(MN, MN).then_inc(vector_done, 1)
            v.wait_ge(vector_done, v.done(vector_done))
            e.tensor_tensor(HP, HP, MN, ALU.mult).then_inc(vector_done, 1)
            v.wait_ge(vector_done, v.done(vector_done))
            for j in range(2):
                e.tensor_scalar(HP[:, j], HP[:, j], ml_cols[:, j, 5:6], None, ALU.mult).then_inc(vector_done, 1)
                v.wait_ge(vector_done, v.done(vector_done))
                e.scalar_tensor_tensor(out=HP[:, j], in0=CA[:, j], scalar=ml_cols[:, j, 6:7], in1=HP[:, j],
                                            op0=ALU.mult, op1=ALU.add).then_inc(vector_done, 1)
                v.wait_ge(vector_done, v.done(vector_done))
            e.tensor_tensor(HP, HP, OG, ALU.mult).then_inc(vector_done, 1)
            v.wait_ge(vector_done, v.done(vector_done))
            v.eng.sem_inc(vector_for_sync, v.one(vector_for_sync))

        BIG = 1e9
        arena.at = base
        NQ = arena.take(64, 8, R)
        NR = arena.take(P, 9, 792)
        NG = NR[:, :, 768:792]
        nsa_g = arena.take(64, 4)
        ngr = arena.take(P, 2, DH)
        ngb = arena.take(P, 24)
        GB_ = arena.take(64, 3)
        GS = arena.take(64, NB, 3)
        wc = arena.take(64, 2, 2, DH)
        ns_keep = arena.at
        KST = arena.take(64, 2, TP)
        KWT = arena.take(64, 2, TP)
        OUT = arena.take(P, 8, 512)
        ns_mid = arena.at
        nsq = arena.take(P, 9, 2, 2, DH)
        nsr = arena.take(P, 36)
        qsq = arena.take(64, 2, R)
        qrt = arena.take(64, 2, R)

        def kview(x):
            return x[:, :, 256:768].rearrange("p i (b k g d) -> p i b k g d", b=2, k=2, g=2)[:, :, :, 0]

        def nr_sp(sp):
            sp.wait_ge(gpsimd_for_sync, sp.due(gpsimd_for_sync))
            sp.eng.dma_start(NR[:, 0:8], pR[0:TP, 256:1048].rearrange("(i p) c -> p i c", p=P),
                             allow_slow_non_contiguous=True).then_inc(loads_for_vector, 16)
            sp.eng.dma_start(NR[0:64, 8], pR[TP:R, 256:1048],
                             allow_slow_non_contiguous=True).then_inc(loads_for_vector, 16)
            for i, r in enumerate((2, 3)):
                sp.eng.dma_start(ngr[:, i], I["nsa_qk_g"][0, r:r + 1].broadcast_to([P, DH]),
                                 allow_slow_non_contiguous=True).then_inc(loads_for_vector, 16)
            sp.eng.dma_start(ngb, I["nsa_gate_b"].broadcast_to([P, 24]),
                             allow_slow_non_contiguous=True).then_inc(loads_for_vector, 16)
            sp.eng.dma_start(NQ, pT[PT_Q:PT_Q + 512].rearrange("(h d) r -> d h r", d=DH),
                             allow_slow_non_contiguous=True).then_inc(loads_for_vector, 16)
            sp.eng.dma_start(nsa_g, I["nsa_qk_g"][0].rearrange("i d -> d i"),
                             allow_slow_non_contiguous=True).then_inc(loads_for_vector, 16)
            for h in range(8):
                sp.eng.dma_start(GS[8 * h:8 * h + 8], pR[TP:R, PR_G + 3 * h:PR_G + 3 * h + 3].rearrange("(b t) c -> t b c", b=NB),
                                 allow_slow_non_contiguous=True).then_inc(loads_for_vector, 16)
                sp.eng.dma_start(GB_[8 * h:8 * h + 8], I["nsa_gate_b"][:, 3 * h:3 * h + 3].broadcast_to([8, 3]),
                                 allow_slow_non_contiguous=True).then_inc(loads_for_vector, 16)
            sp.eng.dma_start(wc, I["nsa_wc"][0].rearrange("c g d e -> d c g e"),
                             allow_slow_non_contiguous=True).then_inc(loads_for_tensor, 16)
            sp.wait_ge(vector_for_sync, sp.due(vector_for_sync))
            rows = lambda o: o.rearrange("t c g d -> t (c g d)")
            for name, c in (("cmp", 0), ("sel", 256)):
                sp.eng.dma_start(rows(O[name + "_p"][0, 0]).rearrange("(i p) c -> p i c", p=P), NR[:, 0:8, c:c + 256],
                                 allow_slow_non_contiguous=True).then_inc(outputs_stored, 16)
                sp.eng.dma_start(O[name + "_s"][0].rearrange("b t c g d -> (b t) (c g d)"), NR[0:64, 8, c:c + 256],
                                 allow_slow_non_contiguous=True).then_inc(outputs_stored, 16)
            sp.eng.dma_start(rows(O["win_p"][0, 0]).rearrange("(i p) c -> p i c", p=P), NR[:, 4:8, 512:768],
                             allow_slow_non_contiguous=True).then_inc(outputs_stored, 16)
            for b in range(NB):
                sp.eng.dma_start(rows(O["win_s"][0, b, WIN - TS:WIN]), NR[b * TS:(b + 1) * TS, 8, 512:768],
                                 allow_slow_non_contiguous=True).then_inc(outputs_stored, 16)
                sp.eng.dma_start(rows(O["win_s"][0, b, 0:WIN - TS]), rows(I["cache_nsa_win"][0, b, TS:WIN]),
                                 allow_slow_non_contiguous=True).then_inc(outputs_stored, 16)
            sp.wait_ge(outputs_stored, sp.due(outputs_stored, 16 * 21))

        def nr_gp(gp):
            gp.eng.memset(NR[64:128, 8], 0.0).then_inc(gpsimd_done, 1)
            gp.wait_ge(gpsimd_done, gp.done(gpsimd_done))
            gp.eng.sem_inc(gpsimd_for_sync, gp.one(gpsimd_for_sync))
            gp.eng.sem_inc(gpsimd_for_vector, gp.one(gpsimd_for_vector))

        def nr_dve(v):
            e = v.eng
            v.wait_ge(loads_for_vector, v.due(loads_for_vector, 16 * 23))
            v.wait_ge(gpsimd_for_vector, v.due(gpsimd_for_vector))
            for i in range(9):
                kv = kview(NR)[:, i]
                e.tensor_tensor(nsq[:, i], kv, kv, ALU.mult).then_inc(vector_done, 1)
                v.wait_ge(vector_done, v.done(vector_done))
            e.tensor_reduce(nsr, nsq.rearrange("p i b g d -> p (i b g) d"), AX.X, ALU.add).then_inc(vector_done, 1)
            v.wait_ge(vector_done, v.done(vector_done))
            e.tensor_tensor(NG, NG, ngb.unsqueeze(1).broadcast_to([P, 9, 24]), ALU.add).then_inc(vector_done, 1)
            v.wait_ge(vector_done, v.done(vector_done))
            e.tensor_tensor(GS, GS, GB_.unsqueeze(1).broadcast_to([64, NB, 3]), ALU.add).then_inc(vector_done, 1)
            v.wait_ge(vector_done, v.done(vector_done))
            v.eng.sem_inc(vector_for_scalar, v.one(vector_for_scalar))
            v.wait_ge(scalar_for_vector, v.due(scalar_for_vector))
            e.reciprocal(nsr, nsr).then_inc(vector_done, 1)
            v.wait_ge(vector_done, v.done(vector_done))
            rr = nsr.rearrange("p (i b g) -> p i b g", b=2, g=2)
            for i in range(9):
                kv = kview(NR)[:, i]
                for b in range(2):
                    e.tensor_tensor(kv[:, b], kv[:, b], rr[:, i, b].unsqueeze(2).broadcast_to([P, 2, DH]), ALU.mult).then_inc(vector_done, 1)
                    v.wait_ge(vector_done, v.done(vector_done))
                    e.tensor_tensor(kv[:, b], kv[:, b], ngr[:, b].unsqueeze(1).broadcast_to([P, 2, DH]), ALU.mult).then_inc(vector_done, 1)
                    v.wait_ge(vector_done, v.done(vector_done))
            v.eng.sem_inc(vector_for_sync, v.one(vector_for_sync))
            for h in range(0, 8, 2):
                q = NQ[:, h:h + 2]
                e.tensor_tensor(qsq, q, q, ALU.mult).then_inc(vector_for_tensor, 1)
                v.wait_ge(vector_for_tensor, v.done(vector_for_tensor))
                v.wait_ge(scalar_for_vector, v.due(scalar_for_vector))
                e.reciprocal(qrt, qrt).then_inc(vector_done, 1)
                v.wait_ge(vector_done, v.done(vector_done))
                e.tensor_tensor(q, q, qrt, ALU.mult).then_inc(vector_done, 1)
                v.wait_ge(vector_done, v.done(vector_done))
                e.tensor_scalar(q, q, nsa_g[:, 0:1], None, ALU.mult).then_inc(vector_done, 1)
                v.wait_ge(vector_done, v.done(vector_done))

        def nr_act(act):
            a = act.eng
            act.wait_ge(vector_for_scalar, act.due(vector_for_scalar))
            a.activation(nsr, nsr, ACT.Sqrt, bias=eps[:, 0:1], scale=1.0 / DH).then_inc(scalar_done, 1)
            act.wait_ge(scalar_done, act.done(scalar_done))
            a.activation(NG, NG, ACT.Sigmoid).then_inc(scalar_done, 1)
            act.wait_ge(scalar_done, act.done(scalar_done))
            a.activation(GS, GS, ACT.Sigmoid).then_inc(scalar_done, 1)
            act.wait_ge(scalar_done, act.done(scalar_done))
            act.eng.sem_inc(scalar_for_vector, act.one(scalar_for_vector))
            for h in range(0, 8, 2):
                for j in range(2):
                    for c0, n in CHUNKS:
                        act.wait_ge(bank_full_a, act.due(bank_full_a))
                        b = act.ra.next()
                        a.activation(qrt[:, j, c0:c0 + n], b[0:64, 0:n], ACT.Sqrt, bias=eps[0:64, 0:1],
                                                      scale=1.0 / DH).then_inc(bank_read_a, 1)
                        act.wait_ge(bank_read_a, act.done(bank_read_a))
                act.eng.sem_inc(scalar_for_vector, act.one(scalar_for_vector))

        def nr_pe(pe):
            for h in range(0, 8, 2):
                pe.wait_ge(vector_for_tensor, pe.due(vector_for_tensor))
                for j in range(2):
                    for c0, n in CHUNKS:
                        pe.wait_ge(bank_read_a, pe.ra.freed())
                        b = pe.ra.next()
                        pe.eng.matmul(b[0:64, 0:n], ones[0:64, 0:64], qsq[:, j, c0:c0 + n],
                                                      start=True, stop=True).then_inc(bank_full_a, 1)

        arena.at = ns_mid
        wpr = arena.take(64, 256)
        wpT = arena.take(64, 4, 64)
        cmul = arena.take(64, 4, 2, 64)
        CT = arena.take(64, 4, 16)
        cks, ckr = arena.take(64, 32), arena.take(64, 32)
        CK = arena.take(64, 2, 16)
        CV = arena.take(16, 2, 64)
        CVD = arena.take(P, 512)
        SCR = arena.take(P, 8, 8, 16)
        mx, sm = arena.take(P, 64), arena.take(P, 64)
        vis = arena.take(P, 8, 16)
        fbias, finr = arena.take(P, 8, 16), arena.take(P, 8, 16)
        IMP, REP = arena.take(P, 16, 16), arena.take(P, 16, 16)
        top = arena.take(P, 16, 8)
        PcT = arena.take(P, P)
        SELB = arena.take(P, 16, 16)
        causal = arena.take(P, P)
        WM = arena.take(P, 5 * P)
        cm_end = arena.at

        def cm_sp(sp):
            sp.eng.dma_start(wpr, I["nsa_wpos"][0].rearrange("l c g d -> l (c g d)"),
                             allow_slow_non_contiguous=True).then_inc(loads_for_tensor, 16)
            sp.wait_ge(vector_for_sync, sp.due(vector_for_sync))
            for h in range(8):
                sp.eng.dma_start(CVD[16 * h:16 * h + 16, 64 * h:64 * h + 64], CV[:, h // 4],
                                 allow_slow_non_contiguous=True).then_inc(heads_moved, 16)
            sp.wait_ge(heads_moved, sp.due(heads_moved, 128))
            sp.eng.sem_inc(sync_for_tensor, sp.one(sync_for_tensor))

        def cm_gp(gp):
            g = gp.eng

            def keep(m, op, by, pat, b0, fill):
                g.affine_select(out=m, in_=m, compare_op=op, fill=fill, base=b0, pattern=pat,
                                      channel_multiplier=by).then_inc(gpsimd_done, 1)
                gp.wait_ge(gpsimd_done, gp.done(gpsimd_done))
            g.memset(CVD, 0.0).then_inc(gpsimd_done, 1)
            gp.wait_ge(gpsimd_done, gp.done(gpsimd_done))
            g.memset(vis, 0.0).then_inc(gpsimd_done, 1)
            gp.wait_ge(gpsimd_done, gp.done(gpsimd_done))
            keep(vis, ALU.is_ge, 1, [[P, 8], [-64, 16]], -63, NEG)
            g.memset(fbias, 0.0).then_inc(gpsimd_done, 1)
            gp.wait_ge(gpsimd_done, gp.done(gpsimd_done))
            g.memset(finr, 1.0).then_inc(gpsimd_done, 1)
            gp.wait_ge(gpsimd_done, gp.done(gpsimd_done))
            keep(fbias, ALU.is_ge, 1, [[P, 8], [-64, 16]], -128, BIG)
            keep(fbias, ALU.is_ge, 1, [[P, 8], [-64, 16]], 0, -BIG)
            keep(finr, ALU.is_ge, 1, [[P, 8], [-64, 16]], -128, 0.0)
            g.memset(fbias[:, :, 0:1], BIG).then_inc(gpsimd_done, 1)
            gp.wait_ge(gpsimd_done, gp.done(gpsimd_done))
            g.memset(finr[:, :, 0:1], 0.0).then_inc(gpsimd_done, 1)
            gp.wait_ge(gpsimd_done, gp.done(gpsimd_done))
            g.memset(causal, 0.0).then_inc(gpsimd_done, 1)
            gp.wait_ge(gpsimd_done, gp.done(gpsimd_done))
            keep(causal, ALU.is_ge, 1, [[-1, P]], 0, NEG)
            g.memset(WM, 0.0).then_inc(gpsimd_done, 1)
            gp.wait_ge(gpsimd_done, gp.done(gpsimd_done))
            keep(WM[:, 0:P], ALU.is_gt, -1, [[1, P]], 0, NEG)
            keep(WM[:, 4 * P:5 * P], ALU.is_ge, 1, [[-1, P]], 0, NEG)
            gp.eng.sem_inc(gpsimd_for_vector, gp.one(gpsimd_for_vector))

        def keys_turn_pe(pe, c, i):
            pe.wait_ge(bank_read_a, pe.ra.freed())
            b = pe.ra.next()
            for g in range(2):
                ins = pe.eng.transpose(b[0:64, g * P:(g + 1) * P], NR[:, i, c + g * 64:c + (g + 1) * 64], ident)
            ins.then_inc(bank_full_a, 1)

        def cm_pe(pe):
            mm = pe.eng.matmul
            for i in range(8):
                keys_turn_pe(pe, 256, i)
                keys_turn_pe(pe, 512, i)
            pe.wait_ge(loads_for_tensor, pe.due(loads_for_tensor, 32))
            pe.wait_ge(bank_read_v, pe.rv.freed())
            b = pe.rv.next()
            for q in range(4):
                ins = pe.eng.transpose(b[0:64, q * 64:(q + 1) * 64], wpr[:, q * 64:(q + 1) * 64], ident[0:64, 0:64])
            ins.then_inc(bank_full_v, 1)
            for i in range(8):
                pe.wait_ge(bank_read_v, pe.rv.freed())
                b = pe.rv.next()
                for q in range(4):
                    ins = pe.eng.transpose(b[0:64, q * P:(q + 1) * P], NR[:, i, q * 64:(q + 1) * 64], ident)
                ins.then_inc(bank_full_v, 1)
            pe.wait_ge(vector_for_tensor, pe.due(vector_for_tensor))
            pe.wait_ge(bank_read_v, pe.rv.freed())
            b = pe.rv.next()
            for g in range(2):
                ins = mm(b[0:64, g * 16:(g + 1) * 16], wc[:, 0, g], CT[:, g], start=True, stop=True)
            ins.then_inc(bank_full_v, 1)
            pe.wait_ge(bank_read_v, pe.rv.freed())
            b = pe.rv.next()
            for g in range(2):
                ins = mm(b[0:16, g * 64:(g + 1) * 64], CT[:, 2 + g], wc[:, 1, g], start=True, stop=True)
            ins.then_inc(bank_full_v, 1)
            pe.wait_ge(vector_for_tensor, pe.due(vector_for_tensor))
            pe.wait_ge(bank_read_a, pe.ra.freed())
            b = pe.ra.next()
            mm(b[0:64, 0:32], ones[0:64, 0:64], cks, start=True, stop=True).then_inc(bank_full_a, 1)
            pe.wait_ge(vector_for_tensor, pe.due(vector_for_tensor))
            for i in range(8):
                pe.wait_ge(bank_read_v, pe.rv.freed())
                b = pe.rv.next()
                for h in range(8):
                    ins = mm(b[:, h * 16:(h + 1) * 16], NQ[:, h, i * P:(i + 1) * P], CK[:, h // 4], start=True, stop=True)
                ins.then_inc(bank_full_v, 1)
            pe.wait_ge(vector_for_tensor, pe.due(vector_for_tensor))
            pe.wait_ge(sync_for_tensor, pe.due(sync_for_tensor))
            for i in range(8):
                pe.wait_ge(bank_read_a, pe.ra.freed())
                b = pe.ra.next()
                pe.eng.transpose(b[:, 0:P], SCR[:, i].rearrange("p h n -> p (h n)"), ident).then_inc(bank_full_a, 1)
                pe.wait_ge(scalar_for_tensor, pe.due(scalar_for_tensor))
                pe.wait_ge(bank_read_v, pe.rv.freed())
                b = pe.rv.next()
                mm(b, PcT, CVD, start=True, stop=True).then_inc(bank_full_v, 1)

        def cm_act(act):
            a = act.eng
            for i in range(8):
                for dst in (KST, KWT):
                    act.wait_ge(bank_full_a, act.due(bank_full_a))
                    b = act.ra.next()
                    a.copy(dst[:, :, i * P:(i + 1) * P], b[0:64, 0:256].rearrange("p (g c) -> p g c", g=2)).then_inc(bank_read_a, 1)
                    act.wait_ge(bank_read_a, act.done(bank_read_a))
            act.wait_ge(bank_full_a, act.due(bank_full_a))
            b = act.ra.next()
            a.activation(ckr, b[0:64, 0:32], ACT.Sqrt, bias=eps[0:64, 0:1], scale=1.0 / DH).then_inc(bank_read_a, 1)
            act.wait_ge(bank_read_a, act.done(bank_read_a))
            act.eng.sem_inc(scalar_for_vector, act.one(scalar_for_vector))
            act.wait_ge(vector_for_scalar, act.due(vector_for_scalar))
            a.activation(SCR, SCR, ACT.Exp, scale=SCALE).then_inc(scalar_done, 1)
            act.wait_ge(scalar_done, act.done(scalar_done))
            act.eng.sem_inc(scalar_for_vector, act.one(scalar_for_vector))
            for i in range(8):
                act.wait_ge(bank_full_a, act.due(bank_full_a))
                b = act.ra.next()
                if i:
                    act.wait_ge(vector_for_scalar, act.due(vector_for_scalar))
                a.copy(PcT, b[:, 0:P]).then_inc(bank_read_a, 1)
                act.wait_ge(bank_read_a, act.done(bank_read_a))
                act.eng.sem_inc(scalar_for_tensor, act.one(scalar_for_tensor))
            act.wait_ge(vector_for_scalar, act.due(vector_for_scalar))

        def softmax_dve(v, s, m, z, rows, groups, n):
            e = v.eng
            e.tensor_reduce(m, s, AX.X, ALU.max).then_inc(vector_done, 1)
            v.wait_ge(vector_done, v.done(vector_done))
            e.tensor_scalar(m, m, -1e29, None, ALU.max).then_inc(vector_done, 1)
            v.wait_ge(vector_done, v.done(vector_done))
            e.tensor_tensor(s, s, m.unsqueeze(2).broadcast_to([rows, groups, n]), ALU.subtract).then_inc(vector_done, 1)
            v.wait_ge(vector_done, v.done(vector_done))
            v.eng.sem_inc(vector_for_scalar, v.one(vector_for_scalar))
            v.wait_ge(scalar_for_vector, v.due(scalar_for_vector))
            e.tensor_reduce(z, s, AX.X, ALU.add).then_inc(vector_done, 1)
            v.wait_ge(vector_done, v.done(vector_done))
            e.tensor_scalar(z, z, 1e-30, None, ALU.max).then_inc(vector_done, 1)
            v.wait_ge(vector_done, v.done(vector_done))
            e.reciprocal(z, z).then_inc(vector_done, 1)
            v.wait_ge(vector_done, v.done(vector_done))
            e.tensor_tensor(s, s, z.unsqueeze(2).broadcast_to([rows, groups, n]), ALU.mult).then_inc(vector_done, 1)
            v.wait_ge(vector_done, v.done(vector_done))

        def cm_dve(v):
            e = v.eng
            v.wait_ge(gpsimd_for_vector, v.due(gpsimd_for_vector))
            v.wait_ge(bank_full_v, v.due(bank_full_v))
            b = v.rv.next()
            e.tensor_copy(wpT, b[0:64, 0:256].rearrange("p (q l) -> p q l", q=4)).then_inc(bank_read_v, 1)
            v.wait_ge(bank_read_v, v.done(bank_read_v))
            for i in range(8):
                v.wait_ge(bank_full_v, v.due(bank_full_v))
                b = v.rv.next()
                for n in range(2):
                    ins = e.tensor_tensor(cmul[:, :, n], b[0:64].rearrange("p (q n l) -> p q n l", q=4, n=2)[:, :, n],
                                          wpT, ALU.mult)
                    if n == 0:
                        ins.then_inc(vector_done, 1)
                        v.wait_ge(vector_done, v.done(vector_done))
                ins.then_inc(bank_read_v, 1)
                v.wait_ge(bank_read_v, v.done(bank_read_v))
                e.tensor_reduce(CT[:, :, 2 * i:2 * i + 2], cmul, AX.X, ALU.add).then_inc(vector_done, 1)
                v.wait_ge(vector_done, v.done(vector_done))
            v.eng.sem_inc(vector_for_tensor, v.one(vector_for_tensor))
            v.wait_ge(bank_full_v, v.due(bank_full_v))
            b = v.rv.next()
            e.tensor_copy(CK, b[0:64, 0:32].rearrange("p (g n) -> p g n", g=2)).then_inc(bank_read_v, 1)
            v.wait_ge(bank_read_v, v.done(bank_read_v))
            ckf = CK.rearrange("p g n -> p (g n)")
            v.wait_ge(bank_full_v, v.due(bank_full_v))
            b = v.rv.next()
            e.tensor_copy(CV, b[0:16, 0:128].rearrange("p (g d) -> p g d", g=2)).then_inc(bank_read_v, 1)
            v.wait_ge(bank_read_v, v.done(bank_read_v))
            v.eng.sem_inc(vector_for_sync, v.one(vector_for_sync))
            e.tensor_tensor(cks, ckf, ckf, ALU.mult).then_inc(vector_for_tensor, 1)
            v.wait_ge(vector_for_tensor, v.done(vector_for_tensor))
            v.wait_ge(scalar_for_vector, v.due(scalar_for_vector))
            e.reciprocal(ckr, ckr).then_inc(vector_done, 1)
            v.wait_ge(vector_done, v.done(vector_done))
            e.tensor_tensor(ckf, ckf, ckr, ALU.mult).then_inc(vector_done, 1)
            v.wait_ge(vector_done, v.done(vector_done))
            e.tensor_scalar(ckf, ckf, nsa_g[:, 1:2], None, ALU.mult).then_inc(vector_done, 1)
            v.wait_ge(vector_done, v.done(vector_done))
            v.eng.sem_inc(vector_for_tensor, v.one(vector_for_tensor))
            for i in range(8):
                v.wait_ge(bank_full_v, v.due(bank_full_v))
                b = v.rv.next()
                e.tensor_tensor(SCR[:, i], b[:, 0:128].rearrange("p (h n) -> p h n", h=8),
                                             vis[:, i].unsqueeze(1).broadcast_to([P, 8, 16]), ALU.add).then_inc(bank_read_v, 1)
                v.wait_ge(bank_read_v, v.done(bank_read_v))
            softmax_dve(v, SCR.rearrange("p i h n -> p (i h) n"), mx, sm, P, 64, 16)
            v.eng.sem_inc(vector_for_tensor, v.one(vector_for_tensor))
            e.tensor_reduce(IMP, SCR.rearrange("p i (g r) n -> p (i g) n r", g=2), AX.X, ALU.add).then_inc(vector_done, 1)
            v.wait_ge(vector_done, v.done(vector_done))
            im = IMP.rearrange("p (i g) n -> p i g n", g=2)
            for x, op in ((finr, ALU.mult), (fbias, ALU.add)):
                e.tensor_tensor(im, im, x.unsqueeze(2).broadcast_to([P, 8, 2, 16]), op).then_inc(vector_done, 1)
                v.wait_ge(vector_done, v.done(vector_done))
            for k in range(16):
                e.max(top[:, k], IMP[:, k]).then_inc(vector_done, 1)
                v.wait_ge(vector_done, v.done(vector_done))
                e.match_replace(REP[:, k], top[:, k], IMP[:, k], -3e38).then_inc(vector_done, 1)
                v.wait_ge(vector_done, v.done(vector_done))
            e.tensor_tensor(SELB, REP, IMP, ALU.not_equal).then_inc(vector_done, 1)
            v.wait_ge(vector_done, v.done(vector_done))
            e.tensor_scalar(SELB, SELB, -1.0, -NEG, ALU.add, ALU.mult).then_inc(vector_done, 1)
            v.wait_ge(vector_done, v.done(vector_done))
            for i in range(8):
                v.wait_ge(bank_full_v, v.due(bank_full_v))
                b = v.rv.next()
                e.tensor_tensor(OUT[:, i].rearrange("p (h d) -> p h d", h=8),
                                             b.rearrange("p (h d) -> p h d", h=8),
                                             NG[:, i, 0:24:3].unsqueeze(2).broadcast_to([P, 8, 64]), ALU.mult).then_inc(bank_read_v, 1)
                v.wait_ge(bank_read_v, v.done(bank_read_v))
                v.eng.sem_inc(vector_for_scalar, v.one(vector_for_scalar))

        arena.at = cm_end
        SS = arena.take(P, 3, TP)
        PT2 = arena.take(P, 2, 8, P)
        SM = arena.take(P, TP)
        am = arena.take(P, 3, 4)
        UNITS = [(br, i, h) for br in range(2) for i in range(8) for h in range(8)]

        def keys_of(u):
            br, i, h = u
            return (0 if br == 0 else max(0, i - 4)), i + 1

        def at_pe(pe):
            mm = pe.eng.matmul

            def scores(u):
                br, i, h = u
                a, z = keys_of(u)
                kt = KST if br == 0 else KWT
                for c in range(a * P, z * P, BANK):
                    n = min(BANK, z * P - c)
                    pe.wait_ge(bank_read_v, pe.rv.freed())
                    b = pe.rv.next()
                    mm(b[:, 0:n], NQ[:, h, i * P:(i + 1) * P], kt[:, h // 4, c:c + n],
                                       start=True, stop=True).then_inc(bank_full_v, 1)
            def turn(k, u):
                a, z = keys_of(u)
                pe.wait_ge(scalar_for_tensor, pe.due(scalar_for_tensor))
                for t in range(0, z - a, 4):
                    pe.wait_ge(bank_read_a, pe.ra.freed())
                    b = pe.ra.next()
                    for s in range(t, min(t + 4, z - a)):
                        ins = pe.eng.transpose(b[:, (s - t) * P:(s - t + 1) * P], SS[:, k % 3, s * P:(s + 1) * P], ident)
                    ins.then_inc(bank_full_a, 1)
            scores(UNITS[0])
            scores(UNITS[1])
            turn(0, UNITS[0])
            for k, u in enumerate(UNITS):
                if k + 2 < len(UNITS):
                    scores(UNITS[k + 2])
                if k + 1 < len(UNITS):
                    turn(k + 1, UNITS[k + 1])
                br, i, h = u
                a, z = keys_of(u)
                pe.wait_ge(scalar_turned, pe.due(scalar_turned))
                c = (384 if br == 0 else 640) + 64 * (h // 4)
                pe.wait_ge(bank_read_v, pe.rv.freed())
                b = pe.rv.next()
                for s in range(z - a):
                    ins = mm(b[:, 0:64], PT2[:, k % 2, s], NR[:, a + s, c:c + 64], start=(s == 0), stop=(s == z - a - 1))
                ins.then_inc(bank_full_v, 1)

        def at_act(act):
            a_ = act.eng
            for k, u in enumerate(UNITS):
                a, z = keys_of(u)
                s = SS[:, k % 3, 0:(z - a) * P]
                act.wait_ge(vector_for_scalar, act.due(vector_for_scalar))
                a_.activation(s, s, ACT.Exp, bias=am[:, k % 3, 1:2], scale=SCALE, accum_out=am[:, k % 3, 2:3]).then_inc(scalar_done, 1)
                act.wait_ge(scalar_done, act.done(scalar_done))
                act.eng.sem_inc(scalar_for_tensor, act.one(scalar_for_tensor))
                act.eng.sem_inc(scalar_for_vector, act.one(scalar_for_vector))
                for t in range(0, z - a, 4):
                    n = min(4, z - a - t)
                    act.wait_ge(bank_full_a, act.due(bank_full_a))
                    b = act.ra.next()
                    a_.copy(PT2[:, k % 2, t:t + n], b[:, 0:n * P].rearrange("p (s c) -> p s c", c=P)).then_inc(bank_read_a, 1)
                    act.wait_ge(bank_read_a, act.done(bank_read_a))
                act.eng.sem_inc(scalar_turned, act.one(scalar_turned))

        def at_dve(v):
            e = v.eng

            def prepare(k, u):
                br, i, h = u
                a, z = keys_of(u)
                if br == 0 and h % 4 == 0:
                    nb = 2 * z
                    e.tensor_copy(SM[:, 0:z * P].rearrange("p (n l) -> p n l", l=64),
                                       SELB[:, 2 * i + h // 4, 0:nb].unsqueeze(2).broadcast_to([P, nb, 64])).then_inc(vector_done, 1)
                    v.wait_ge(vector_done, v.done(vector_done))
                    e.tensor_tensor(SM[:, i * P:z * P], SM[:, i * P:z * P], causal, ALU.add).then_inc(vector_done, 1)
                    v.wait_ge(vector_done, v.done(vector_done))
                mask = SM if br == 0 else WM[:, (4 - (i - a)) * P:]
                w = am[:, k % 3]
                for j, c in enumerate(range(0, (z - a) * P, BANK)):
                    n = min(BANK, (z - a) * P - c)
                    v.wait_ge(bank_full_v, v.due(bank_full_v))
                    b = v.rv.next()
                    e.tensor_tensor(SS[:, k % 3, c:c + n], b[:, 0:n], mask[:, c:c + n], ALU.add).then_inc(bank_read_v, 1)
                    v.wait_ge(bank_read_v, v.done(bank_read_v))
                e.tensor_reduce(w[:, 0:1], SS[:, k % 3, 0:(z - a) * P], AX.X, ALU.max).then_inc(vector_done, 1)
                v.wait_ge(vector_done, v.done(vector_done))
                e.tensor_scalar(w[:, 1:2], w[:, 0:1], -SCALE, None, ALU.mult).then_inc(vector_done, 1)
                v.wait_ge(vector_done, v.done(vector_done))
                v.eng.sem_inc(vector_for_scalar, v.one(vector_for_scalar))

            def finish(k, u):
                br, i, h = u
                w = am[:, k % 3]
                v.wait_ge(scalar_for_vector, v.due(scalar_for_vector))
                e.reciprocal(w[:, 3:4], w[:, 2:3]).then_inc(vector_done, 1)
                v.wait_ge(vector_done, v.done(vector_done))
                e.tensor_tensor(w[:, 3:4], w[:, 3:4], NG[:, i, 3 * h + 1 + br:3 * h + 2 + br], ALU.mult).then_inc(vector_done, 1)
                v.wait_ge(vector_done, v.done(vector_done))
                v.wait_ge(bank_full_v, v.due(bank_full_v))
                b = v.rv.next()
                o = OUT[:, i, h * 64:(h + 1) * 64]
                e.scalar_tensor_tensor(out=o, in0=b[:, 0:64], scalar=w[:, 3:4], in1=o,
                                                    op0=ALU.mult, op1=ALU.add).then_inc(bank_read_v, 1)
                v.wait_ge(bank_read_v, v.done(bank_read_v))
            prepare(0, UNITS[0])
            prepare(1, UNITS[1])
            for k, u in enumerate(UNITS):
                if k + 2 < len(UNITS):
                    prepare(k + 2, UNITS[k + 2])
                finish(k, u)

        OS = arena.array[:, ns_mid:ns_mid + 2 * 512].rearrange("p (s j c) -> p s j c", s=2, j=4)

        def ot_pe(pe):
            for i in range(8):
                pe.wait_ge(bank_read_a, pe.ra.freed())
                b = pe.ra.next()
                for j in range(4):
                    ins = pe.eng.transpose(b[:, j * P:(j + 1) * P], OUT[:, i, j * P:(j + 1) * P], ident)
                ins.then_inc(bank_full_a, 1)

        def ot_act(act):
            for i in range(8):
                if i >= 2:
                    act.wait_ge(slot_stored[i % 2], act.due(slot_stored[i % 2], 16))
                act.wait_ge(bank_full_a, act.due(bank_full_a))
                b = act.ra.next()
                act.eng.copy(OS[:, i % 2], b.rearrange("p (j c) -> p j c", j=4)).then_inc(bank_read_a, 1)
                act.wait_ge(bank_read_a, act.done(bank_read_a))
                act.eng.dma_start(mixT[512:1024, i * P:(i + 1) * P].rearrange("(j p) r -> p j r", p=P), OS[:, i % 2],
                                 allow_slow_non_contiguous=True).then_inc(slot_stored[i % 2], 16)
            act.wait_ge(slot_stored[0], act.due(slot_stored[0], 16))
            act.wait_ge(slot_stored[1], act.due(slot_stored[1], 16))

        arena.at = ns_keep
        QB = arena.take(P, NB, 64)
        selgt = arena.take(64, 64)
        selt8 = arena.take(8, 64)
        m8 = arena.take(8, 2, 512)
        MN_ = arena.take(64, NB, TS)
        seqm = arena.take(64, NB, NB)
        blk2 = arena.take(64, 2)
        MW = arena.take(64, 512)
        SB = arena.take(64, NB, 65)
        OB = arena.take(64, NB, 64)
        KTn = arena.take(P, 2, 64)
        OTs = arena.take(64, 8, NB, TS)
        sa_keep = arena.at
        CTs = arena.take(64, 4, 512)
        cq, cr = arena.take(64, 2, 512), arena.take(64, 2, 512)
        CKs = arena.take(64, 2, 512)
        CK2 = arena.take(P, 512)
        CVs = arena.take(64, NB, P)
        PS = arena.take(64, NB, 64)
        pmx, psm = arena.take(64, NB), arena.take(64, NB)
        PTs = arena.take(64, NB, 64)
        IMs, REs = arena.take(64, NB, 65), arena.take(64, NB, 65)
        tps = arena.take(64, NB, 8)

        def sc_sp(sp):
            sp.eng.dma_start(CTs, pooled,
                             allow_slow_non_contiguous=True).then_inc(loads_for_tensor, 16)
            sp.wait_ge(gpsimd_for_sync, sp.due(gpsimd_for_sync))
            for g in range(2):
                for r in range(4):
                    sp.eng.dma_start(QB[64 * g:64 * g + 64, :, g * 32 + r * 8:g * 32 + r * 8 + 8], NQ[:, 4 * g + r, TP:R].rearrange("p (b t) -> p b t", b=NB),
                                     allow_slow_non_contiguous=True).then_inc(heads_moved, 16)
            for h in range(8):
                sp.eng.dma_start(MN_[8 * h:8 * h + 8].rearrange("p b t -> p (b t)"), m8[:, 0, 0:64],
                                 allow_slow_non_contiguous=True).then_inc(heads_moved, 16)
                sp.eng.dma_start(MW[8 * h:8 * h + 8], m8[:, 1],
                                 allow_slow_non_contiguous=True).then_inc(heads_moved, 16)
            sp.wait_ge(heads_moved, sp.due(heads_moved, 16 * 24))
            sp.eng.sem_inc(sync_for_tensor, sp.one(sync_for_tensor))
            sp.eng.sem_inc(sync_for_vector, sp.one(sync_for_vector))
            sp.wait_ge(vector_for_sync, sp.due(vector_for_sync))
            for g in range(2):
                sp.eng.dma_start(CK2[64 * g:64 * g + 64], CKs[:, g],
                                 allow_slow_non_contiguous=True).then_inc(heads_moved, 16)
            sp.wait_ge(heads_moved, sp.due(heads_moved, 32))
            sp.eng.sem_inc(sync_for_tensor, sp.one(sync_for_tensor))

        def sc_gp(gp):
            g = gp.eng

            def keep(m, op, by, pat, b0, fill):
                g.affine_select(out=m, in_=m, compare_op=op, fill=fill, base=b0, pattern=pat,
                                      channel_multiplier=by).then_inc(gpsimd_done, 1)
                gp.wait_ge(gpsimd_done, gp.done(gpsimd_done))
            g.memset(QB, 0.0).then_inc(gpsimd_done, 1)
            gp.wait_ge(gpsimd_done, gp.done(gpsimd_done))
            g.memset(m8, 0.0).then_inc(gpsimd_done, 1)
            gp.wait_ge(gpsimd_done, gp.done(gpsimd_done))
            mn = m8[:, 0, 0:64].rearrange("p (b t) -> p b t", b=NB)
            keep(mn, ALU.is_ge, 1, [[0, NB], [-1, TS]], 0, NEG)
            keep(m8[:, 1], ALU.is_gt, -1, [[1, 512]], 0, NEG)
            g.memset(seqm, 0.0).then_inc(gpsimd_done, 1)
            gp.wait_ge(gpsimd_done, gp.done(gpsimd_done))
            keep(seqm, ALU.is_equal, 0, [[1, NB], [-1, NB]], 0, NEG)
            g.memset(blk2, 1.0).then_inc(gpsimd_done, 1)
            gp.wait_ge(gpsimd_done, gp.done(gpsimd_done))
            keep(blk2[:, 0:1], ALU.is_ge, -1, [[0, 1]], 31, 0.0)
            keep(blk2[:, 1:2], ALU.is_ge, 1, [[0, 1]], -32, 0.0)
            g.memset(selt8, 1.0).then_inc(gpsimd_done, 1)
            gp.wait_ge(gpsimd_done, gp.done(gpsimd_done))
            keep(selt8.rearrange("p (h t) -> p h t", h=8), ALU.is_equal, 1, [[0, 8], [-1, TS]], 0, 0.0)
            gp.eng.sem_inc(gpsimd_for_vector, gp.one(gpsimd_for_vector))
            gp.eng.sem_inc(gpsimd_for_sync, gp.one(gpsimd_for_sync))
            gp.eng.sem_inc(gpsimd_for_tensor, gp.one(gpsimd_for_tensor))

        def sc_pe(pe):
            mm = pe.eng.matmul
            pe.wait_ge(gpsimd_for_tensor, pe.due(gpsimd_for_tensor))
            pe.wait_ge(bank_read_v, pe.rv.freed())
            b = pe.rv.next()
            mm(b[0:64, 0:64], selt8, selt8, start=True, stop=True).then_inc(bank_full_v, 1)
            pe.wait_ge(bank_read_v, pe.rv.freed())
            b = pe.rv.next()
            for i, c in enumerate((256, 512)):
                ins = pe.eng.transpose(b[:, i * 64:(i + 1) * 64], NR[0:64, 8, c:c + P], ident[0:64, 0:64])
            ins.then_inc(bank_full_v, 1)
            pe.wait_ge(loads_for_tensor, pe.due(loads_for_tensor, 16))
            for g in range(2):
                pe.wait_ge(bank_read_v, pe.rv.freed())
                b = pe.rv.next()
                mm(b[0:64], wc[:, 0, g], CTs[:, g], start=True, stop=True).then_inc(bank_full_v, 1)
            for half in range(2):
                pe.wait_ge(bank_read_v, pe.rv.freed())
                b = pe.rv.next()
                for q in range(4):
                    for g in range(2):
                        k = 4 * half + q
                        ins = mm(b[0:64, q * P + g * 64:q * P + g * 64 + 64], CTs[:, 2 + g, k * 64:(k + 1) * 64],
                                 wc[:, 1, g], start=True, stop=True)
                ins.then_inc(bank_full_v, 1)
            pe.wait_ge(vector_for_tensor, pe.due(vector_for_tensor))
            for g in range(2):
                pe.wait_ge(bank_read_a, pe.ra.freed())
                b = pe.ra.next()
                mm(b[0:64], ones[0:64, 0:64], cq[:, g], start=True, stop=True).then_inc(bank_full_a, 1)
            pe.wait_ge(sync_for_tensor, pe.due(sync_for_tensor, 2))
            pe.wait_ge(bank_read_v, pe.rv.freed())
            b = pe.rv.next()
            for k in range(NB):
                ins = mm(b[0:64, k * 64:(k + 1) * 64], QB[:, k], CK2[:, k * 64:(k + 1) * 64], start=True, stop=True)
            ins.then_inc(bank_full_v, 1)
            pe.wait_ge(vector_for_tensor, pe.due(vector_for_tensor))
            pe.wait_ge(bank_read_v, pe.rv.freed())
            b = pe.rv.next()
            mm(b[0:64], selgt, PS.rearrange("p b n -> p (b n)"), start=True, stop=True).then_inc(bank_full_v, 1)
            pe.wait_ge(bank_read_v, pe.rv.freed())
            b = pe.rv.next()
            for k in range(NB):
                ins = pe.eng.transpose(b[0:64, k * 64:(k + 1) * 64], PS[:, k], ident[0:64, 0:64])
            ins.then_inc(bank_full_v, 1)
            pe.wait_ge(vector_for_tensor, pe.due(vector_for_tensor))
            for half in range(2):
                pe.wait_ge(bank_read_v, pe.rv.freed())
                b = pe.rv.next()
                for q in range(4):
                    k = 4 * half + q
                    ins = mm(b[0:64, q * P:(q + 1) * P], PTs[:, k], CVs[:, k], start=True, stop=True)
                ins.then_inc(bank_full_v, 1)

        def sc_act(act):
            a = act.eng
            for g in range(2):
                act.wait_ge(bank_full_a, act.due(bank_full_a))
                b = act.ra.next()
                a.activation(cr[:, g], b[0:64], ACT.Sqrt, bias=eps[0:64, 0:1], scale=1.0 / DH).then_inc(bank_read_a, 1)
                act.wait_ge(bank_read_a, act.done(bank_read_a))
            act.eng.sem_inc(scalar_for_vector, act.one(scalar_for_vector))
            act.wait_ge(vector_for_scalar, act.due(vector_for_scalar))
            a.activation(PS, PS, ACT.Exp, scale=SCALE).then_inc(scalar_done, 1)
            act.wait_ge(scalar_done, act.done(scalar_done))
            act.eng.sem_inc(scalar_for_vector, act.one(scalar_for_vector))

        def sc_dve(v):
            e = v.eng
            v.wait_ge(gpsimd_for_vector, v.due(gpsimd_for_vector))
            v.wait_ge(bank_full_v, v.due(bank_full_v))
            b = v.rv.next()
            e.tensor_copy(selgt, b[0:64, 0:64]).then_inc(bank_read_v, 1)
            v.wait_ge(bank_read_v, v.done(bank_read_v))
            e.tensor_tensor(selgt[:, 0:32], selgt[:, 0:32], blk2[0:64, 0:1].broadcast_to([64, 32]), ALU.mult).then_inc(vector_done, 1)
            v.wait_ge(vector_done, v.done(vector_done))
            e.tensor_tensor(selgt[:, 32:64], selgt[:, 32:64], blk2[0:64, 1:2].broadcast_to([64, 32]), ALU.mult).then_inc(vector_done, 1)
            v.wait_ge(vector_done, v.done(vector_done))
            v.wait_ge(bank_full_v, v.due(bank_full_v))
            b = v.rv.next()
            e.tensor_copy(KTn, b[:, 0:128].rearrange("p (i c) -> p i c", i=2)).then_inc(bank_read_v, 1)
            v.wait_ge(bank_read_v, v.done(bank_read_v))
            v.wait_ge(sync_for_vector, v.due(sync_for_vector))

            for g in range(2):
                v.wait_ge(bank_full_v, v.due(bank_full_v))
                b = v.rv.next()
                e.tensor_copy(CKs[:, g], b[0:64]).then_inc(bank_read_v, 1)
                v.wait_ge(bank_read_v, v.done(bank_read_v))
            for half in range(2):
                v.wait_ge(bank_full_v, v.due(bank_full_v))
                b = v.rv.next()
                e.tensor_copy(CVs[:, 4 * half:4 * half + 4], b[0:64].rearrange("p (q c) -> p q c", q=4)).then_inc(bank_read_v, 1)
                v.wait_ge(bank_read_v, v.done(bank_read_v))
            e.tensor_tensor(cq, CKs, CKs, ALU.mult).then_inc(vector_for_tensor, 1)
            v.wait_ge(vector_for_tensor, v.done(vector_for_tensor))
            v.wait_ge(scalar_for_vector, v.due(scalar_for_vector))
            e.reciprocal(cr, cr).then_inc(vector_done, 1)
            v.wait_ge(vector_done, v.done(vector_done))
            e.tensor_tensor(CKs, CKs, cr, ALU.mult).then_inc(vector_done, 1)
            v.wait_ge(vector_done, v.done(vector_done))
            e.tensor_scalar(CKs, CKs, nsa_g[:, 1:2], None, ALU.mult).then_inc(vector_done, 1)
            v.wait_ge(vector_done, v.done(vector_done))
            v.eng.sem_inc(vector_for_sync, v.one(vector_for_sync))
            v.wait_ge(bank_full_v, v.due(bank_full_v))
            b = v.rv.next()
            e.tensor_copy(PS, b[0:64].rearrange("p (b n) -> p b n", b=NB)).then_inc(bank_read_v, 1)
            v.wait_ge(bank_read_v, v.done(bank_read_v))
            softmax_dve(v, PS, pmx, psm, 64, NB, 64)
            v.eng.sem_inc(vector_for_tensor, v.one(vector_for_tensor))
            v.wait_ge(bank_full_v, v.due(bank_full_v))
            b = v.rv.next()
            e.tensor_copy(IMs[:, :, 0:64], b[0:64].rearrange("p (b n) -> p b n", b=NB)).then_inc(bank_read_v, 1)
            v.wait_ge(bank_read_v, v.done(bank_read_v))
            e.memset(IMs[:, :, 0:1], BIG).then_inc(vector_done, 1)
            v.wait_ge(vector_done, v.done(vector_done))
            e.memset(IMs[:, :, 63:65], BIG).then_inc(vector_done, 1)
            v.wait_ge(vector_done, v.done(vector_done))
            v.wait_ge(bank_full_v, v.due(bank_full_v))
            b = v.rv.next()
            e.tensor_copy(PTs, b[0:64].rearrange("p (b n) -> p b n", b=NB)).then_inc(bank_read_v, 1)
            v.wait_ge(bank_read_v, v.done(bank_read_v))
            v.eng.sem_inc(vector_for_tensor, v.one(vector_for_tensor))
            for k in range(NB):
                e.max(tps[:, k], IMs[:, k]).then_inc(vector_done, 1)
                v.wait_ge(vector_done, v.done(vector_done))
                e.match_replace(REs[:, k], tps[:, k], IMs[:, k], -3e38).then_inc(vector_done, 1)
                v.wait_ge(vector_done, v.done(vector_done))
            e.tensor_tensor(SB, REs, IMs, ALU.not_equal).then_inc(vector_done, 1)
            v.wait_ge(vector_done, v.done(vector_done))
            e.tensor_scalar(SB, SB, -1.0, -NEG, ALU.add, ALU.mult).then_inc(vector_done, 1)
            v.wait_ge(vector_done, v.done(vector_done))
            for half in range(2):
                v.wait_ge(bank_full_v, v.due(bank_full_v))
                b = v.rv.next()
                bs = b[0:64].rearrange("p (q c) -> p q c", q=4)
                for g in range(2):
                    p = slice(32 * g, 32 * g + 32)
                    gt = GS[p, 4 * half:4 * half + 4, 0:1].broadcast_to([32, 4, 64])
                    ins = e.tensor_tensor(OB[p, 4 * half:4 * half + 4], bs[p, :, g * 64:(g + 1) * 64], gt, ALU.mult)
                    if g == 0:
                        ins.then_inc(vector_done, 1)
                        v.wait_ge(vector_done, v.done(vector_done))
                ins.then_inc(bank_read_v, 1)
                v.wait_ge(bank_read_v, v.done(bank_read_v))

        arena.at = sa_keep
        VBs = arena.take(P, 2, NPG, 256)
        aw = arena.take(64, 2, 4)
        arena.at = base
        KT = arena.take(P, PAST)
        S4 = arena.take(64, PAST + 64)
        assert arena.at <= base + 8 * R
        arena.at = base + 8 * R
        PT4 = arena.take(P, NPG, 64)
        PTn = arena.take(64, 64)
        VBw = arena.take(P, 2, WIN // P, 256)
        S4w = arena.take(64, WIN + 64)
        KTw = arena.take(P, WIN)
        PT4w = arena.take(P, WIN // P, 64)
        PTnw = arena.take(64, 64)
        assert arena.at <= base + 8 * R + 8 * 792
        S4b, KTb, PT4b, PTnb = (S4, S4w), (KT, KTw), (PT4, PT4w), (PTn, PTnw)
        VB = (VBs, VBw)
        SU = [(br, q) for q in range(NB) for br in range(2)]
        UT = {0: NPG, 1: WIN // P}

        def ss_gp(gp):
            g = gp.eng
            for k, (br, q) in enumerate(SU):
                if k >= 4:
                    gp.wait_ge(vector_for_gpsimd, gp.due(vector_for_gpsimd))
                if br == 0:
                    for t in range(NPG):
                        g.indirect_dma_start(out=VBs[:, q % 2, t], out_offset=None, in_=rows_of(I["cache_nsa_sel"]),
                                                     in_offset=bass.IndirectOffsetOnAxis(
                                                         ap=idx_u[:, q * NPG + t:q * NPG + t + 1], axis=0)).then_inc(cache_in[2 * br + q % 2], 16)
                else:
                    gp.eng.dma_start(VBw[:, q % 2], I["cache_nsa_win"][0, q].rearrange("(i p) c g d -> p i (c g d)", p=P),
                                     allow_slow_non_contiguous=True).then_inc(cache_in[2 * br + q % 2], 16)
            gp.wait_ge(vector_for_gpsimd, gp.due(vector_for_gpsimd, 4))

        def ss_pe(pe):
            mm = pe.eng.matmul

            def scores(k):
                br, q = SU[k]
                nt = UT[br]
                pe.wait_ge(cache_in[2 * br + q % 2], pe.due(cache_in[2 * br + q % 2], 16 * (nt if br == 0 else 1)))

                def turn(t):
                    pe.wait_ge(bank_read_a, pe.ra.freed())
                    b = pe.ra.next()
                    for s in range(4):
                        ins = pe.eng.transpose(b[:, s * P:(s + 1) * P], VB[br][:, q % 2, t + s, 0:P], ident)
                    ins.then_inc(bank_full_a, 1)
                turn(0)
                for t in range(0, nt, 4):
                    if t + 4 < nt:
                        turn(t + 4)
                    pe.wait_ge(scalar_turned, pe.due(scalar_turned))
                    pe.wait_ge(bank_read_v, pe.rv.freed())
                    b = pe.rv.next()
                    mm(b[0:64], QB[:, q], KTb[br][:, t * P:(t + 4) * P], start=True, stop=True).then_inc(bank_full_v, 1)
                pe.wait_ge(bank_read_v, pe.rv.freed())
                b = pe.rv.next()
                mm(b[0:64, 0:64], QB[:, q], KTn[:, br], start=True, stop=True).then_inc(bank_full_v, 1)
            scores(0)
            for k, (br, q) in enumerate(SU):
                nt = UT[br]
                if k + 1 < len(SU):
                    scores(k + 1)
                pe.wait_ge(scalar_for_tensor, pe.due(scalar_for_tensor))
                for t in range(0, nt, 8):
                    n = min(8, nt - t)
                    pe.wait_ge(bank_read_a, pe.ra.freed())
                    b = pe.ra.next()
                    for s in range(n):
                        ins = pe.eng.transpose(b[:, s * 64:(s + 1) * 64], S4b[br][:, (t + s) * P:(t + s + 1) * P],
                                               ident[0:64, 0:64])
                    ins.then_inc(bank_full_a, 1)
                pe.wait_ge(bank_read_a, pe.ra.freed())
                b = pe.ra.next()
                pe.eng.transpose(b[0:64, 0:64], S4b[br][:, nt * P:nt * P + 64], ident[0:64, 0:64]).then_inc(bank_full_a, 1)
                pe.wait_ge(scalar_for_tensor, pe.due(scalar_for_tensor))
                c = 384 if br == 0 else 640
                pe.wait_ge(bank_read_v, pe.rv.freed())
                b = pe.rv.next()
                for t in range(nt):
                    mm(b[0:64, 0:P], PT4b[br][:, t], VB[br][:, q % 2, t, P:2 * P], start=(t == 0), stop=False)
                mm(b[0:64, 0:P], PTnb[br], NR[0:64, 8, c:c + P], start=False, stop=True).then_inc(bank_full_v, 1)
            pe.wait_ge(vector_for_tensor, pe.due(vector_for_tensor))
            pe.wait_ge(bank_read_v, pe.rv.freed())
            b = pe.rv.next()
            for q in range(NB):
                ins = pe.eng.transpose(b[0:64, q * 64:(q + 1) * 64], OB[:, q], ident[0:64, 0:64])
            ins.then_inc(bank_full_v, 1)

        def ss_act(act):
            a = act.eng

            def keys(k):
                br, q = SU[k]
                for t in range(0, UT[br], 4):
                    act.wait_ge(bank_full_a, act.due(bank_full_a))
                    b = act.ra.next()
                    a.copy(KTb[br][:, t * P:(t + 4) * P], b).then_inc(bank_read_a, 1)
                    act.wait_ge(bank_read_a, act.done(bank_read_a))
                    act.eng.sem_inc(scalar_turned, act.one(scalar_turned))
            keys(0)
            for k, (br, q) in enumerate(SU):
                nt = UT[br]
                if k + 1 < len(SU):
                    keys(k + 1)
                act.wait_ge(vector_for_scalar, act.due(vector_for_scalar))
                s, w = S4b[br][:, 0:nt * P + 64], aw[:, k % 2]
                a.activation(s, s, ACT.Exp, bias=w[:, 1:2], scale=SCALE, accum_out=w[:, 2:3]).then_inc(scalar_done, 1)
                act.wait_ge(scalar_done, act.done(scalar_done))
                act.eng.sem_inc(scalar_for_vector, act.one(scalar_for_vector))
                act.eng.sem_inc(scalar_for_tensor, act.one(scalar_for_tensor))
                for t in range(0, nt, 8):
                    n = min(8, nt - t)
                    act.wait_ge(bank_full_a, act.due(bank_full_a))
                    b = act.ra.next()
                    a.copy(PT4b[br][:, t:t + n], b[:, 0:n * 64].rearrange("p (s c) -> p s c", c=64)).then_inc(bank_read_a, 1)
                    act.wait_ge(bank_read_a, act.done(bank_read_a))
                act.wait_ge(bank_full_a, act.due(bank_full_a))
                b = act.ra.next()
                a.copy(PTnb[br], b[0:64, 0:64]).then_inc(bank_read_a, 1)
                act.wait_ge(bank_read_a, act.done(bank_read_a))
                act.eng.sem_inc(scalar_for_tensor, act.one(scalar_for_tensor))

        def ss_dve(v):
            e = v.eng

            def prepare(k):
                br, q = SU[k]
                nt, S, w = UT[br], S4b[br], aw[:, k % 2]
                for t in range(0, nt, 4):
                    v.wait_ge(bank_full_v, v.due(bank_full_v))
                    b = v.rv.next()
                    o = S[:, t * P:(t + 4) * P]
                    if br == 0:
                        e.tensor_tensor(o.rearrange("p (n l) -> p n l", l=64),
                                                     b[0:64].rearrange("p (n l) -> p n l", l=64),
                                                     SB[:, q, 2 * t:2 * t + 8].unsqueeze(2).broadcast_to([64, 8, 64]), ALU.add).then_inc(bank_read_v, 1)
                        v.wait_ge(bank_read_v, v.done(bank_read_v))
                    else:
                        e.tensor_tensor(o, b[0:64], MW, ALU.add).then_inc(bank_read_v, 1)
                        v.wait_ge(bank_read_v, v.done(bank_read_v))
                n = nt * P
                v.wait_ge(bank_full_v, v.due(bank_full_v))
                b = v.rv.next()
                e.tensor_tensor(S[:, n:n + 64], b[0:64, 0:64], MN_.rearrange("p b t -> p (b t)"), ALU.add).then_inc(bank_read_v, 1)
                v.wait_ge(bank_read_v, v.done(bank_read_v))
                new = S[:, n:n + 64].rearrange("p (b t) -> p b t", b=NB)
                e.tensor_tensor(new, new, seqm[:, q].unsqueeze(2).broadcast_to([64, NB, TS]), ALU.add).then_inc(vector_done, 1)
                v.wait_ge(vector_done, v.done(vector_done))
                e.tensor_reduce(w[:, 0:1], S[:, 0:n + 64], AX.X, ALU.max).then_inc(vector_done, 1)
                v.wait_ge(vector_done, v.done(vector_done))
                e.tensor_scalar(w[:, 1:2], w[:, 0:1], -SCALE, None, ALU.mult).then_inc(vector_done, 1)
                v.wait_ge(vector_done, v.done(vector_done))
                v.eng.sem_inc(vector_for_scalar, v.one(vector_for_scalar))

            def finish(k):
                br, q = SU[k]
                w = aw[:, k % 2]
                v.wait_ge(scalar_for_vector, v.due(scalar_for_vector))
                e.reciprocal(w[:, 3:4], w[:, 2:3]).then_inc(vector_done, 1)
                v.wait_ge(vector_done, v.done(vector_done))
                e.tensor_tensor(w[:, 3:4], w[:, 3:4], GS[:, q, 1 + br:2 + br], ALU.mult).then_inc(vector_done, 1)
                v.wait_ge(vector_done, v.done(vector_done))
                v.wait_ge(bank_full_v, v.due(bank_full_v))
                b = v.rv.next()
                p = slice(0, 32)
                e.scalar_tensor_tensor(out=OB[p, q], in0=b[p, 0:64], scalar=w[p, 3:4], in1=OB[p, q],
                                            op0=ALU.mult, op1=ALU.add).then_inc(vector_done, 1)
                v.wait_ge(vector_done, v.done(vector_done))
                p = slice(32, 64)
                e.scalar_tensor_tensor(out=OB[p, q], in0=b[p, 64:128], scalar=w[p, 3:4], in1=OB[p, q],
                                                    op0=ALU.mult, op1=ALU.add).then_inc(bank_read_v, 1)
                v.wait_ge(bank_read_v, v.done(bank_read_v))
                v.eng.sem_inc(vector_for_gpsimd, v.one(vector_for_gpsimd))
            prepare(0)
            for k in range(len(SU)):
                if k + 1 < len(SU):
                    prepare(k + 1)
                finish(k)
            v.eng.sem_inc(vector_for_tensor, v.one(vector_for_tensor))
            v.wait_ge(bank_full_v, v.due(bank_full_v))
            b = v.rv.next()
            e.tensor_copy(OTs, b[0:64].rearrange("p (b h t) -> p h b t", b=NB, h=8)).then_inc(bank_read_v, 1)
            v.wait_ge(bank_read_v, v.done(bank_read_v))
            v.eng.sem_inc(vector_for_sync, v.one(vector_for_sync))

        def ss_sp(sp):
            sp.wait_ge(vector_for_sync, sp.due(vector_for_sync))
            sp.eng.dma_start(mixT[512:1024, TP:R].rearrange("(h d) r -> d h r", d=DH), OTs.rearrange("p h b t -> p h (b t)"),
                             allow_slow_non_contiguous=True).then_inc(outputs_stored, 16)
            sp.wait_ge(outputs_stored, sp.due(outputs_stored, 16))

        arena.at = base
        MX = arena.take(P, KD, R)
        wo = arena.take(P, KD, D)

        def out_sp(sp):
            sp.eng.dma_start(MX, mixT.rearrange("(k p) r -> p k r", p=P),
                             allow_slow_non_contiguous=True).then_inc(loads_for_tensor, 16)
            sp.eng.dma_start(wo, I["w_out"][0].rearrange("(k p) c -> p k c", p=P),
                             allow_slow_non_contiguous=True).then_inc(loads_for_tensor, 16)

        def out_pe(pe):
            pe.wait_ge(loads_for_tensor, pe.due(loads_for_tensor, 32))
            for d in range(KD):
                for c0, n in CHUNKS:
                    pe.wait_ge(bank_read_v, pe.rv.freed())
                    b = pe.rv.next()
                    for k in range(KD):
                        ins = pe.eng.matmul(b[:, 0:n], wo[:, k, d * P:(d + 1) * P], MX[:, k, c0:c0 + n],
                                            start=(k == 0), stop=(k == KD - 1))
                    ins.then_inc(bank_full_v, 1)

        def out_dve(v):
            for d in range(KD):
                for c0, n in CHUNKS:
                    v.wait_ge(bank_full_v, v.due(bank_full_v))
                    b = v.rv.next()
                    v.eng.tensor_tensor(xT[:, d, c0:c0 + n], b[:, 0:n], xT[:, d, c0:c0 + n], ALU.add).then_inc(bank_read_v, 1)
                    v.wait_ge(bank_read_v, v.done(bank_read_v))

        arena.at = base
        arena.at = after_norm
        memX = arena.take(P, KD, MEM)
        mrow = arena.take(P, 2, D)
        wkv = arena.take(P, KD, 512)
        wq = arena.take(P, KD, 256)
        wmo = arena.take(P, 2, D)
        kv = arena.take(P, 2, 512)
        mkg = arena.take(P, DH)
        qg = arena.take(P, 1)
        ksq, ksr = arena.take(P, 2, 4, DH), arena.take(P, 8)
        mem_tail = arena.at

        def memkv_sp(sp):
            sp.eng.dma_start(mrow, I["mem_prompt"][0].rearrange("(i p) d -> p i d", p=P),
                             allow_slow_non_contiguous=True).then_inc(loads_for_tensor, 16)
            sp.eng.dma_start(wkv, I["mem_w_kv"][0].rearrange("(k p) c -> p k c", p=P),
                             allow_slow_non_contiguous=True).then_inc(loads_for_tensor, 16)
            sp.eng.dma_start(wq, I["mem_w_q"][0].rearrange("(k p) c -> p k c", p=P),
                             allow_slow_non_contiguous=True).then_inc(loads_for_tensor, 16)
            sp.eng.dma_start(mkg, I["mem_qk_g"][0, 1:2].broadcast_to([P, DH]),
                             allow_slow_non_contiguous=True).then_inc(loads_for_vector, 16)
            for k in range(2):
                sp.eng.dma_start(qg[64 * k:64 * k + 64], I["mem_qk_g"][0, 0].rearrange("(d o) -> d o", o=1),
                                 allow_slow_non_contiguous=True).then_inc(loads_for_vector, 16)
            sp.wait_ge(vector_for_sync, sp.due(vector_for_sync))
            sp.eng.dma_start(O["mem_p"][0, 0].rearrange("(i p) c h d -> p i (c h d)", p=P), kv,
                             allow_slow_non_contiguous=True).then_inc(outputs_stored, 16)
            sp.wait_ge(outputs_stored, sp.due(outputs_stored, 16))

        def memkv_pe(pe):
            pe.wait_ge(loads_for_tensor, pe.due(loads_for_tensor, 48))
            for i in range(2):
                for ring, k0 in ((pe.rv, 0), (pe.rv, 4)):
                    pe.wait_ge(ring.read, ring.freed())
                    b = ring.next()
                    for k in range(4):
                        ins = pe.eng.transpose(b[:, k * P:(k + 1) * P], mrow[:, i, (k0 + k) * P:(k0 + k + 1) * P], ident)
                    ins.then_inc(ring.full, 1)
            norm_pe(pe, [(0, MEM)])
            pe.wait_ge(vector_for_tensor, pe.due(vector_for_tensor))
            for i in range(2):
                pe.wait_ge(bank_read_v, pe.rv.freed())
                b = pe.rv.next()
                for k in range(KD):
                    ins = pe.eng.matmul(b, memX[:, k, i * P:(i + 1) * P], wkv[:, k], start=(k == 0), stop=(k == KD - 1))
                ins.then_inc(bank_full_v, 1)

        def memkv_act(act):
            norm_act(act, [(0, MEM)])
            act.wait_ge(vector_for_scalar, act.due(vector_for_scalar))
            act.eng.activation(ksr, ksr, ACT.Sqrt, bias=eps[:, 0:1], scale=1.0 / DH).then_inc(scalar_done, 1)
            act.wait_ge(scalar_done, act.done(scalar_done))
            act.eng.sem_inc(scalar_for_vector, act.one(scalar_for_vector))

        def memkv_dve(v):
            e = v.eng
            for i in range(2):
                for k0 in (0, 4):
                    v.wait_ge(bank_full_v, v.due(bank_full_v))
                    b = v.rv.next()
                    e.tensor_copy(memX[:, k0:k0 + 4, i * P:(i + 1) * P], four(b, P)).then_inc(bank_read_v, 1)
                    v.wait_ge(bank_read_v, v.done(bank_read_v))
            norm_dve(v, 3, src=memX, dst=memX, chunks=[(0, MEM)])
            v.eng.sem_inc(vector_for_tensor, v.one(vector_for_tensor))
            for i in range(2):
                v.wait_ge(bank_full_v, v.due(bank_full_v))
                b = v.rv.next()
                e.tensor_copy(kv[:, i], b).then_inc(bank_read_v, 1)
                v.wait_ge(bank_read_v, v.done(bank_read_v))
            v.wait_ge(loads_for_vector, v.due(loads_for_vector, 48))
            kk = kv.rearrange("p i (c h d) -> p i c h d", c=2, h=4)[:, :, 0]
            e.tensor_tensor(ksq, kk, kk, ALU.mult).then_inc(vector_done, 1)
            v.wait_ge(vector_done, v.done(vector_done))
            e.tensor_reduce(ksr, ksq.rearrange("p i h d -> p (i h) d"), AX.X, ALU.add).then_inc(vector_done, 1)
            v.wait_ge(vector_done, v.done(vector_done))
            v.eng.sem_inc(vector_for_scalar, v.one(vector_for_scalar))
            v.wait_ge(scalar_for_vector, v.due(scalar_for_vector))
            e.reciprocal(ksr, ksr).then_inc(vector_done, 1)
            v.wait_ge(vector_done, v.done(vector_done))
            for i in range(2):
                e.tensor_tensor(kk[:, i], kk[:, i], ksr[:, 4 * i:4 * i + 4].unsqueeze(2).broadcast_to([P, 4, DH]), ALU.mult).then_inc(vector_done, 1)
                v.wait_ge(vector_done, v.done(vector_done))
                e.tensor_tensor(kk[:, i], kk[:, i], mkg.unsqueeze(1).broadcast_to([P, 4, DH]), ALU.mult).then_inc(vector_done, 1)
                v.wait_ge(vector_done, v.done(vector_done))
            v.eng.sem_inc(vector_for_sync, v.one(vector_for_sync))

        arena.at = after_h
        qP = arena.take(P, 2, R)
        qR = arena.take(P, 2, R)
        assert arena.at <= after_norm

        def memq_pe(pe):
            for j in range(2):
                for c0, n in CHUNKS:
                    pe.wait_ge(bank_read_v, pe.rv.freed())
                    b = pe.rv.next()
                    for k in range(KD):
                        ins = pe.eng.matmul(b[:, 0:n], wq[:, k, j * P:(j + 1) * P], hT[:, k, c0:c0 + n],
                                            start=(k == 0), stop=(k == KD - 1))
                    ins.then_inc(bank_full_v, 1)
            head_sums_pe(pe, qR)

        def memq_act(act):
            head_roots_act(act, qR)

        def memq_dve(v):
            e = v.eng
            for j in range(2):
                for c0, n in CHUNKS:
                    v.wait_ge(bank_full_v, v.due(bank_full_v))
                    b = v.rv.next()
                    e.tensor_copy(qP[:, j, c0:c0 + n], b[:, 0:n]).then_inc(bank_read_v, 1)
                    v.wait_ge(bank_read_v, v.done(bank_read_v))
            e.tensor_tensor(qR, qP, qP, ALU.mult).then_inc(vector_for_tensor, 1)
            v.wait_ge(vector_for_tensor, v.done(vector_for_tensor))
            v.wait_ge(scalar_for_vector, v.due(scalar_for_vector))
            e.reciprocal(qR, qR).then_inc(vector_done, 1)
            v.wait_ge(vector_done, v.done(vector_done))
            e.tensor_tensor(qP, qP, qR, ALU.mult).then_inc(vector_done, 1)
            v.wait_ge(vector_done, v.done(vector_done))
            e.tensor_scalar(qP, qP, qg[:, 0:1], None, ALU.mult).then_inc(vector_done, 1)
            v.wait_ge(vector_done, v.done(vector_done))
            v.eng.sem_inc(vector_for_sync, v.one(vector_for_sync))

        arena.at = base
        q64 = arena.take(64, 4, R)
        kT64 = arena.take(64, 4, MEM)
        qm = arena.take(64, 4, 64)
        assert arena.at <= after_h
        def memq_sp(sp):
            sp.wait_ge(vector_for_sync, sp.due(vector_for_sync))

        arena.at = after_norm
        mS = arena.take(P, 2, 4, MEM)
        mP = arena.take(P, 2, 8, P)
        mo = arena.take(P, 256)
        mst = arena.take(P, 2, 16)
        oT = arena.take(P, 2, R)
        assert arena.at <= after_norm + KD * MEM + 2 * D + KD * 512

        def memat_sp(sp):
            for e in range(2):
                sp.eng.dma_start(q64[:, e:4:2], qP[64 * e:64 * e + 64],
                                 allow_slow_non_contiguous=True).then_inc(loads_for_tensor, 16)
            sp.eng.dma_start(wmo, I["mem_w_o"][0].rearrange("(k p) c -> p k c", p=P),
                             allow_slow_non_contiguous=True).then_inc(loads_for_tensor, 16)

        def kt_pe(pe, src):
            for half in range(2):
                pe.wait_ge(bank_read_a, pe.ra.freed())
                b = pe.ra.next()
                for hh in range(2):
                    for i in range(2):
                        h = 2 * half + hh
                        ins = pe.eng.transpose(b[0:64, hh * 256 + i * P:hh * 256 + (i + 1) * P],
                                               src[:, i, h * DH:(h + 1) * DH], ident)
                ins.then_inc(bank_full_a, 1)

        def kt_act(act):
            for half in range(2):
                act.wait_ge(bank_full_a, act.due(bank_full_a))
                b = act.ra.next()
                act.eng.copy(kT64[:, 2 * half:2 * half + 2], b[0:64].rearrange("p (h c) -> p h c", h=2)).then_inc(bank_read_a, 1)
                act.wait_ge(bank_read_a, act.done(bank_read_a))
            act.eng.sem_inc(scalar_for_tensor, act.one(scalar_for_tensor))

        def memat_pe(pe):
            mm = pe.eng.matmul
            kt_pe(pe, kv)
            pe.wait_ge(loads_for_tensor, pe.due(loads_for_tensor, 48))
            pe.wait_ge(scalar_for_tensor, pe.due(scalar_for_tensor))

            def scores(i):
                for half in range(2):
                    pe.wait_ge(bank_read_v, pe.rv.freed())
                    b = pe.rv.next()
                    for hh in range(2):
                        ins = mm(b[:, hh * 256:(hh + 1) * 256], q64[:, 2 * half + hh, i * P:(i + 1) * P],
                                 kT64[:, 2 * half + hh], start=True, stop=True)
                    ins.then_inc(bank_full_v, 1)
            scores(0)
            for i in range(8):
                if i < 7:
                    scores(i + 1)
                pe.wait_ge(scalar_for_tensor, pe.due(scalar_for_tensor))
                for half in range(2):
                    pe.wait_ge(bank_read_a, pe.ra.freed())
                    b = pe.ra.next()
                    for hh in range(2):
                        for s in range(2):
                            ins = pe.eng.transpose(b[:, (2 * hh + s) * P:(2 * hh + s + 1) * P],
                                                   mS[:, i % 2, 2 * half + hh, s * P:(s + 1) * P], ident)
                    ins.then_inc(bank_full_a, 1)
                pe.wait_ge(scalar_for_tensor, pe.due(scalar_for_tensor))
                pe.wait_ge(bank_read_v, pe.rv.freed())
                b = pe.rv.next()
                for h in range(4):
                    for s in range(2):
                        ins = mm(b[:, h * 64:(h + 1) * 64], mP[:, i % 2, 2 * h + s],
                                 kv[:, s, 256 + h * DH:256 + (h + 1) * DH], start=(s == 0), stop=(s == 1))
                ins.then_inc(bank_full_v, 1)
                pe.wait_ge(vector_for_tensor, pe.due(vector_for_tensor))
                pe.wait_ge(bank_read_a, pe.ra.freed())
                b = pe.ra.next()
                for j in range(2):
                    ins = pe.eng.transpose(b[:, j * P:(j + 1) * P], mo[:, j * P:(j + 1) * P], ident)
                ins.then_inc(bank_full_a, 1)

        def memat_act(act):
            a = act.eng
            kt_act(act)
            for i in range(8):
                act.wait_ge(vector_for_scalar, act.due(vector_for_scalar))
                for h in range(4):
                    s = mS[:, i % 2, h]
                    a.activation(s, s, ACT.Exp, bias=mst[:, i % 2, 4 + h:5 + h], scale=SCALE,
                                        accum_out=mst[:, i % 2, 8 + h:9 + h]).then_inc(scalar_done, 1)
                    act.wait_ge(scalar_done, act.done(scalar_done))
                act.eng.sem_inc(scalar_for_tensor, act.one(scalar_for_tensor))
                act.eng.sem_inc(scalar_for_vector, act.one(scalar_for_vector))
                for half in range(2):
                    act.wait_ge(bank_full_a, act.due(bank_full_a))
                    b = act.ra.next()
                    a.copy(mP[:, i % 2, 4 * half:4 * half + 4], b.rearrange("p (s c) -> p s c", s=4)).then_inc(bank_read_a, 1)
                    act.wait_ge(bank_read_a, act.done(bank_read_a))
                act.eng.sem_inc(scalar_for_tensor, act.one(scalar_for_tensor))
                act.wait_ge(bank_full_a, act.due(bank_full_a))
                b = act.ra.next()
                a.copy(oT[:, :, i * P:(i + 1) * P], b[:, 0:256].rearrange("p (j c) -> p j c", j=2)).then_inc(bank_read_a, 1)
                act.wait_ge(bank_read_a, act.done(bank_read_a))
            act.eng.sem_inc(scalar_for_vector, act.one(scalar_for_vector))

        def max4_dve(v, s, st):
            v.eng.tensor_reduce(st[:, 0:4], s, AX.X, ALU.max).then_inc(vector_done, 1)
            v.wait_ge(vector_done, v.done(vector_done))
            v.eng.tensor_scalar(st[:, 4:8], st[:, 0:4], -SCALE, None, ALU.mult).then_inc(vector_done, 1)
            v.wait_ge(vector_done, v.done(vector_done))
            v.eng.sem_inc(vector_for_scalar, v.one(vector_for_scalar))

        def memat_dve(v):
            e = v.eng

            def prepare(i):
                for half in range(2):
                    v.wait_ge(bank_full_v, v.due(bank_full_v))
                    b = v.rv.next()
                    e.tensor_copy(mS[:, i % 2, 2 * half:2 * half + 2], b.rearrange("p (h c) -> p h c", h=2)).then_inc(bank_read_v, 1)
                    v.wait_ge(bank_read_v, v.done(bank_read_v))
                max4_dve(v, mS[:, i % 2], mst[:, i % 2])
            prepare(0)
            for i in range(8):
                if i < 7:
                    prepare(i + 1)
                v.wait_ge(scalar_for_vector, v.due(scalar_for_vector))
                st = mst[:, i % 2]
                e.reciprocal(st[:, 12:16], st[:, 8:12]).then_inc(vector_done, 1)
                v.wait_ge(vector_done, v.done(vector_done))
                v.wait_ge(bank_full_v, v.due(bank_full_v))
                b = v.rv.next()
                e.tensor_tensor(mo.rearrange("p (h d) -> p h d", h=4),
                                             b[:, 0:256].rearrange("p (h d) -> p h d", h=4),
                                             st[:, 12:16].unsqueeze(2).broadcast_to([P, 4, DH]), ALU.mult).then_inc(bank_read_v, 1)
                v.wait_ge(bank_read_v, v.done(bank_read_v))
                v.eng.sem_inc(vector_for_tensor, v.one(vector_for_tensor))
            v.wait_ge(scalar_for_vector, v.due(scalar_for_vector))

        arena.at = mem_tail
        MC = arena.take(P, NB, 2, 512)
        kTs = arena.take(64, 2, 4, MEM)
        mSs = arena.array[0:8, after_h:after_h + NB * 4 * MEM].rearrange("p (b h c) -> p b h c", b=NB, h=4)
        arena.at = base + 4 * R + 4 * MEM
        mPs = arena.take(P, NB * 4 * 2, TS)
        oM = arena.take(64, 4, NB * TS)
        msx, msz = arena.take(8, NB * 4), arena.take(8, NB * 4)
        assert arena.at <= after_h

        def mems_sp(sp):
            sp.eng.dma_start(MC, I["cache_mem_kv"][0].rearrange("b (i p) c h d -> p b i (c h d)", p=P),
                             allow_slow_non_contiguous=True).then_inc(loads_for_tensor, 16)
            sp.wait_ge(vector_for_sync, sp.due(vector_for_sync))
            for e in range(2):
                sp.eng.dma_start(oT[64 * e:64 * e + 64, :, TP:R], oM[:, e:4:2],
                                 allow_slow_non_contiguous=True).then_inc(heads_moved, 16)
            sp.wait_ge(heads_moved, sp.due(heads_moved, 32))

        def mems_pe(pe):
            mm = pe.eng.matmul
            pe.wait_ge(loads_for_tensor, pe.due(loads_for_tensor, 16))
            for q in range(NB):
                kt_pe(pe, MC[:, q])
                pe.wait_ge(scalar_for_tensor, pe.due(scalar_for_tensor))
                for half in range(2):
                    pe.wait_ge(bank_read_v, pe.rv.freed())
                    b = pe.rv.next()
                    for hh in range(2):
                        h = 2 * half + hh
                        ins = mm(b[0:8, hh * 256:(hh + 1) * 256], q64[:, h, TP + q * TS:TP + (q + 1) * TS],
                                 kTs[:, q % 2, h], start=True, stop=True)
                    ins.then_inc(bank_full_v, 1)
            pe.wait_ge(vector_for_tensor, pe.due(vector_for_tensor))
            pe.wait_ge(bank_read_v, pe.rv.freed())
            b = pe.rv.next()
            for q in range(NB):
                for h in range(4):
                    for s in range(2):
                        k = (q * 4 + h) * 2 + s
                        ins = pe.eng.transpose(b[:, k * TS:(k + 1) * TS], mSs[:, q, h, s * P:(s + 1) * P], ident[0:8, 0:8])
            ins.then_inc(bank_full_v, 1)
            pe.wait_ge(vector_for_tensor, pe.due(vector_for_tensor))
            pe.wait_ge(bank_read_v, pe.rv.freed())
            b = pe.rv.next()
            for q in range(NB):
                for h in range(4):
                    for s in range(2):
                        ins = mm(b[0:64, h * 64 + q * TS:h * 64 + (q + 1) * TS],
                                 MC[:, q, s, 256 + h * DH:256 + (h + 1) * DH], mPs[:, (q * 4 + h) * 2 + s],
                                 start=(s == 0), stop=(s == 1))
            ins.then_inc(bank_full_v, 1)

        def mems_act(act):
            for q in range(NB):
                for half in range(2):
                    act.wait_ge(bank_full_a, act.due(bank_full_a))
                    b = act.ra.next()
                    if q >= 2 and half == 0:
                        act.wait_ge(vector_for_scalar, act.due(vector_for_scalar))
                    act.eng.copy(kTs[:, q % 2, 2 * half:2 * half + 2],
                                                  b[0:64].rearrange("p (h c) -> p h c", h=2)).then_inc(bank_read_a, 1)
                    act.wait_ge(bank_read_a, act.done(bank_read_a))
                act.eng.sem_inc(scalar_for_tensor, act.one(scalar_for_tensor))
            act.wait_ge(vector_for_scalar, act.due(vector_for_scalar, 3))
            act.eng.activation(mSs, mSs, ACT.Exp, scale=SCALE).then_inc(scalar_done, 1)
            act.wait_ge(scalar_done, act.done(scalar_done))
            act.eng.sem_inc(scalar_for_vector, act.one(scalar_for_vector))

        def mems_dve(v):
            e = v.eng
            for q in range(NB):
                for half in range(2):
                    v.wait_ge(bank_full_v, v.due(bank_full_v))
                    b = v.rv.next()
                    e.tensor_copy(mSs[:, q, 2 * half:2 * half + 2], b[0:8].rearrange("p (h c) -> p h c", h=2)).then_inc(bank_read_v, 1)
                    v.wait_ge(bank_read_v, v.done(bank_read_v))
                v.eng.sem_inc(vector_for_scalar, v.one(vector_for_scalar))
            softmax_dve(v, mSs.rearrange("p b h c -> p (b h) c"), msx, msz, 8, NB * 4, MEM)
            v.eng.sem_inc(vector_for_tensor, v.one(vector_for_tensor))
            v.wait_ge(bank_full_v, v.due(bank_full_v))
            b = v.rv.next()
            e.tensor_copy(mPs, b.rearrange("p (k t) -> p k t", t=TS)).then_inc(bank_read_v, 1)
            v.wait_ge(bank_read_v, v.done(bank_read_v))
            v.eng.sem_inc(vector_for_tensor, v.one(vector_for_tensor))
            v.wait_ge(bank_full_v, v.due(bank_full_v))
            b = v.rv.next()
            e.tensor_copy(oM, b[0:64, 0:256].rearrange("p (h c) -> p h c", h=4)).then_inc(bank_read_v, 1)
            v.wait_ge(bank_read_v, v.done(bank_read_v))
            v.eng.sem_inc(vector_for_sync, v.one(vector_for_sync))

        def memo_pe(pe):
            for d in range(KD):
                for c0, n in CHUNKS:
                    pe.wait_ge(bank_read_v, pe.rv.freed())
                    b = pe.rv.next()
                    for k in range(2):
                        ins = pe.eng.matmul(b[:, 0:n], wmo[:, k, d * P:(d + 1) * P], oT[:, k, c0:c0 + n],
                                            start=(k == 0), stop=(k == 1))
                    ins.then_inc(bank_full_v, 1)

        block = ctx.enter_context(nc.Block())

        @block.sync
        def _(eng):
            sp = engine(eng)
            setup_sp(sp)
            eng.sem_inc(stage_ends, 1)
            eng.wait_ge(stage_ends, sp.met())
            ff_first_sp(sp, I["ffa_up"], True)
            eng.sem_inc(stage_ends, 1)
            eng.wait_ge(stage_ends, sp.met())
            ff_up_sp(sp, I["ffa_up"])
            eng.sem_inc(stage_ends, 1)
            eng.wait_ge(stage_ends, sp.met())
            ff_down_sp(sp, I["ffa_down"])
            eng.sem_inc(stage_ends, 1)
            eng.wait_ge(stage_ends, sp.met())
            proj_first_sp(sp)
            eng.sem_inc(stage_ends, 1)
            eng.wait_ge(stage_ends, sp.met())
            proj_sp(sp)
            eng.sem_inc(stage_ends, 1)
            eng.wait_ge(stage_ends, sp.met())
            rwkv_sp(sp)
            eng.sem_inc(stage_ends, 1)
            eng.wait_ge(stage_ends, sp.met())
            scan_sp(sp)
            eng.sem_inc(stage_ends, 1)
            eng.wait_ge(stage_ends, sp.met())
            scan_s_sp(sp)
            eng.sem_inc(stage_ends, 1)
            eng.wait_ge(stage_ends, sp.met())
            gn_sp(sp)
            eng.sem_inc(stage_ends, 1)
            eng.wait_ge(stage_ends, sp.met())
            ml_sp(sp)
            eng.sem_inc(stage_ends, 1)
            eng.wait_ge(stage_ends, sp.met())
            mlc_sp(sp)
            eng.sem_inc(stage_ends, 1)
            eng.wait_ge(stage_ends, sp.met())
            mls_sp(sp)
            eng.sem_inc(stage_ends, 1)
            eng.wait_ge(stage_ends, sp.met())
            mlo_sp(sp)
            eng.sem_inc(stage_ends, 1)
            eng.wait_ge(stage_ends, sp.met())
            nr_sp(sp)
            eng.sem_inc(stage_ends, 1)
            eng.wait_ge(stage_ends, sp.met())
            cm_sp(sp)
            eng.sem_inc(stage_ends, 1)
            eng.wait_ge(stage_ends, sp.met())
            eng.sem_inc(stage_ends, 1)
            eng.wait_ge(stage_ends, sp.met())
            eng.sem_inc(stage_ends, 1)
            eng.wait_ge(stage_ends, sp.met())
            sc_sp(sp)
            eng.sem_inc(stage_ends, 1)
            eng.wait_ge(stage_ends, sp.met())
            ss_sp(sp)
            eng.sem_inc(stage_ends, 1)
            eng.wait_ge(stage_ends, sp.met())
            out_sp(sp)
            eng.sem_inc(stage_ends, 1)
            eng.wait_ge(stage_ends, sp.met())
            memkv_sp(sp)
            eng.sem_inc(stage_ends, 1)
            eng.wait_ge(stage_ends, sp.met())
            eng.sem_inc(stage_ends, 1)
            eng.wait_ge(stage_ends, sp.met())
            memq_sp(sp)
            eng.sem_inc(stage_ends, 1)
            eng.wait_ge(stage_ends, sp.met())
            memat_sp(sp)
            eng.sem_inc(stage_ends, 1)
            eng.wait_ge(stage_ends, sp.met())
            mems_sp(sp)
            eng.sem_inc(stage_ends, 1)
            eng.wait_ge(stage_ends, sp.met())
            eng.sem_inc(stage_ends, 1)
            eng.wait_ge(stage_ends, sp.met())
            ff_first_sp(sp, I["ffb_up"])
            eng.sem_inc(stage_ends, 1)
            eng.wait_ge(stage_ends, sp.met())
            ff_up_sp(sp, I["ffb_up"])
            eng.sem_inc(stage_ends, 1)
            eng.wait_ge(stage_ends, sp.met())
            ff_down_sp(sp, I["ffb_down"])
            eng.sem_inc(stage_ends, 1)
            eng.wait_ge(stage_ends, sp.met())
            final_sp(sp)
            eng.sem_inc(stage_ends, 1)
            eng.wait_ge(stage_ends, sp.met())

        @block.gpsimd
        def _(eng):
            gp = engine(eng)
            setup_gp(gp)
            eng.sem_inc(stage_ends, 1)
            eng.wait_ge(stage_ends, gp.met())
            eng.sem_inc(stage_ends, 1)
            eng.wait_ge(stage_ends, gp.met())
            pages_gp(gp)
            eng.sem_inc(stage_ends, 1)
            eng.wait_ge(stage_ends, gp.met())
            eng.sem_inc(stage_ends, 1)
            eng.wait_ge(stage_ends, gp.met())
            eng.sem_inc(stage_ends, 1)
            eng.wait_ge(stage_ends, gp.met())
            proj_gp(gp)
            eng.sem_inc(stage_ends, 1)
            eng.wait_ge(stage_ends, gp.met())
            rwkv_gp(gp)
            eng.sem_inc(stage_ends, 1)
            eng.wait_ge(stage_ends, gp.met())
            eng.sem_inc(stage_ends, 1)
            eng.wait_ge(stage_ends, gp.met())
            eng.sem_inc(stage_ends, 1)
            eng.wait_ge(stage_ends, gp.met())
            eng.sem_inc(stage_ends, 1)
            eng.wait_ge(stage_ends, gp.met())
            ml_gp(gp)
            eng.sem_inc(stage_ends, 1)
            eng.wait_ge(stage_ends, gp.met())
            eng.sem_inc(stage_ends, 1)
            eng.wait_ge(stage_ends, gp.met())
            eng.sem_inc(stage_ends, 1)
            eng.wait_ge(stage_ends, gp.met())
            eng.sem_inc(stage_ends, 1)
            eng.wait_ge(stage_ends, gp.met())
            nr_gp(gp)
            eng.sem_inc(stage_ends, 1)
            eng.wait_ge(stage_ends, gp.met())
            cm_gp(gp)
            eng.sem_inc(stage_ends, 1)
            eng.wait_ge(stage_ends, gp.met())
            eng.sem_inc(stage_ends, 1)
            eng.wait_ge(stage_ends, gp.met())
            eng.sem_inc(stage_ends, 1)
            eng.wait_ge(stage_ends, gp.met())
            sc_gp(gp)
            eng.sem_inc(stage_ends, 1)
            eng.wait_ge(stage_ends, gp.met())
            ss_gp(gp)
            eng.sem_inc(stage_ends, 1)
            eng.wait_ge(stage_ends, gp.met())
            eng.sem_inc(stage_ends, 1)
            eng.wait_ge(stage_ends, gp.met())
            eng.sem_inc(stage_ends, 1)
            eng.wait_ge(stage_ends, gp.met())
            eng.sem_inc(stage_ends, 1)
            eng.wait_ge(stage_ends, gp.met())
            eng.sem_inc(stage_ends, 1)
            eng.wait_ge(stage_ends, gp.met())
            eng.sem_inc(stage_ends, 1)
            eng.wait_ge(stage_ends, gp.met())
            eng.sem_inc(stage_ends, 1)
            eng.wait_ge(stage_ends, gp.met())
            eng.sem_inc(stage_ends, 1)
            eng.wait_ge(stage_ends, gp.met())
            eng.sem_inc(stage_ends, 1)
            eng.wait_ge(stage_ends, gp.met())
            eng.sem_inc(stage_ends, 1)
            eng.wait_ge(stage_ends, gp.met())
            eng.sem_inc(stage_ends, 1)
            eng.wait_ge(stage_ends, gp.met())
            eng.sem_inc(stage_ends, 1)
            eng.wait_ge(stage_ends, gp.met())

        @block.scalar
        def _(eng):
            act = engine(eng)
            setup_act(act)
            eng.sem_inc(stage_ends, 1)
            eng.wait_ge(stage_ends, act.met())
            norm_act(act)
            eng.sem_inc(stage_ends, 1)
            eng.wait_ge(stage_ends, act.met())
            ff_up_act(act)
            eng.sem_inc(stage_ends, 1)
            eng.wait_ge(stage_ends, act.met())
            eng.sem_inc(stage_ends, 1)
            eng.wait_ge(stage_ends, act.met())
            norm_act(act)
            eng.sem_inc(stage_ends, 1)
            eng.wait_ge(stage_ends, act.met())
            proj_act(act)
            eng.sem_inc(stage_ends, 1)
            eng.wait_ge(stage_ends, act.met())
            rwkv_act(act)
            eng.sem_inc(stage_ends, 1)
            eng.wait_ge(stage_ends, act.met())
            scan_act(act)
            eng.sem_inc(stage_ends, 1)
            eng.wait_ge(stage_ends, act.met())
            scan_s_act(act)
            eng.sem_inc(stage_ends, 1)
            eng.wait_ge(stage_ends, act.met())
            gn_act(act)
            eng.sem_inc(stage_ends, 1)
            eng.wait_ge(stage_ends, act.met())
            ml_act(act)
            eng.sem_inc(stage_ends, 1)
            eng.wait_ge(stage_ends, act.met())
            mlc_act(act)
            eng.sem_inc(stage_ends, 1)
            eng.wait_ge(stage_ends, act.met())
            mls_act(act)
            eng.sem_inc(stage_ends, 1)
            eng.wait_ge(stage_ends, act.met())
            mlo_act(act)
            eng.sem_inc(stage_ends, 1)
            eng.wait_ge(stage_ends, act.met())
            nr_act(act)
            eng.sem_inc(stage_ends, 1)
            eng.wait_ge(stage_ends, act.met())
            cm_act(act)
            eng.sem_inc(stage_ends, 1)
            eng.wait_ge(stage_ends, act.met())
            at_act(act)
            eng.sem_inc(stage_ends, 1)
            eng.wait_ge(stage_ends, act.met())
            ot_act(act)
            eng.sem_inc(stage_ends, 1)
            eng.wait_ge(stage_ends, act.met())
            sc_act(act)
            eng.sem_inc(stage_ends, 1)
            eng.wait_ge(stage_ends, act.met())
            ss_act(act)
            eng.sem_inc(stage_ends, 1)
            eng.wait_ge(stage_ends, act.met())
            eng.sem_inc(stage_ends, 1)
            eng.wait_ge(stage_ends, act.met())
            memkv_act(act)
            eng.sem_inc(stage_ends, 1)
            eng.wait_ge(stage_ends, act.met())
            norm_act(act)
            eng.sem_inc(stage_ends, 1)
            eng.wait_ge(stage_ends, act.met())
            memq_act(act)
            eng.sem_inc(stage_ends, 1)
            eng.wait_ge(stage_ends, act.met())
            memat_act(act)
            eng.sem_inc(stage_ends, 1)
            eng.wait_ge(stage_ends, act.met())
            mems_act(act)
            eng.sem_inc(stage_ends, 1)
            eng.wait_ge(stage_ends, act.met())
            eng.sem_inc(stage_ends, 1)
            eng.wait_ge(stage_ends, act.met())
            norm_act(act)
            eng.sem_inc(stage_ends, 1)
            eng.wait_ge(stage_ends, act.met())
            ff_up_act(act)
            eng.sem_inc(stage_ends, 1)
            eng.wait_ge(stage_ends, act.met())
            eng.sem_inc(stage_ends, 1)
            eng.wait_ge(stage_ends, act.met())
            final_act(act)
            eng.sem_inc(stage_ends, 1)
            eng.wait_ge(stage_ends, act.met())

        @block.tensor
        def _(eng):
            pe = engine(eng)
            setup_pe(pe)
            eng.sem_inc(stage_ends, 1)
            eng.wait_ge(stage_ends, pe.met())
            norm_pe(pe)
            eng.sem_inc(stage_ends, 1)
            eng.wait_ge(stage_ends, pe.met())
            ff_up_pe(pe, True)
            eng.sem_inc(stage_ends, 1)
            eng.wait_ge(stage_ends, pe.met())
            ff_down_pe(pe)
            eng.sem_inc(stage_ends, 1)
            eng.wait_ge(stage_ends, pe.met())
            norm_pe(pe)
            eng.sem_inc(stage_ends, 1)
            eng.wait_ge(stage_ends, pe.met())
            proj_pe(pe)
            eng.sem_inc(stage_ends, 1)
            eng.wait_ge(stage_ends, pe.met())
            rwkv_pe(pe)
            eng.sem_inc(stage_ends, 1)
            eng.wait_ge(stage_ends, pe.met())
            scan_pe(pe)
            eng.sem_inc(stage_ends, 1)
            eng.wait_ge(stage_ends, pe.met())
            scan_s_pe(pe)
            eng.sem_inc(stage_ends, 1)
            eng.wait_ge(stage_ends, pe.met())
            gn_pe(pe)
            eng.sem_inc(stage_ends, 1)
            eng.wait_ge(stage_ends, pe.met())
            ml_pe(pe)
            eng.sem_inc(stage_ends, 1)
            eng.wait_ge(stage_ends, pe.met())
            mlc_pe(pe)
            eng.sem_inc(stage_ends, 1)
            eng.wait_ge(stage_ends, pe.met())
            mls_pe(pe)
            eng.sem_inc(stage_ends, 1)
            eng.wait_ge(stage_ends, pe.met())
            mlo_pe(pe)
            eng.sem_inc(stage_ends, 1)
            eng.wait_ge(stage_ends, pe.met())
            nr_pe(pe)
            eng.sem_inc(stage_ends, 1)
            eng.wait_ge(stage_ends, pe.met())
            cm_pe(pe)
            eng.sem_inc(stage_ends, 1)
            eng.wait_ge(stage_ends, pe.met())
            at_pe(pe)
            eng.sem_inc(stage_ends, 1)
            eng.wait_ge(stage_ends, pe.met())
            ot_pe(pe)
            eng.sem_inc(stage_ends, 1)
            eng.wait_ge(stage_ends, pe.met())
            sc_pe(pe)
            eng.sem_inc(stage_ends, 1)
            eng.wait_ge(stage_ends, pe.met())
            ss_pe(pe)
            eng.sem_inc(stage_ends, 1)
            eng.wait_ge(stage_ends, pe.met())
            out_pe(pe)
            eng.sem_inc(stage_ends, 1)
            eng.wait_ge(stage_ends, pe.met())
            memkv_pe(pe)
            eng.sem_inc(stage_ends, 1)
            eng.wait_ge(stage_ends, pe.met())
            norm_pe(pe)
            eng.sem_inc(stage_ends, 1)
            eng.wait_ge(stage_ends, pe.met())
            memq_pe(pe)
            eng.sem_inc(stage_ends, 1)
            eng.wait_ge(stage_ends, pe.met())
            memat_pe(pe)
            eng.sem_inc(stage_ends, 1)
            eng.wait_ge(stage_ends, pe.met())
            mems_pe(pe)
            eng.sem_inc(stage_ends, 1)
            eng.wait_ge(stage_ends, pe.met())
            memo_pe(pe)
            eng.sem_inc(stage_ends, 1)
            eng.wait_ge(stage_ends, pe.met())
            norm_pe(pe)
            eng.sem_inc(stage_ends, 1)
            eng.wait_ge(stage_ends, pe.met())
            ff_up_pe(pe)
            eng.sem_inc(stage_ends, 1)
            eng.wait_ge(stage_ends, pe.met())
            ff_down_pe(pe)
            eng.sem_inc(stage_ends, 1)
            eng.wait_ge(stage_ends, pe.met())
            final_pe(pe)
            eng.sem_inc(stage_ends, 1)
            eng.wait_ge(stage_ends, pe.met())

        @block.vector
        def _(eng):
            v = engine(eng)
            setup_dve(v)
            eng.sem_inc(stage_ends, 1)
            eng.wait_ge(stage_ends, v.met())
            norm_dve(v, 0)
            eng.sem_inc(stage_ends, 1)
            eng.wait_ge(stage_ends, v.met())
            ff_up_dve(v, True)
            eng.sem_inc(stage_ends, 1)
            eng.wait_ge(stage_ends, v.met())
            ff_down_dve(v)
            eng.sem_inc(stage_ends, 1)
            eng.wait_ge(stage_ends, v.met())
            norm_dve(v, 1)
            eng.sem_inc(stage_ends, 1)
            eng.wait_ge(stage_ends, v.met())
            proj_dve(v)
            eng.sem_inc(stage_ends, 1)
            eng.wait_ge(stage_ends, v.met())
            rwkv_dve(v)
            eng.sem_inc(stage_ends, 1)
            eng.wait_ge(stage_ends, v.met())
            scan_dve(v)
            eng.sem_inc(stage_ends, 1)
            eng.wait_ge(stage_ends, v.met())
            scan_s_dve(v)
            eng.sem_inc(stage_ends, 1)
            eng.wait_ge(stage_ends, v.met())
            gn_dve(v)
            eng.sem_inc(stage_ends, 1)
            eng.wait_ge(stage_ends, v.met())
            ml_dve(v)
            eng.sem_inc(stage_ends, 1)
            eng.wait_ge(stage_ends, v.met())
            mlc_dve(v)
            eng.sem_inc(stage_ends, 1)
            eng.wait_ge(stage_ends, v.met())
            mls_dve(v)
            eng.sem_inc(stage_ends, 1)
            eng.wait_ge(stage_ends, v.met())
            mlo_dve(v)
            eng.sem_inc(stage_ends, 1)
            eng.wait_ge(stage_ends, v.met())
            nr_dve(v)
            eng.sem_inc(stage_ends, 1)
            eng.wait_ge(stage_ends, v.met())
            cm_dve(v)
            eng.sem_inc(stage_ends, 1)
            eng.wait_ge(stage_ends, v.met())
            at_dve(v)
            eng.sem_inc(stage_ends, 1)
            eng.wait_ge(stage_ends, v.met())
            eng.sem_inc(stage_ends, 1)
            eng.wait_ge(stage_ends, v.met())
            sc_dve(v)
            eng.sem_inc(stage_ends, 1)
            eng.wait_ge(stage_ends, v.met())
            ss_dve(v)
            eng.sem_inc(stage_ends, 1)
            eng.wait_ge(stage_ends, v.met())
            out_dve(v)
            eng.sem_inc(stage_ends, 1)
            eng.wait_ge(stage_ends, v.met())
            memkv_dve(v)
            eng.sem_inc(stage_ends, 1)
            eng.wait_ge(stage_ends, v.met())
            norm_dve(v, 2)
            eng.sem_inc(stage_ends, 1)
            eng.wait_ge(stage_ends, v.met())
            memq_dve(v)
            eng.sem_inc(stage_ends, 1)
            eng.wait_ge(stage_ends, v.met())
            memat_dve(v)
            eng.sem_inc(stage_ends, 1)
            eng.wait_ge(stage_ends, v.met())
            mems_dve(v)
            eng.sem_inc(stage_ends, 1)
            eng.wait_ge(stage_ends, v.met())
            out_dve(v)
            eng.sem_inc(stage_ends, 1)
            eng.wait_ge(stage_ends, v.met())
            norm_dve(v, 4)
            eng.sem_inc(stage_ends, 1)
            eng.wait_ge(stage_ends, v.met())
            ff_up_dve(v)
            eng.sem_inc(stage_ends, 1)
            eng.wait_ge(stage_ends, v.met())
            ff_down_dve(v)
            eng.sem_inc(stage_ends, 1)
            eng.wait_ge(stage_ends, v.met())
            final_dve(v)
            eng.sem_inc(stage_ends, 1)
            eng.wait_ge(stage_ends, v.met())



_OUTS = [("y_prompt", (1, TP, D)), ("y_sample", (NB, TS, D)),
         ("cmp_p", (1, 1, TP, 2, 2, DH)), ("cmp_s", (1, NB, TS, 2, 2, DH)),
         ("sel_p", (1, 1, TP, 2, 2, DH)), ("sel_s", (1, NB, TS, 2, 2, DH)),
         ("win_p", (1, 1, WIN, 2, 2, DH)), ("win_s", (1, NB, WIN, 2, 2, DH)),
         ("mem_p", (1, 1, MEM, 2, 4, DH)),
         ("shift_p", (1, 1, 1, 1024)), ("shift_s", (1, NB, 1, 1024)),
         ("S_p", (1, 1, 4, DH, DH)), ("S_s", (1, NB, 4, DH, DH)),
         ("conv_p", (1, 1, 3, 256)), ("conv_s", (1, NB, 3, 256)),
         ("C_p", (1, 1, 4, DH, DH)), ("C_s", (1, NB, 4, DH, DH)),
         ("n_p", (1, 1, 4, DH)), ("n_s", (1, NB, 4, DH)),
         ("m_p", (1, 1, 4)), ("m_s", (1, NB, 4))]


def kernel(**inputs):
    import concourse.bacc as _bacc
    from concourse.bass_utils import run_bass_kernel_spmd as _run

    nc = _bacc.Bacc("TRN2", target_bir_lowering=False, num_devices=1)
    arrays, I, O = {}, {}, {}
    for name, value in inputs.items():
        a = np.ascontiguousarray(value)
        arrays[f"in_{name}"] = a
        I[name] = nc.dram_tensor(f"in_{name}", a.shape, mybir.dt.from_np(a.dtype), kind="ExternalInput").ap()
    for name, shape in _OUTS:
        O[name] = nc.dram_tensor(f"out_{name}", shape, F32, kind="ExternalOutput").ap()
    build(nc, I, O)
    r = _run(nc, [arrays], core_ids=[0])
    return tuple(r.results[0][f"out_{name}"] for name, _ in _OUTS)
```
